# Optimizing a Trainium2 kernel written in Bass

```python
import functools
import jax, jax.numpy as jnp
from jax import lax
import numpy as np

D_MODEL = 1024
BATCH = 1
SEQ = 2048
DEPTH = 1
DEC_BATCH = 8
DEC_SEQ = 4
PAST_LEN = 2048
PAGE_SIZE = 128

C_CONV = 512
CONV_W = 31
N_HEADS = 8
N_KV_HEADS = 4
HEAD_DIM = 64
Q_PER_KV = N_HEADS // N_KV_HEADS
ATTN_W = N_HEADS * HEAD_DIM
N_IDX_HEADS = 8
IDX_DIM = 64
TOPK_MAX = 256
Q_BLOCK = 128
N_GROUPS = 4
EXP_PER_GROUP = 8
N_EXPERTS = N_GROUPS * EXP_PER_GROUP
EXPERT_TOP_K = 2
D_EXPERT = 256
MOE_BLOCK = 128
DN_ALPHA = (2 * DEPTH) ** 0.25
DN_BETA = (8 * DEPTH) ** -0.25
LN_EPS = 1e-5
SPLIT_SIZES = (C_CONV, C_CONV, N_HEADS * HEAD_DIM, N_KV_HEADS * HEAD_DIM, N_KV_HEADS * HEAD_DIM,
               N_IDX_HEADS * IDX_DIM, IDX_DIM, N_IDX_HEADS, 2 * D_MODEL)
N_IN = sum(SPLIT_SIZES)
SPLIT_POINTS = tuple(np.cumsum(SPLIT_SIZES)[:-1].tolist())

kernel_name = 'hybrid_conformer_dsa_hmoe_step'

def layer_norm(x, g, b):
    xf = x.astype(jnp.float32)
    mu = jnp.mean(xf, axis=-1, keepdims=True)
    var = jnp.mean(jnp.square(xf - mu), axis=-1, keepdims=True)
    y = (xf - mu) * lax.rsqrt(var + LN_EPS) * g.astype(jnp.float32) + b.astype(jnp.float32)
    return y.astype(x.dtype)

def gather_rows(rows, idx):
    return jax.vmap(lambda r, i: r[i])(rows, idx)

def project_inputs(x, w_in, b_in):
    B, S = x.shape[:2]
    h = jnp.einsum('bsd,dn->bsn', x, w_in) + b_in
    ca, cb, q, k, v, qi, ki, wi, gates = jnp.split(h, list(SPLIT_POINTS), axis=-1)
    u = ca * jax.nn.sigmoid(cb)
    q = q.reshape(B, S, N_HEADS, HEAD_DIM)
    k = k.reshape(B, S, N_KV_HEADS, HEAD_DIM)
    v = v.reshape(B, S, N_KV_HEADS, HEAD_DIM)
    qi = qi.reshape(B, S, N_IDX_HEADS, IDX_DIM)
    wi = wi * (N_IDX_HEADS ** -0.5)
    g_conv, g_attn = jnp.split(jax.nn.sigmoid(gates), 2, axis=-1)
    return u, q, k, v, qi, ki, wi, g_conv, g_attn

def conv_branch(u_hist, conv_w, conv_b, ln_g, ln_b, w_conv_out):
    y = lax.conv_general_dilated(u_hist, conv_w[:, None, :], window_strides=(1,), padding='VALID',
                                 dimension_numbers=('NWC', 'WIO', 'NWC'),
                                 feature_group_count=C_CONV) + conv_b
    y = jax.nn.silu(layer_norm(y, ln_g, ln_b))
    return jnp.einsum('bsc,cd->bsd', y, w_conv_out)

def indexer_select(qi, wi, kidx, qpos, k_sel):
    dots = jnp.einsum('bqhd,bsd->bqhs', qi, kidx) * (IDX_DIM ** -0.5)
    score = jnp.einsum('bqhs,bqh->bqs', jax.nn.relu(dots), wi).astype(jnp.float32)
    kpos = jnp.arange(kidx.shape[1])
    score = jnp.where(kpos[None, None, :] <= qpos[None, :, None], score, -jnp.inf)
    return lax.top_k(score, k_sel)[1]

def sparse_attend(q, k_sel, v_sel, valid):
    B, Q = q.shape[:2]
    qg = q.reshape(B, Q, N_KV_HEADS, Q_PER_KV, HEAD_DIM)
    s = jnp.einsum('bqkgd,bqnkd->bqkgn', qg, k_sel).astype(jnp.float32) * (HEAD_DIM ** -0.5)
    s = jnp.where(valid[:, :, None, None, :], s, -jnp.inf)
    p = jax.nn.softmax(s, axis=-1).astype(v_sel.dtype)
    o = jnp.einsum('bqkgn,bqnkd->bqkgd', p, v_sel)
    return o.reshape(B, Q, ATTN_W)

def dsa_prompt(q, k, v, qi, ki, wi):
    B, T = q.shape[:2]
    k_sel = min(TOPK_MAX, T // 4)

    def block(i):
        s0 = i * Q_BLOCK
        sl = lambda a: lax.dynamic_slice_in_dim(a, s0, Q_BLOCK, axis=1)
        qpos = s0 + jnp.arange(Q_BLOCK)
        idx = indexer_select(sl(qi), sl(wi), ki, qpos, k_sel)
        valid = idx <= qpos[None, :, None]
        return sparse_attend(sl(q), gather_rows(k, idx), gather_rows(v, idx), valid)

    o = lax.map(block, jnp.arange(T // Q_BLOCK))
    return jnp.swapaxes(o, 0, 1).reshape(B, T, ATTN_W)

def dsa_sample(q, k, v, qi, ki, wi, k_pool, v_pool, ki_pool, page_table):
    DB, S = q.shape[:2]
    past = page_table.shape[1] * PAGE_SIZE
    k_sel = min(TOPK_MAX, (past + S) // 4)
    ki_past = ki_pool[page_table].reshape(DB, past, IDX_DIM)
    ki_all = jnp.concatenate([ki_past, ki], axis=1)
    qpos = past + jnp.arange(S)
    idx = indexer_select(qi, wi, ki_all, qpos, k_sel)
    is_past = idx < past
    pidx = jnp.minimum(idx, past - 1)
    phys = gather_rows(page_table, pidx // PAGE_SIZE)
    off = pidx % PAGE_SIZE
    nidx = jnp.clip(idx - past, 0, S - 1)
    sel = lambda pool, new: jnp.where(is_past[..., None, None], pool[phys, off], gather_rows(new, nidx))
    valid = idx <= qpos[None, :, None]
    return sparse_attend(q, sel(k_pool, k), sel(v_pool, v), valid)

def grouped_experts(xf, experts, gates, w_gate, w_up, w_down):
    n_tok = xf.shape[0]
    n_asg = n_tok * EXPERT_TOP_K
    flat_e = experts.reshape(-1)
    flat_t = jnp.repeat(jnp.arange(n_tok, dtype=jnp.int32), EXPERT_TOP_K)
    flat_g = gates.reshape(-1)
    order = jnp.argsort(flat_e)
    se, st, sg = flat_e[order], flat_t[order], flat_g[order]
    counts = jnp.bincount(flat_e, length=N_EXPERTS)
    padded = (counts + MOE_BLOCK - 1) // MOE_BLOCK * MOE_BLOCK
    pad_end = jnp.cumsum(padded)
    pad_start = pad_end - padded
    start = jnp.cumsum(counts) - counts
    dest = pad_start[se] + jnp.arange(n_asg) - start[se]
    n_blocks = -(-n_asg // MOE_BLOCK) + N_EXPERTS
    slot_tok = jnp.full((n_blocks * MOE_BLOCK,), n_tok, jnp.int32).at[dest].set(st)
    blk_exp = jnp.minimum(jnp.searchsorted(pad_end, jnp.arange(n_blocks) * MOE_BLOCK, side='right'), N_EXPERTS - 1)
    x_pad = jnp.concatenate([xf, jnp.zeros((1, xf.shape[1]), xf.dtype)], axis=0)
    xb = x_pad[slot_tok].reshape(n_blocks, MOE_BLOCK, xf.shape[1])

    def expert_block(args):
        xblk, e = args
        h = jax.nn.silu(xblk @ w_gate[e]) * (xblk @ w_up[e])
        return h @ w_down[e]

    yb = lax.map(expert_block, (xb, blk_exp)).reshape(n_blocks * MOE_BLOCK, -1)
    y = yb[dest] * sg[:, None].astype(yb.dtype)
    return jax.ops.segment_sum(y, st, num_segments=n_tok)

def hier_moe(x, rgw, rgb, rew, reb, w_gate, w_up, w_down):
    shape = x.shape
    xf = x.reshape(-1, D_MODEL)
    n_tok = xf.shape[0]
    g_logits = (xf @ rgw + rgb).astype(jnp.float32)
    grp = jnp.argmax(g_logits, axis=-1).astype(jnp.int32)
    p_grp = jnp.take_along_axis(jax.nn.softmax(g_logits, axis=-1), grp[:, None], axis=1)
    e_logits = (xf @ rew + reb).astype(jnp.float32).reshape(n_tok, N_GROUPS, EXP_PER_GROUP)
    e_logits = jnp.take_along_axis(e_logits, grp[:, None, None], axis=1)[:, 0]
    top_p, top_i = lax.top_k(jax.nn.softmax(e_logits, axis=-1), EXPERT_TOP_K)
    gates = p_grp * top_p / jnp.sum(top_p, axis=-1, keepdims=True)
    experts = grp[:, None] * EXP_PER_GROUP + top_i.astype(jnp.int32)
    return grouped_experts(xf, experts, gates.astype(x.dtype), w_gate, w_up, w_down).reshape(shape)

def decoder_layer(x, conv_prefix, attend, w_in, b_in, conv_w, conv_b, conv_ln_g, conv_ln_b, w_conv_out,
                  w_attn_out, w_out, ln1_g, ln1_b, router_group_w, router_group_b, router_expert_w,
                  router_expert_b, w_gate, w_up, w_down, ln2_g, ln2_b):
    u, q, k, v, qi, ki, wi, g_conv, g_attn = project_inputs(x, w_in, b_in)
    u_hist = jnp.concatenate([conv_prefix.astype(u.dtype), u], axis=1)
    y_conv = conv_branch(u_hist, conv_w, conv_b, conv_ln_g, conv_ln_b, w_conv_out)
    y_attn = jnp.einsum('bsa,ad->bsd', attend(q, k, v, qi, ki, wi), w_attn_out)
    mix = jnp.einsum('bsd,de->bse', g_conv * y_conv + g_attn * y_attn, w_out)
    x = layer_norm(DN_ALPHA * x + mix, ln1_g, ln1_b)
    ffn = hier_moe(x, router_group_w, router_group_b, router_expert_w, router_expert_b, w_gate, w_up, w_down)
    x = layer_norm(DN_ALPHA * x + ffn, ln2_g, ln2_b)
    return x, k, v, ki, u_hist[:, -(CONV_W - 1):]

def setup_inputs(seed: int = 0) -> dict:
    key = jax.random.key(seed)
    ks = jax.random.split(key, 32)
    f32 = jnp.float32
    n_pages = PAST_LEN // PAGE_SIZE
    n_used = DEC_BATCH * n_pages
    n_phys = n_used + max(1, n_used // 4)

    def nrm(k, shape, scale):
        return jax.random.normal(k, shape, f32) * scale

    page_table = jax.random.permutation(ks[6], n_phys)[:n_used].reshape(DEC_BATCH, n_pages).astype(jnp.int32)
    return {
        'x_prompt': nrm(ks[0], (BATCH, SEQ, D_MODEL), 1.0),
        'x_sample': nrm(ks[1], (DEC_BATCH, DEC_SEQ, D_MODEL), 1.0),
        'cache_k': nrm(ks[2], (DEPTH, n_phys, PAGE_SIZE, N_KV_HEADS, HEAD_DIM), 1.0),
        'cache_v': nrm(ks[3], (DEPTH, n_phys, PAGE_SIZE, N_KV_HEADS, HEAD_DIM), 1.0),
        'cache_kidx': nrm(ks[4], (DEPTH, n_phys, PAGE_SIZE, IDX_DIM), 1.0),
        'state_conv': nrm(ks[5], (DEPTH, DEC_BATCH, CONV_W - 1, C_CONV), 0.5),
        'page_table': page_table,
        'w_in': nrm(ks[7], (DEPTH, D_MODEL, N_IN), D_MODEL ** -0.5),
        'b_in': nrm(ks[8], (DEPTH, N_IN), 0.02),
        'conv_w': nrm(ks[9], (DEPTH, CONV_W, C_CONV), CONV_W ** -0.5),
        'conv_b': nrm(ks[10], (DEPTH, C_CONV), 0.02),
        'conv_ln_g': 1.0 + nrm(ks[11], (DEPTH, C_CONV), 0.02),
        'conv_ln_b': nrm(ks[12], (DEPTH, C_CONV), 0.02),
        'w_conv_out': nrm(ks[13], (DEPTH, C_CONV, D_MODEL), C_CONV ** -0.5),
        'w_attn_out': nrm(ks[14], (DEPTH, ATTN_W, D_MODEL), ATTN_W ** -0.5),
        'w_out': nrm(ks[15], (DEPTH, D_MODEL, D_MODEL), DN_BETA * D_MODEL ** -0.5),
        'ln1_g': 1.0 + nrm(ks[16], (DEPTH, D_MODEL), 0.02),
        'ln1_b': nrm(ks[17], (DEPTH, D_MODEL), 0.02),
        'router_group_w': nrm(ks[18], (DEPTH, D_MODEL, N_GROUPS), D_MODEL ** -0.5),
        'router_group_b': nrm(ks[19], (DEPTH, N_GROUPS), 0.01),
        'router_expert_w': nrm(ks[20], (DEPTH, D_MODEL, N_EXPERTS), D_MODEL ** -0.5),
        'router_expert_b': nrm(ks[21], (DEPTH, N_EXPERTS), 0.01),
        'w_gate': nrm(ks[22], (DEPTH, N_EXPERTS, D_MODEL, D_EXPERT), D_MODEL ** -0.5),
        'w_up': nrm(ks[23], (DEPTH, N_EXPERTS, D_MODEL, D_EXPERT), D_MODEL ** -0.5),
        'w_down': nrm(ks[24], (DEPTH, N_EXPERTS, D_EXPERT, D_MODEL), DN_BETA * D_EXPERT ** -0.5),
        'ln2_g': 1.0 + nrm(ks[25], (DEPTH, D_MODEL), 0.02),
        'ln2_b': nrm(ks[26], (DEPTH, D_MODEL), 0.02),
    }

def reference(x_prompt, x_sample, cache_k, cache_v, cache_kidx, state_conv, page_table, w_in, b_in,
              conv_w, conv_b, conv_ln_g, conv_ln_b, w_conv_out, w_attn_out, w_out, ln1_g, ln1_b,
              router_group_w, router_group_b, router_expert_w, router_expert_b, w_gate, w_up, w_down,
              ln2_g, ln2_b):
    xp, xs = x_prompt, x_sample
    kp_l, vp_l, ip_l, cp_l = [], [], [], []
    ks_l, vs_l, is_l, cs_l = [], [], [], []
    conv_zero = jnp.zeros((x_prompt.shape[0], CONV_W - 1, C_CONV), x_prompt.dtype)
    for l in range(DEPTH):
        params = (w_in[l], b_in[l], conv_w[l], conv_b[l], conv_ln_g[l], conv_ln_b[l], w_conv_out[l],
                  w_attn_out[l], w_out[l], ln1_g[l], ln1_b[l], router_group_w[l], router_group_b[l],
                  router_expert_w[l], router_expert_b[l], w_gate[l], w_up[l], w_down[l], ln2_g[l], ln2_b[l])
        xp, kp, vp, ip, cp = decoder_layer(xp, conv_zero, dsa_prompt, *params)
        sample_attend = functools.partial(dsa_sample, k_pool=cache_k[l], v_pool=cache_v[l],
                                          ki_pool=cache_kidx[l], page_table=page_table)
        xs, k_s, v_s, i_s, c_s = decoder_layer(xs, state_conv[l], sample_attend, *params)
        kp_l.append(kp); vp_l.append(vp); ip_l.append(ip); cp_l.append(cp)
        ks_l.append(k_s); vs_l.append(v_s); is_l.append(i_s); cs_l.append(c_s)
    return (xp, xs, jnp.stack(kp_l), jnp.stack(vp_l), jnp.stack(ip_l), jnp.stack(cp_l),
            jnp.stack(ks_l), jnp.stack(vs_l), jnp.stack(is_l), jnp.stack(cs_l))


_drawn_inputs = setup_inputs


def setup_inputs(seed=0):
    import zlib

    import numpy as np

    out = dict(_drawn_inputs(seed))
    spreads = {}
    factors = {'conv_b': 5.173,
     'conv_ln_g': 7.016,
     'conv_ln_b': 7.13,
     'router_group_b': 8.0,
     'router_expert_b': 25.35,
     'ln2_g': 7.853,
     'ln2_b': 7.797,
     'cache_k': 4.338}
    for name, (base, spread) in spreads.items():
        noise = np.random.default_rng([zlib.crc32(name.encode()), seed]).standard_normal(out[name].shape)
        drawn = base * np.exp(spread * noise) if base else spread * noise
        out[name] = __import__('jax').numpy.asarray(drawn.astype(out[name].dtype))
    for name, factor in factors.items():
        out[name] = (out[name] * factor).astype(out[name].dtype)
    return out
```

```python
from contextlib import ExitStack

import concourse.bass as bass
from concourse import mybir

F32 = mybir.dt.float32
I32 = mybir.dt.int32
ALU = mybir.AluOpType
ACT = mybir.ActivationFunctionType
AX = mybir.AxisListType

P = 128
D = 1024
KD = D // P
T = 2048
DB, DS = 8, 4
S = DB * DS
TT = T + S
NT = T // P
CC = 512
CB = CC // P
TAPS = 31
HIST = TAPS - 1
NH, NKV, HD = 8, 4, 64
NIH = 8
TOPK = 256
N_IN = 4680
COL_Q, COL_K, COL_V, COL_QI, COL_KI, COL_WI, COL_G = 1024, 1536, 1792, 2048, 2560, 2624, 2632
LN_EPS = 1e-5
ALPHA = 2.0 ** 0.25

VEC_BIN, VEC_CB, VEC_LG, VEC_LB, VEC_N = 0, 37, 41, 45, 49
KI_BLK = 20
KI_ROWS = COL_G - KI_BLK * P
TOK_BLOCKS = [(i * 512, 512) for i in range(T // 512)] + [(T, S)]


class Chain:

    def __init__(self, eng, sem):
        self.eng, self.sem, self.count = eng, sem, 0

    def link(self, ins):
        self.count += 1
        ins.then_inc(self.sem, 1)
        self.eng.wait_ge(self.sem, self.count)

    def mark(self, ins):
        self.count += 1
        ins.then_inc(self.sem, 1)

    def sync(self):
        self.eng.wait_ge(self.sem, self.count)

    def restart(self):
        if self.count:
            self.eng.wait_ge(self.sem, self.count)
            self.eng.sem_clear(self.sem)
            self.count = 0


class Phase:

    def __init__(self, nc, tag):
        self.nc, self.tag, self.ctx, self.sems = nc, tag, ExitStack(), []

    def __enter__(self):
        self.ctx.__enter__()
        return self

    def __exit__(self, *e):
        if self.sems:
            self.nc.clear_and_free_semaphores(self.sems)
            self.nc.all_engine_barrier()
        return self.ctx.__exit__(*e)

    def sb(self, name, shape, dt=F32):
        return self.ctx.enter_context(self.nc.sbuf_tensor(self.tag + name, shape, dt))

    def ps(self, name, shape, dt=F32):
        return self.ctx.enter_context(self.nc.psum_tensor(self.tag + "ps_" + name, shape, dt))

    def sem(self, name):
        self.sems.append(self.nc.alloc_semaphore(self.tag + name))
        return self.sems[-1]

    def block(self):
        return self.nc.Block()


def constants(nc, c):
    with Phase(nc, "c_") as ph:
        made = ph.sem("made")
        with ph.block() as block:
            @block.gpsimd
            def _(pool):
                nc.gpsimd.memset(c.ident[:], 0.0).then_inc(made, 1)
                pool.wait_ge(made, 1)
                nc.gpsimd.affine_select(out=c.ident[:], in_=c.ident[:], compare_op=ALU.not_equal, fill=1.0,
                                        base=0, pattern=[[-1, P]], channel_multiplier=1).then_inc(made, 1)
                pool.wait_ge(made, 2)


def turn_input(nc, c, xT, cols, taps):
    with Phase(nc, "t_") as ph:
        xt = ph.sb("xt", [P, 2, D])
        vec = ph.sb("vec", [VEC_N, P])
        tap_rows = ph.sb("tap_rows", [TAPS, CC])
        acc = [ph.ps(f"acc{i}", [P, 4, P]) for i in range(4)]
        pv = ph.ps("pv", [P, 512])
        x_loaded = [ph.sem(f"x_loaded{i}") for i in range(2)]
        vec_zero, vec_loaded, vec_turned, vec_kept = (ph.sem(n) for n in ("vec_zero", "vec_loaded", "vec_turned", "vec_kept"))
        turned = ph.sem("turned")
        kept = ph.sem("kept")

        def pairs(e):
            with e.Fori(0, NT // 2) as i:
                yield i, 0, P
                yield i, 1, P
            yield NT // 2, 0, S

        with ph.block() as block:
            @block.sync
            def _(sp):
                sp.wait_ge(vec_zero, 1)
                for row, name in ((VEC_CB, "conv_b"), (VEC_LG, "conv_ln_g"), (VEC_LB, "conv_ln_b")):
                    sp.dma_start(vec[row:row + CB, :], c.inp[name][0].rearrange("(b f) -> b f", f=P)).then_inc(vec_loaded, 16)
                b_in = c.inp["b_in"]
                sp.dma_start(vec[0:KI_BLK, :], b_in[0, 0:KI_BLK * P].rearrange("(b f) -> b f", f=P)).then_inc(vec_loaded, 16)
                sp.dma_start(vec[KI_BLK:KI_BLK + 1, 0:KI_ROWS], b_in[0:1, KI_BLK * P:COL_G]).then_inc(vec_loaded, 16)
                sp.dma_start(vec[KI_BLK + 1:VEC_CB, :], b_in[0, COL_G:N_IN].rearrange("(b f) -> b f", f=P)).then_inc(vec_loaded, 16)
                sp.dma_start(tap_rows[:], c.inp["conv_w"][0]).then_inc(vec_loaded, 16)
                for i, slot, n in pairs(sp):
                    sp.wait_ge(kept, 4 * i + 2 * slot + 2)
                    src = c.xp[bass.ds((2 * i + slot) * P, P), :] if n == P else c.xs
                    sp.dma_start(xt[0:n, slot, :], src).then_inc(x_loaded[slot], 16)

            @block.tensor
            def _(pe):
                for i, slot, n in pairs(pe):
                    pe.wait_ge(x_loaded[slot], 16 * i + 16)
                    pe.wait_ge(kept, 4 * i + 2 * slot + 2)
                    for h in range(2):
                        for k in range(4):
                            f = (4 * h + k) * P
                            t = nc.tensor.transpose(acc[2 * slot + h][:, k, 0:n], xt[0:n, slot, f:f + P], c.ident[0:n, 0:n])
                        t.then_inc(turned, 1)
                pe.wait_ge(vec_loaded, 112)
                nc.tensor.transpose(pv[:, 0:VEC_N], vec[:], c.ident[0:VEC_N, 0:VEC_N])
                for b in range(CB):
                    t = nc.tensor.transpose(pv[:, 64 + 32 * b:64 + 32 * b + TAPS], tap_rows[:, b * P:(b + 1) * P], c.ident[0:TAPS, 0:TAPS])
                t.then_inc(vec_turned, 1)

            @block.vector
            def _(dve):
                nc.vector.memset(vec[:], 0.0).then_inc(vec_zero, 1)
                dve.sem_inc(kept, 4)
                for i, slot, n in pairs(dve):
                    for h in range(2):
                        dve.wait_ge(turned, 4 * i + 2 * slot + h + 1)
                        at = bass.ds((2 * i + slot) * P, n)
                        nc.vector.tensor_copy(xT[:, 4 * h:4 * h + 4, at], acc[2 * slot + h][:, :, 0:n]).then_inc(kept, 1)
                dve.wait_ge(vec_turned, 1)
                nc.vector.tensor_copy(cols[:], pv[:, 0:VEC_N]).then_inc(vec_kept, 1)
                nc.vector.tensor_copy(taps[:], pv[:, 64:64 + 32 * CB].rearrange("p (b t) -> p b t", b=CB)[:, :, 0:TAPS]).then_inc(vec_kept, 1)
                dve.wait_ge(vec_kept, 2)


def project(nc, c, xT, cols, taps):
    with Phase(nc, "p_") as ph:
        w = ph.sb("w", [P, 2, KD, P])
        stage = ph.sb("stage", [P, 2, TT])
        glu = ph.sb("glu", [P, 2, TT])
        uh = ph.sb("uh", [P, CB, HIST + T])
        conv = ph.sb("conv", [P, CB, TT])
        ush = ph.sb("ush", [P, CB, DB, HIST + DS])
        hist_rows = ph.sb("hist_rows", [120, 2, CC])
        acc = [ph.ps(f"acc{i}", [P, 512]) for i in range(5)]
        ph_h = ph.ps("hist", [P, 512])
        w_loaded = [ph.sem(f"w_loaded{i}") for i in range(2)]
        w_free = [ph.sem(f"w_free{i}") for i in range(2)]
        stored = [ph.sem(f"stored{i}") for i in range(2)]
        acc_full, acc_kept, glu_done, conv_done, u_stored = (
            ph.sem(n) for n in ("acc_full", "acc_kept", "glu_done", "conv_done", "u_stored"))
        h_loaded, h_turned, h_kept, s_chain, bias_kept = (ph.sem(n) for n in ("h_loaded", "h_turned", "h_kept", "chain", "bias_kept"))
        bias = ph.sb("bias", [P, 2])

        def steps(e, rest=False):
            if not rest:
                with e.Fori(0, CB) as i:
                    yield 2 * i, i, 0, i, i * P, P, "ca"
                    yield 2 * i + 1, i, 1, i + CB, i * P + CC, P, "cb"
            with e.Fori(0, 6) as i:
                yield 2 * i + 8, i + 4, 0, 2 * i + 8, i * (2 * P) + 8 * P, P, "plain"
                yield 2 * i + 9, i + 4, 1, 2 * i + 9, i * (2 * P) + 9 * P, P, "plain"
            yield 20, 10, 0, KI_BLK, KI_BLK * P, KI_ROWS, "plain"
            with e.Fori(0, 8) as i:
                yield 2 * i + 21, i + 10, 1, 2 * i + 21, i * (2 * P) + COL_G, P, "gate"
                yield 2 * i + 22, i + 11, 0, 2 * i + 22, i * (2 * P) + COL_G + P, P, "gate"

        with ph.block() as block:
            @block.sync
            def _(sp):
                for r in range(2):
                    sp.dma_start(hist_rows[:, r, :], c.inp["state_conv"][0, 4 * r:4 * r + 4].rearrange("b h c -> (b h) c")).then_inc(h_loaded, 16)
                w_in = c.inp["w_in"][0].rearrange("(k p) n -> p k n", p=P)
                for s, use, slot, blk, col, rows, kind in steps(sp):
                    sp.wait_ge(w_free[slot], use + 1)
                    sp.dma_start(w[:, slot, :, 0:rows], w_in[:, :, bass.ds(col, rows)]).then_inc(w_loaded[slot], 16)

            @block.tensor
            def _(pe):
                pe.sem_inc(w_free[0], 1)
                pe.sem_inc(w_free[1], 1)
                pe.wait_ge(h_loaded, 32)
                for b in range(CB):
                    for r in range(2):
                        if r == 0 and b > 0:
                            pe.wait_ge(h_kept, b)
                        t = nc.tensor.transpose(ph_h[:, r * 120:r * 120 + 120], hist_rows[:, r, b * P:(b + 1) * P], c.ident[0:120, 0:120])
                    t.then_inc(h_turned, 1)
                for s, use, slot, blk, col, rows, kind in steps(pe):
                    pe.wait_ge(w_loaded[slot], 16 * use + 16)
                    for tb, (t0, n) in enumerate(TOK_BLOCKS):
                        pe.wait_ge(acc_kept, 5 * s + tb + 1)
                        for k in range(KD):
                            m = nc.tensor.matmul(acc[tb][0:rows, 0:n], w[:, slot, k, 0:rows], xT[:, k, t0:t0 + n], start=(k == 0), stop=(k == KD - 1))
                        m.then_inc(acc_full, 1)
                    pe.wait_ge(acc_full, 5 * s + 5)
                    pe.sem_inc(w_free[slot], 1)

            @block.scalar
            def _(act):
                act.sem_inc(acc_kept, 5)
                for s, use, slot, blk, col, rows, kind in steps(act):
                    nc.scalar.copy(bias[:, slot:slot + 1], cols[:, bass.ds(blk, 1)]).then_inc(bias_kept, 1)
                    act.wait_ge(bias_kept, s + 1)
                    if kind == "ca":
                        act.wait_ge(glu_done, 2 * blk)
                    if kind in ("plain", "gate"):
                        act.wait_ge(stored[slot], (use - 4) * 16)
                    out = glu if kind in ("ca", "cb") else stage
                    func = ACT.Sigmoid if kind in ("cb", "gate") else ACT.Identity
                    for tb, (t0, n) in enumerate(TOK_BLOCKS):
                        act.wait_ge(acc_full, 5 * s + tb + 1)
                        nc.scalar.activation(out[0:rows, slot, t0:t0 + n], acc[tb][0:rows, 0:n], func,
                                             bias=bias[0:rows, slot:slot + 1]).then_inc(acc_kept, 1)

            @block.vector
            def _(dve):
                ch = Chain(dve, s_chain)
                ch.mark(nc.vector.memset(uh[:, :, 0:HIST], 0.0))
                for b in range(CB):
                    dve.wait_ge(h_turned, b + 1)
                    nc.vector.tensor_copy(ush[:, b, :, 0:HIST], ph_h[:, 0:240].rearrange("p (b h) -> p b h", b=DB)).then_inc(h_kept, 1)
                with dve.Fori(0, CB) as i:
                    dve.wait_ge(acc_kept, 10 * i + 15)
                    nc.vector.tensor_tensor(uh[:, bass.ds(i, 1), HIST:HIST + T], glu[:, 0:1, 0:T], glu[:, 1:2, 0:T], ALU.mult).then_inc(glu_done, 1)
                    nc.vector.tensor_tensor(ush[:, bass.ds(i, 1), :, HIST:HIST + DS],
                                            glu[:, 0:1, T:TT].rearrange("p a (b t) -> p a b t", b=DB), glu[:, 1:2, T:TT].rearrange("p a (b t) -> p a b t", b=DB), ALU.mult).then_inc(glu_done, 1)
                dve.wait_ge(glu_done, 2 * CB)
                ch.sync()
                dve.wait_ge(h_kept, CB)
                for b in range(CB):
                    out, outs = conv[:, b, 0:T], conv[:, b, T:TT].rearrange("p (b t) -> p b t", b=DB)
                    for tap in range(TAPS):
                        wt = taps[:, b, tap:tap + 1]
                        big, small = uh[:, b, tap:tap + T], ush[:, b, :, tap:tap + DS]
                        if tap == 0:
                            bias = cols[:, VEC_CB + b:VEC_CB + b + 1]
                            ch.mark(nc.vector.tensor_scalar(out, big, wt, bias, ALU.mult, ALU.add))
                            ch.mark(nc.vector.tensor_scalar(outs, small, wt, bias, ALU.mult, ALU.add))
                        else:
                            ch.sync()
                            ch.mark(nc.vector.scalar_tensor_tensor(out, big, wt, out, ALU.mult, ALU.add))
                            ch.mark(nc.vector.scalar_tensor_tensor(outs, small, wt, outs, ALU.mult, ALU.add))
                    ch.sync()
                    dve.sem_inc(conv_done, 1)

            @block.gpsimd
            def _(pool):
                pool.wait_ge(glu_done, 2 * CB)
                pool.dma_start(c.featT[0:CC, 0:T].rearrange("(b p) t -> p b t", p=P), uh[:, :, HIST:HIST + T]).then_inc(u_stored, 16)
                for b in range(CB):
                    pool.dma_start(c.featT[b * P:(b + 1) * P, T:TT].rearrange("p (b t) -> p b t", b=DB), ush[:, b, :, HIST:HIST + DS]).then_inc(u_stored, 16)
                for s, use, slot, blk, col, rows, kind in steps(pool, rest=True):
                    pool.wait_ge(acc_kept, 5 * s + 10)
                    pool.dma_start(c.featT[bass.ds(col, rows), :], stage[0:rows, slot, :]).then_inc(stored[slot], 16)
                pool.wait_ge(conv_done, CB)
                pool.dma_start(c.convT.rearrange("(b p) t -> p b t", p=P), conv[:]).then_inc(u_stored, 16)
                pool.wait_ge(u_stored, 16 * (CB + 2))
                pool.wait_ge(stored[0], 16 * (7 + 8))
                pool.wait_ge(stored[1], 16 * (6 + 8))


def keep_keys(nc, c, kT, kiT, v_tok, wi_tok):
    with Phase(nc, "k_") as ph:
        st = ph.sb("st", [P, 2, 4, P])
        sti = ph.sb("sti", [KI_ROWS, 2, P])
        ulast = ph.sb("ulast", [P, CB, HIST + S])
        utok = ph.sb("utok", [HIST + S, CC])
        k_tok = ph.sb("k_tok", [P, NT + 1, 2 * P])
        vs_tok = ph.sb("vs_tok", [S, 2 * P])
        ki_tok = ph.sb("ki_tok", [P, NT + 1, HD])
        kv = [ph.ps(f"kv{i}", [P, 512]) for i in range(2)]
        kw = [ph.ps(f"kw{i}", [P, 512]) for i in range(2)]
        pu = ph.ps("pu", [P, 512])
        keys_loaded, turned, kv_kept, ki_kept, u_loaded, u_turned, u_kept, saved = (
            ph.sem(n) for n in ("keys_loaded", "turned", "kv_kept", "ki_kept", "u_loaded", "u_turned", "u_kept", "saved"))
        loaded = [ph.sem(f"loaded{i}") for i in range(2)]

        def tiles(e):
            with e.Fori(0, NT // 2) as i:
                yield i, 0, P
                yield i, 1, P
            yield NT // 2, 0, S

        with ph.block() as block:
            @block.sync
            def _(sp):
                for i, slot, n in tiles(sp):
                    sp.wait_ge(turned, 2 * i + slot + 1)
                    t0 = (2 * i + slot) * P
                    sp.dma_start(st[:, slot, :, 0:n], c.featT[COL_K:COL_QI, bass.ds(t0, n)].rearrange("(b p) t -> p b t", p=P)).then_inc(loaded[slot], 16)
                    sp.dma_start(sti[:, slot, 0:n], c.featT[COL_KI:COL_G, bass.ds(t0, n)]).then_inc(loaded[slot], 16)
                out = c.out
                sp.wait_ge(kv_kept, 2 * (NT + 1) + 4)
                sp.wait_ge(ki_kept, NT + 1 + 2)
                sp.dma_start(out["k_prompt"][0, 0].rearrange("(i p) h d -> p i (h d)", p=P), k_tok[:, 0:NT]).then_inc(saved, 16)
                sp.dma_start(out["k_sample"][0].rearrange("b s h d -> (b s) (h d)"), k_tok[0:S, NT]).then_inc(saved, 16)
                sp.dma_start(out["v_prompt"][0, 0].rearrange("(i p) h d -> p i (h d)", p=P), v_tok[:]).then_inc(saved, 16)
                sp.dma_start(out["v_sample"][0].rearrange("b s h d -> (b s) (h d)"), vs_tok[:]).then_inc(saved, 16)
                sp.dma_start(out["ki_prompt"][0, 0].rearrange("(i p) d -> p i d", p=P), ki_tok[:, 0:NT]).then_inc(saved, 16)
                sp.dma_start(out["ki_sample"][0].rearrange("b s d -> (b s) d"), ki_tok[0:S, NT]).then_inc(saved, 16)
                sp.wait_ge(saved, 96)

            @block.gpsimd
            def _(pool):
                out = c.out
                pool.dma_start(kT[:], c.featT[COL_K:COL_V, 0:T].rearrange("(b p) t -> p b t", p=P)).then_inc(keys_loaded, 16)
                pool.dma_start(kiT[0:HD], c.featT[COL_KI:COL_WI, 0:T]).then_inc(keys_loaded, 16)
                pool.dma_start(ulast[:], c.featT[0:CC, T - HIST:TT].rearrange("(b p) t -> p b t", p=P)).then_inc(u_loaded, 16)
                pool.dma_start(out["conv_sample"][0, :, 0:HIST - DS], c.inp["state_conv"][0, :, DS:HIST]).then_inc(keys_loaded, 16)
                pool.wait_ge(u_kept, 1)
                pool.dma_start(out["conv_prompt"][0, 0], utok[0:HIST]).then_inc(keys_loaded, 16)
                for b in range(DB):
                    pool.dma_start(out["conv_sample"][0, b, HIST - DS:HIST], utok[HIST + b * DS:HIST + b * DS + DS]).then_inc(keys_loaded, 16)
                pool.wait_ge(keys_loaded, 16 * (4 + DB))

            @block.tensor
            def _(pe):
                pe.sem_inc(turned, 2)
                for i, slot, n in tiles(pe):
                    t = 2 * i + slot
                    pe.wait_ge(loaded[slot], 32 * i + 32)
                    pe.wait_ge(kv_kept, 2 * t + 2)
                    for b in range(4):
                        nc.tensor.transpose(kv[slot][0:n, b * P:(b + 1) * P], st[:, slot, b, 0:n], c.ident[:])
                    pe.wait_ge(ki_kept, t + 1)
                    nc.tensor.transpose(kw[slot][0:n, 0:KI_ROWS], sti[:, slot, 0:n], c.ident[0:KI_ROWS, 0:KI_ROWS]).then_inc(turned, 1)
                pe.wait_ge(u_loaded, 16)
                for b in range(CB):
                    u = nc.tensor.transpose(pu[0:HIST + S, b * P:(b + 1) * P], ulast[:, b, :], c.ident[:])
                u.then_inc(u_turned, 1)

            @block.scalar
            def _(act):
                act.sem_inc(kv_kept, 4)
                for i, slot, n in tiles(act):
                    t = 2 * i + slot
                    act.wait_ge(turned, t + 3)
                    act.nop()
                    nc.scalar.copy(k_tok[0:n, bass.ds(t, 1), :], kv[slot][0:n, 0:2 * P].rearrange("p (a c) -> p a c", a=1)).then_inc(kv_kept, 1)
                    v_out = v_tok[0:n, bass.ds(t, 1), :] if n == P else vs_tok[:].rearrange("p (a c) -> p a c", a=1)
                    nc.scalar.copy(v_out, kv[slot][0:n, 2 * P:4 * P].rearrange("p (a c) -> p a c", a=1)).then_inc(kv_kept, 1)

            @block.vector
            def _(dve):
                dve.sem_inc(ki_kept, 2)
                for i, slot, n in tiles(dve):
                    t = 2 * i + slot
                    dve.wait_ge(turned, t + 3)
                    nc.vector.tensor_copy(ki_tok[0:n, bass.ds(t, 1), :], kw[slot][0:n, 0:HD].rearrange("p (a c) -> p a c", a=1))
                    nc.vector.tensor_scalar(wi_tok[0:n, bass.ds(t, 1), :], kw[slot][0:n, HD:KI_ROWS].rearrange("p (a c) -> p a c", a=1),
                                            float(NIH) ** -0.5, None, ALU.mult).then_inc(ki_kept, 1)
                dve.wait_ge(u_turned, 1)
                nc.vector.tensor_copy(utok[:], pu[0:HIST + S, :]).then_inc(u_kept, 1)


ROUNDS = 28
BIG = 1e30
NQ = 4
IDX_SCALE = float(HD) ** -0.5
SM_SCALE = float(HD) ** -0.5


class ThresholdMemory:

    def __init__(self, ph, n, rows=P):
        self.low, self.width, self.mid, self.count, self.step, self.high, self.top, self.need = (
            ph.sb(f"th_{x}", [rows, n]) for x in ("low", "width", "mid", "count", "step", "high", "top", "need"))


def search_start(ch, nc, th):
    ch.link(nc.vector.tensor_tensor(th.width[:], th.top[:], th.low[:], ALU.subtract))
    ch.link(nc.vector.tensor_scalar(th.width[:], th.width[:], 2.0, 1e-30, ALU.mult, ALU.add))


def search_middle(ch, nc, th):
    ch.link(nc.vector.tensor_scalar(th.width[:], th.width[:], 0.5, None, ALU.mult))
    ch.link(nc.vector.tensor_tensor(th.mid[:], th.low[:], th.width[:], ALU.add))


def select_row_tile(ch, nc, score, low, high, need, sure, edge, run):
    ch.link(nc.vector.tensor_scalar(sure, score, high, None, ALU.is_gt, ALU.add, accum_out=need))
    ch.mark(nc.vector.tensor_scalar(need, need, -1.0, float(TOPK), ALU.mult, ALU.add))
    ch.link(nc.vector.scalar_tensor_tensor(edge, score, low, sure, ALU.is_ge, ALU.subtract))
    ch.link(nc.vector.tensor_tensor_scan(run, edge, edge, 0.0, ALU.add, ALU.max))
    ch.link(nc.vector.scalar_tensor_tensor(edge, run, need, edge, ALU.is_le, ALU.mult))
    ch.link(nc.vector.scalar_tensor_tensor(sure, edge, -1.0, sure, ALU.add, ALU.add))
    ch.link(nc.vector.tensor_scalar(sure, sure, BIG, None, ALU.mult))


def attend_prompt_class(nc, c, mem, cls):
    L = 512 * (cls + 1)
    G = cls + 1
    units = [(u, min(u + 1024, L)) for u in range(0, L, 1024)]
    U = len(units)
    TG = 8 * G + 2
    Q0 = 512 * cls
    th = mem.th
    with Phase(nc, f"a{cls}_") as ph:
        qi_loaded = [ph.sem(f"qi_loaded{i}") for i in range(2)]
        q_loaded = [ph.sem(f"q_loaded{i}") for i in range(2)]
        dots_full, dots_kept, relu_used, qi_used = (
            ph.sem(n) for n in ("dots_full", "dots_kept", "relu_used", "qi_used"))
        mid_ready, act_counted = ph.sem("mid_ready"), ph.sem("act_counted")
        s_full, s_kept, max_ready, exp_done, t_done, t_full, t_kept, pv_done, o_done, ot_full, o_stored = (
            ph.sem(n) for n in ("s_full", "s_kept", "max_ready", "exp_done", "t_done", "t_full", "t_kept", "pv_done",
                                "o_done", "ot_full", "o_stored"))
        s_chain, seen = ph.sem("chain"), ph.sem("seen")

        def tiles(e):
            with e.Fori(0, NQ // 2) as i:
                yield i, 0, 2 * i
                yield i, 1, 2 * i + 1

        with ph.block() as block:
            @block.sync
            def _(sp):
                for i, slot, j in tiles(sp):
                    sp.wait_ge(qi_used, j + 1)
                    sp.dma_start(mem.qi_st[0:HD, slot], c.featT[COL_QI:COL_KI, bass.ds(j * P + Q0, P)].rearrange("(h d) t -> d h t", d=HD)).then_inc(qi_loaded[slot], 16)
                for i, slot, j in tiles(sp):
                    sp.wait_ge(pv_done, 8 * j + 2)
                    for gl in range(2):
                        for gh in range(2):
                            r0 = COL_Q + (2 * gh + gl) * P
                            sp.dma_start(mem.q_st[gl * HD:(gl + 1) * HD, slot, 4 * gh + 2 * gl:4 * gh + 2 * gl + 2], c.featT[r0:r0 + P, bass.ds(j * P + Q0, P)].rearrange("(r d) t -> d r t", d=HD)).then_inc(q_loaded[slot], 16)

            @block.tensor
            def _(pe):
                pe.sem_inc(qi_used, 2)
                for i, slot, j in tiles(pe):
                    pe.wait_ge(qi_loaded[slot], 16 * i + 16)
                    for kc in range(G):
                        for hp in range(4):
                            pe.wait_ge(dots_kept, j * (4 * G) + (4 * kc + hp + 1))
                            for h in range(2):
                                m = nc.tensor.matmul(mem.ps_s[hp % 2][:, h * 512:(h + 1) * 512], mem.qi_st[:, slot, 2 * hp + h, :],
                                                     mem.kiT[:, kc * 512:(kc + 1) * 512], start=True, stop=True)
                            m.then_inc(dots_full, 1)
                    pe.wait_ge(dots_full, j * (4 * G) + 4 * G)
                    pe.sem_inc(qi_used, 1)
                pe.sem_inc(t_done, 2)
                pe.sem_inc(pv_done, 2)
                pe.wait_ge(dots_kept, 4 * G * NQ + 2)
                for i, slot, j in tiles(pe):
                    pe.wait_ge(q_loaded[slot], 64 * i + 64)

                    def scores(h):
                        for u, (a, b) in enumerate(units):
                            n = h * U + u
                            pe.wait_ge(s_kept, j * (8 * U) + (n + 1))
                            for k in range(a, b, 512):
                                m = nc.tensor.matmul(mem.ps_s[n % 2][:, k - a:k - a + 512], mem.q_st[:, slot, h, :],
                                                     mem.kT[:, h // 4, k:k + 512], start=True, stop=True)
                            m.then_inc(s_full, 1)

                    def turn(h):
                        pe.wait_ge(exp_done, 8 * j + (h + 1))
                        for g in range(G):
                            n = h * G + g
                            pe.wait_ge(t_kept, j * TG + (n + 1))
                            for b in range(4):
                                k = 4 * g + b
                                m = nc.tensor.transpose(mem.ps_t[n % 2][:, b * P:(b + 1) * P], mem.sm[:, h % 2, k * P:(k + 1) * P], c.ident[:])
                            m.then_inc(t_full, 1)
                        pe.wait_ge(t_full, j * TG + (h + 1) * G)
                        pe.sem_inc(t_done, 1)

                    def values(h):
                        pe.wait_ge(o_done, 8 * j + (h + 1))
                        pe.wait_ge(t_kept, j * TG + ((h + 1) * G + 2))
                        for k in range(4 * G):
                            m = nc.tensor.matmul(mem.ps_o[h % 2][:, 0:P], mem.pT[:, h % 2, k, :],
                                                 mem.v_tok[:, k, (h // 4) * P:(h // 4 + 1) * P], start=(k == 0), stop=(k == 4 * G - 1))
                        m.then_inc(pv_done, 1)

                    scores(0)
                    for h in range(NH):
                        if h + 1 < NH:
                            scores(h + 1)
                        turn(h)
                        if h:
                            values(h - 1)
                    values(NH - 1)
                    pe.wait_ge(o_done, 8 * j + 10)
                    for n in range(2):
                        pe.wait_ge(t_kept, j * TG + (8 * G + n + 1))
                        for b in range(2):
                            m = nc.tensor.transpose(mem.ps_t[n][:, b * P:(b + 1) * P], mem.o_sb[:, (2 * n + b) * P:(2 * n + b + 1) * P], c.ident[:])
                        m.then_inc(t_full, 1)
                    pe.wait_ge(t_full, j * TG + TG)
                    pe.sem_inc(ot_full, 1)

            @block.scalar
            def _(act):
                act.sem_inc(dots_kept, 2)
                for i, slot, j in tiles(act):
                    for kc in range(G):
                        for hp in range(4):
                            n = 4 * kc + hp + 1
                            act.wait_ge(dots_full, j * (4 * G) + n)
                            act.wait_ge(relu_used, j * (4 * G) + n)
                            nc.scalar.activation(mem.relu[:, hp % 2], mem.ps_s[hp % 2][:].rearrange("p (h k) -> p h k", h=2), ACT.Relu,
                                                 scale=IDX_SCALE).then_inc(dots_kept, 1)
                with act.Fori(0, ROUNDS) as r:
                    act.wait_ge(mid_ready, r + 1)
                    for j in (2, 3):
                        act.wait_ge(act_counted, 2 * r + (j - 2))
                        nc.scalar.activation(mem.junk_act[:, 0:L], mem.sc[:, j, 0:L], ACT.Sign, bias=th.mid[:, j:j + 1], scale=-1.0,
                                             accum_out=th.count[:, j:j + 1]).then_inc(act_counted, 1)
                act.sem_inc(t_kept, 2)
                for i, slot, j in tiles(act):
                    for h in range(NH):
                        act.wait_ge(max_ready, 8 * j + (h + 1))
                        nc.scalar.activation(mem.sm[:, h % 2, 0:L], mem.sm[:, h % 2, 0:L], ACT.Exp, bias=mem.negmax[:, h:h + 1],
                                             scale=SM_SCALE, accum_out=mem.total[:, h:h + 1]).then_inc(exp_done, 1)
                        act.wait_ge(pv_done, 8 * j + (h + 1))
                        for g in range(G):
                            act.wait_ge(t_full, j * TG + (h * G + g + 1))
                            nc.scalar.copy(mem.pT[:, h % 2, 4 * g:4 * g + 4, :], mem.ps_t[(h * G + g) % 2][:].rearrange("p (b q) -> p b q", b=4)).then_inc(t_kept, 1)
                    act.wait_ge(o_stored, 16 * j)
                    for n in range(2):
                        act.wait_ge(t_full, j * TG + (8 * G + n + 1))
                        nc.scalar.copy(mem.oT_st[:, 2 * n:2 * n + 2, :], mem.ps_t[n][:, 0:2 * P].rearrange("p (b q) -> p b q", b=2)).then_inc(t_kept, 1)

            @block.vector
            def _(dve):
                ch = Chain(dve, s_chain)
                dve.sem_inc(relu_used, 2)
                for i, slot, j in tiles(dve):
                    ch.link(nc.vector.tensor_copy(mem.wi_now[:], mem.wi_tok[:, bass.ds(j + NQ * cls, 1), :]))
                    for kc in range(G):
                        at = mem.sc[:, bass.ds(j, 1), kc * 512:(kc + 1) * 512]
                        for hp in range(4):
                            dve.wait_ge(dots_kept, j * (4 * G) + (4 * kc + hp + 3))
                            for h in range(2):
                                src, w = mem.relu[:, hp % 2, h:h + 1, :], mem.wi_now[:, 0, 2 * hp + h:2 * hp + h + 1]
                                if hp == 0 and h == 0:
                                    ch.link(nc.vector.tensor_scalar(at, src, w, None, ALU.mult))
                                else:
                                    ch.link(nc.vector.scalar_tensor_tensor(at, src, w, at, ALU.mult, ALU.add))
                            dve.sem_inc(relu_used, 1)
                    row = mem.sc[:, bass.ds(j, 1), 0:L]
                    last = mem.sc[:, bass.ds(j, 1), L - 512:L]
                    ch.mark(nc.vector.tensor_reduce(th.low[:, bass.ds(j, 1)], row, AX.X, ALU.min))
                    ch.link(nc.vector.tensor_scalar(mem.edge[:, 0:512], mem.key_no[:], mem.query_no[:, bass.ds(j, 1)], -BIG, ALU.is_gt, ALU.mult))
                    ch.link(nc.vector.tensor_tensor(last, last, mem.edge[:, 0:512].rearrange("p (a k) -> p a k", a=1), ALU.add))
                    ch.link(nc.vector.tensor_reduce(th.top[:, bass.ds(j, 1)], row, AX.X, ALU.max))
                    ch.restart()
                search_start(ch, nc, th)
                ch.restart()
                with dve.Fori(0, ROUNDS) as r:
                    search_middle(ch, nc, th)
                    dve.sem_inc(mid_ready, 1)
                    for j in (0, 1):
                        ch.link(nc.vector.tensor_scalar(mem.junk_dve[:, 0:L], mem.sc[:, j, 0:L], th.mid[:, j:j + 1], None, ALU.is_ge, ALU.add,
                                                        accum_out=th.count[:, j:j + 1]))
                    ch.mark(nc.vector.scalar_tensor_tensor(th.step[:, 0:2], th.count[:, 0:2], TOPK - 0.5, th.width[:, 0:2], ALU.is_ge, ALU.mult))
                    dve.wait_ge(act_counted, 2 * r + 2)
                    ch.link(nc.vector.scalar_tensor_tensor(th.step[:, 2:4], th.count[:, 2:4], L - 2 * TOPK + 0.5, th.width[:, 2:4], ALU.is_le, ALU.mult))
                    ch.link(nc.vector.tensor_tensor(th.low[:], th.low[:], th.step[:], ALU.add))
                    ch.restart()
                ch.link(nc.vector.scalar_tensor_tensor(th.high[:], th.width[:], 4.0, th.low[:], ALU.mult, ALU.add))
                ch.restart()
                dve.sem_inc(s_kept, 2)
                dve.sem_inc(o_done, 2)
                for i, slot, j in tiles(dve):
                    jj = bass.ds(j, 1)
                    ch.mark(nc.vector.tensor_copy(mem.bounds[:, 0:1], th.low[:, jj]))
                    ch.link(nc.vector.tensor_copy(mem.bounds[:, 1:2], th.high[:, jj]))
                    ch.link(nc.vector.tensor_copy(mem.run[:, 0:L], mem.sc[:, jj, 0:L].rearrange("p a k -> p (a k)")))
                    select_row_tile(ch, nc, mem.run[:, 0:L], mem.bounds[:, 0:1], mem.bounds[:, 1:2], mem.bounds[:, 2:3],
                                    mem.mask[:, 0:L], mem.edge[:, 0:L], mem.run[:, 0:L])

                    def normalise(h):
                        dve.wait_ge(exp_done, 8 * j + (h + 1))
                        ch.link(nc.vector.reciprocal(mem.inv[:, h:h + 1], mem.total[:, h:h + 1]))
                        dve.wait_ge(pv_done, 8 * j + (h + 3))
                        if h == 0:
                            dve.wait_ge(ot_full, j)
                        at = (h // 2 % 2) * HD
                        nc.vector.tensor_scalar(mem.o_sb[:, h * HD:(h + 1) * HD], mem.ps_o[h % 2][:, at:at + HD], mem.inv[:, h:h + 1], None,
                                                ALU.mult).then_inc(o_done, 1)

                    for h in range(NH):
                        dve.wait_ge(t_done, 8 * j + (h + 1))
                        for u, (a, b) in enumerate(units):
                            n = h * U + u
                            dve.wait_ge(s_full, j * (8 * U) + (n + 1))
                            dve.sem_inc(seen, 1)
                            start = -3e38 if u == 0 else mem.max2[:, u - 1:u]
                            ch.link(nc.vector.tensor_tensor_reduce(mem.sm[:, h % 2, a:b], mem.ps_s[n % 2][:, 0:b - a], mem.mask[:, a:b], 1.0, start,
                                                                   ALU.add, ALU.max, mem.max2[:, u:u + 1]))
                            dve.sem_inc(s_kept, 1)
                        if h == 0:
                            dve.wait_ge(exp_done, 8 * j)
                        nc.vector.tensor_scalar(mem.negmax[:, h:h + 1], mem.max2[:, U - 1:U], -SM_SCALE, None, ALU.mult).then_inc(max_ready, 1)
                        dve.wait_ge(max_ready, 8 * j + (h + 1))
                        if h >= 2:
                            normalise(h - 2)
                    normalise(NH - 2)
                    normalise(NH - 1)
                    ch.restart()

            @block.gpsimd
            def _(pool):
                for i, slot, j in tiles(pool):
                    pool.wait_ge(t_kept, j * TG + (TG + 2))
                    pool.dma_start(c.oT[:, bass.ds(j * P + Q0, P)].rearrange("(b p) t -> p b t", p=P), mem.oT_st[:]).then_inc(o_stored, 16)
                pool.wait_ge(o_stored, 16 * NQ)


def attend_prompt(nc, c, kT, kiT, v_tok, wi_tok):
    with Phase(nc, "q_") as ph:
        mem = Ctx()
        mem.kT, mem.kiT, mem.v_tok, mem.wi_tok = kT, kiT, v_tok, wi_tok
        mem.th = ThresholdMemory(ph, NQ)
        mem.qi_st = ph.sb("qi_st", [P, 2, NIH, P])
        mem.q_st = ph.sb("q_st", [P, 2, NH, P])
        mem.wi_now = ph.sb("wi_now", [P, 1, NIH])
        mem.sc = ph.sb("sc", [P, NQ, T])
        mem.relu = ph.sb("relu", [P, 2, 2, 512])
        mem.key_no = ph.sb("key_no", [P, 512])
        mem.query_no = ph.sb("query_no", [P, NQ])
        mem.junk_act = ph.sb("junk_act", [P, T], mybir.dt.bfloat16)
        mem.junk_dve = ph.sb("junk_dve", [P, T], mybir.dt.bfloat16)
        mem.bounds = ph.sb("bounds", [P, 4])
        mem.mask, mem.edge, mem.run = (ph.sb(n, [P, T]) for n in ("mask", "edge", "run"))
        mem.sm = ph.sb("sm", [P, 2, T])
        mem.max2, mem.negmax, mem.total, mem.inv = (ph.sb(n, [P, w]) for n, w in (("max2", 2), ("negmax", NH), ("total", NH), ("inv", NH)))
        mem.pT = ph.sb("pT", [P, 2, NT, P])
        mem.o_sb = ph.sb("o_sb", [P, NH * HD])
        mem.oT_st = ph.sb("oT_st", [P, 4, P])
        mem.ps_s = [ph.ps(f"s{i}", [P, 1024]) for i in range(2)]
        mem.ps_t = [ph.ps(f"t{i}", [P, 512]) for i in range(2)]
        mem.ps_o = [ph.ps(f"o{i}", [P, 512]) for i in range(2)]
        made = ph.sem("made")
        with ph.block() as block:
            @block.vector
            def _(dve):
                nc.vector.memset(mem.q_st[:], 0.0)
                nc.vector.memset(mem.qi_st[:], 0.0)
                nc.vector.memset(kiT[HD:P], 0.0)

            @block.gpsimd
            def _(pool):
                nc.gpsimd.iota(mem.key_no[:], [[1, 512]], base=0, channel_multiplier=0, allow_small_or_imprecise_dtypes=True).then_inc(made, 1)
                nc.gpsimd.iota(mem.query_no[:], [[P, NQ]], base=0, channel_multiplier=1, allow_small_or_imprecise_dtypes=True).then_inc(made, 1)
                pool.wait_ge(made, 2)
        for cls in range(NT // NQ):
            attend_prompt_class(nc, c, mem, cls)


class Ctx:
    pass


LS = 2048 + DS
CHUNKS = [(i * 512, 512) for i in range(4)] + [(2048, DS)]
SLOTS = 16
N_PAGES, PAGE = 16, 128


def sample_index(nc, c, mem):
    with Phase(nc, "i_") as ph:
        page_of = ph.sb("page_of", [P, DB], I32)
        part = ph.sb("part", [P, 1], I32)
        fl = ph.sb("fl", [P, DB])
        partf = ph.sb("partf", [P, 1])
        kid = ph.sb("kid", [P, 2, SLOTS * HD])
        kiT = ph.sb("kiT", [P, 2, LS])
        qis = ph.sb("qis", [P, DB, NIH, DS])
        dots = ph.sb("dots", [P, 2, LS])
        wcol = ph.sb("wcol", [P, 2])
        wsel = ph.sb("wsel", [P, 2, S])
        sc, edge, run = (ph.sb(n, [S, LS]) for n in ("sc", "edge", "run"))
        junk = ph.sb("junk", [S, LS], mybir.dt.bfloat16)
        newpos = ph.sb("newpos", [S, DS])
        qmod = ph.sb("qmod", [S, 1])
        bounds = ph.sb("bounds", [S, 1])
        th = ThresholdMemory(ph, 1, S)
        pt = [ph.ps(f"t{i}", [P, 512]) for i in range(2)]
        pd = [ph.ps(f"d{i}", [P, 512]) for i in range(2)]
        pc = [ph.ps(f"c{i}", [P, 512]) for i in range(2)]
        table_loaded, rows_ready, zeroed, made, q_loaded, w_loaded = (ph.sem(n) for n in ("table_loaded", "rows_ready", "zeroed", "made", "q_loaded", "w_loaded"))
        kid_loaded = [ph.sem(f"kid_loaded{i}") for i in range(2)]
        new_loaded = [ph.sem(f"new_loaded{i}") for i in range(2)]
        turned, keys_kept, dots_full, dots_kept, sel_turned, sel_ready, sum_full, sum_kept, s_chain = (
            ph.sem(n) for n in ("turned", "keys_kept", "dots_full", "dots_kept", "sel_turned", "sel_ready", "sum_full", "sum_kept", "chain"))
        with ph.block() as block:
            @block.sync
            def _(sp):
                table = c.inp["page_table"].rearrange("b (g a) -> g a b", a=1)
                for g in range(N_PAGES):
                    sp.dma_start(page_of[8 * g:8 * g + 8, :], table[g].to_broadcast([8, DB]), allow_slow_non_contiguous=True).then_inc(table_loaded, 16)
                sp.wait_ge(zeroed, 1)
                for h in range(NIH):
                    sp.dma_start(qis[0:HD, :, h, :], c.featT[COL_QI + h * HD:COL_QI + (h + 1) * HD, T:TT].rearrange("d (b q) -> d b q", b=DB)).then_inc(q_loaded, 16)
                for g in range(2):
                    for b in range(4):
                        sp.dma_start(wcol[32 * b:32 * b + 32, g:g + 1], c.featT[COL_WI:COL_G, T + 4 * (4 * g + b):T + 4 * (4 * g + b) + 4],
                                     allow_slow_non_contiguous=True).then_inc(w_loaded, 16)
                for b in range(DB):
                    if b >= 2:
                        sp.wait_ge(dots_full, 5 * (b - 1))
                    sp.dma_start(kiT[0:HD, b % 2, 2048:LS], c.featT[COL_KI:COL_WI, T + DS * b:T + DS * b + DS], allow_slow_non_contiguous=True).then_inc(new_loaded[b % 2], 16)

            @block.gpsimd
            def _(pool):
                nc.gpsimd.iota(part[:], [[0, 1]], base=0, channel_multiplier=1).then_inc(made, 1)
                nc.gpsimd.iota(newpos[:], [[1, DS]], base=0, channel_multiplier=0, allow_small_or_imprecise_dtypes=True).then_inc(made, 1)
                nc.gpsimd.memset(mem.selT[:], 0.0).then_inc(made, 1)
                pool.wait_ge(made, 3)
                for g in range(2):
                    v = mem.selT[:, g].rearrange("r (b h q) -> r b h q", b=4, h=NIH)
                    nc.gpsimd.affine_select(out=v, in_=v, compare_op=ALU.not_equal, fill=1.0, base=-16 * g,
                                            pattern=[[-4, 4], [0, NIH], [-1, DS]], channel_multiplier=1).then_inc(made, 1)
                pool.wait_ge(rows_ready, 1)
                pool_rows = c.inp["cache_kidx"][0].rearrange("n (a s) d -> (n a) (s d)", s=SLOTS)
                for b in range(DB):
                    if b >= 2:
                        pool.wait_ge(turned, 4 * (b - 1))
                    pool.indirect_dma_start(kid[:, b % 2, :], None, pool_rows, bass.IndirectOffsetOnAxis(ap=mem.row_no[:, b:b + 1], axis=0)).then_inc(kid_loaded[b % 2], 16)

            @block.tensor
            def _(pe):
                def turn(b):
                    pe.wait_ge(kid_loaded[b % 2], 16 * (b // 2 + 1))
                    for t in range(4):
                        e = 4 * b + t
                        if e >= 2:
                            pe.wait_ge(keys_kept, e - 1)
                        for s in range(4):
                            k = 4 * t + s
                            m = nc.tensor.transpose(pt[e % 2][0:HD, s * P:(s + 1) * P], kid[:, b % 2, k * HD:(k + 1) * HD], c.ident[:])
                        m.then_inc(turned, 1)

                turn(0)
                pe.wait_ge(q_loaded, 16 * NIH)
                for b in range(DB):
                    if b + 1 < DB:
                        turn(b + 1)
                    pe.wait_ge(keys_kept, 4 * (b + 1))
                    pe.wait_ge(new_loaded[b % 2], 16 * (b // 2 + 1))
                    for n, (k0, w) in enumerate(CHUNKS):
                        e = 5 * b + n
                        if e >= 2:
                            pe.wait_ge(dots_kept, e - 1)
                        p0 = 32 * (b % 4)
                        nc.tensor.matmul(pd[e % 2][p0:p0 + 32, 0:w], qis[:, b].rearrange("d h q -> d (h q)"), kiT[:, b % 2, k0:k0 + w], start=True, stop=True).then_inc(dots_full, 1)
                pe.wait_ge(made, 5)
                for g in range(2):
                    m = nc.tensor.transpose(pt[g][:, 0:S], mem.selT[:, g], c.ident[0:S, 0:S])
                m.then_inc(sel_turned, 1)
                pe.wait_ge(sel_ready, 2)
                pe.wait_ge(dots_kept, 5 * DB)
                for n, (k0, w) in enumerate(CHUNKS):
                    if n >= 2:
                        pe.wait_ge(sum_kept, n - 1)
                    for g in range(2):
                        m = nc.tensor.matmul(pc[n % 2][0:S, 0:w], wsel[:, g, :], dots[:, g, k0:k0 + w], start=(g == 0), stop=(g == 1))
                    m.then_inc(sum_full, 1)

            @block.scalar
            def _(act):
                for b in range(DB):
                    p0 = 32 * (b % 4)
                    for n, (k0, w) in enumerate(CHUNKS):
                        e = 5 * b + n
                        act.wait_ge(dots_full, e + 1)
                        nc.scalar.activation(dots[p0:p0 + 32, b // 4, k0:k0 + w], pd[e % 2][p0:p0 + 32, 0:w], ACT.Relu, scale=IDX_SCALE).then_inc(dots_kept, 1)

            @block.vector
            def _(dve):
                ch = Chain(dve, s_chain)
                ch.mark(nc.vector.memset(qis[:], 0.0))
                ch.mark(nc.vector.memset(kiT[:], 0.0))
                ch.sync()
                dve.sem_inc(zeroed, 1)
                dve.wait_ge(table_loaded, 16 * N_PAGES)
                dve.wait_ge(made, 2)
                ch.mark(nc.vector.tensor_copy(fl[:], page_of[:]))
                ch.link(nc.vector.tensor_scalar(part[:], part[:], 7, None, ALU.bitwise_and))
                ch.link(nc.vector.tensor_copy(partf[:], part[:]))
                ch.link(nc.vector.tensor_scalar(mem.row_no[:], fl[:], 8.0, partf[:], ALU.mult, ALU.add))
                dve.sem_inc(rows_ready, 1)
                ch.link(nc.vector.tensor_scalar(part[0:S], part[0:S], 3, None, ALU.bitwise_and))
                ch.link(nc.vector.tensor_copy(qmod[:], part[0:S]))
                for b in range(DB):
                    if b >= 2:
                        dve.wait_ge(dots_full, 5 * (b - 1))
                    for t in range(4):
                        e = 4 * b + t
                        dve.wait_ge(turned, e + 1)
                        out = kiT[0:HD, b % 2, 0:2048].rearrange("d (p s) -> d s p", s=SLOTS)[:, 4 * t:4 * t + 4, :]
                        nc.vector.tensor_copy(out, pt[e % 2][0:HD, :].rearrange("d (s p) -> d s p", s=4)).then_inc(keys_kept, 1)
                dve.wait_ge(sel_turned, 1)
                dve.wait_ge(w_loaded, 128)
                for g in range(2):
                    nc.vector.tensor_scalar(wsel[:, g, :], pt[g][:, 0:S], wcol[:, g:g + 1], float(NIH) ** -0.5, ALU.mult, ALU.mult).then_inc(sel_ready, 1)
                for n, (k0, w) in enumerate(CHUNKS):
                    dve.wait_ge(sum_full, n + 1)
                    nc.vector.tensor_copy(sc[:, k0:k0 + w], pc[n % 2][0:S, 0:w]).then_inc(sum_kept, 1)
                dve.wait_ge(sum_kept, len(CHUNKS))
                ch.link(nc.vector.tensor_reduce(th.low[:], sc[:], AX.X, ALU.min))
                ch.link(nc.vector.tensor_scalar(newpos[:], newpos[:], qmod[:], -BIG, ALU.is_gt, ALU.mult))
                ch.link(nc.vector.tensor_tensor(sc[:, 2048:LS], sc[:, 2048:LS], newpos[:], ALU.add))
                ch.link(nc.vector.tensor_reduce(th.top[:], sc[:], AX.X, ALU.max))
                search_start(ch, nc, th)
                ch.restart()
                with dve.Fori(0, ROUNDS):
                    search_middle(ch, nc, th)
                    ch.link(nc.vector.tensor_scalar(junk[:], sc[:], th.mid[:], None, ALU.is_ge, ALU.add, accum_out=th.count[:]))
                    ch.link(nc.vector.scalar_tensor_tensor(th.step[:], th.count[:], TOPK - 0.5, th.width[:], ALU.is_ge, ALU.mult))
                    ch.link(nc.vector.tensor_tensor(th.low[:], th.low[:], th.step[:], ALU.add))
                    ch.restart()
                ch.link(nc.vector.scalar_tensor_tensor(th.high[:], th.width[:], 4.0, th.low[:], ALU.mult, ALU.add))
                select_row_tile(ch, nc, sc[:], th.low[:], th.high[:], bounds[:], mem.mask[:], edge[:], run[:])


def sample_attend(nc, c, mem):
    with Phase(nc, "s_") as ph:
        masks = ph.sb("masks", [P, 2, LS])
        sm = ph.sb("sm", [P, 2, LS])
        kk = ph.sb("kk", [P, 2, SLOTS * 2 * P])
        vv = ph.sb("vv", [P, 2, SLOTS * 2 * P])
        kT = ph.sb("kT", [P, 2, 2, LS])
        pT = ph.sb("pT", [P, SLOTS + 1, P])
        qbd = ph.sb("qbd", [P, DB, 2, NH, DS])
        vnew = ph.sb("vnew", [DS, DB, 2 * P])
        own = ph.sb("own", [P, 4, NKV])
        own_kv = ph.sb("own_kv", [P, NKV])
        part = ph.sb("part", [P, NKV])
        top = ph.sb("top", [P, 2, len(CHUNKS)])
        negmax, total = ph.sb("negmax", [P, 2]), ph.sb("total", [P, 2])
        o = ph.sb("o", [P, 2, HD])
        oT = ph.sb("oT", [HD, 2, P])
        pt = [ph.ps(f"t{i}", [P, 512]) for i in range(4)]
        pss = [ph.ps(f"s{i}", [P, 512]) for i in range(2)]
        po = ph.ps("o", [P, 512])
        pot = ph.ps("ot", [P, 512])
        zeroed, q_loaded, made, v_new_loaded = (ph.sem(n) for n in ("zeroed", "q_loaded", "made", "v_new_loaded"))
        k_loaded = [ph.sem(f"k_loaded{i}") for i in range(2)]
        v_loaded = [ph.sem(f"v_loaded{i}") for i in range(2)]
        new_loaded = [ph.sem(f"new_loaded{i}") for i in range(2)]
        mask_full, mask_kept, turned, s_full, s_kept, max_ready, exp_done, p_turned, pv_done, o_ready, o_turned, oT_kept, o_stored = (
            ph.sem(n) for n in ("mask_full", "mask_kept", "turned", "s_full", "s_kept", "max_ready", "exp_done", "p_turned", "pv_done", "o_ready",
                                "o_turned", "oT_kept", "o_stored"))
        kept = [ph.sem(f"kept{i}") for i in range(2)]
        p_kept = [ph.sem(f"p_kept{i}") for i in range(2)]
        s_chain = ph.sem("chain")
        NG = SLOTS // 4
        with ph.block() as block:
            @block.sync
            def _(sp):
                sp.wait_ge(zeroed, 1)
                for h in range(NH):
                    g = h // 2
                    p0 = (g % 2) * HD
                    sp.dma_start(qbd[p0:p0 + HD, :, g // 2, h, :], c.featT[COL_Q + h * HD:COL_Q + (h + 1) * HD, T:TT].rearrange("d (b q) -> d b q", b=DB)).then_inc(q_loaded, 16)
                sp.dma_start(vnew[:], c.out["v_sample"][0].rearrange("b q h d -> q b (h d)")).then_inc(v_new_loaded, 16)
                for b in range(DB):
                    if b >= 2:
                        sp.wait_ge(s_full, 5 * (b - 1))
                    sp.dma_start(kT[:, b % 2, :, 2048:LS], c.featT[COL_K:COL_V, T + DS * b:T + DS * b + DS].rearrange("(g p) t -> p g t", p=P),
                                 allow_slow_non_contiguous=True).then_inc(new_loaded[b % 2], 16)

            @block.gpsimd
            def _(pool):
                k_rows = c.inp["cache_k"][0].rearrange("n (a s) h d -> (n a) (s h d)", s=SLOTS)
                v_rows = c.inp["cache_v"][0].rearrange("n (a s) h d -> (n a) (s h d)", s=SLOTS)

                def load_k(b):
                    if b >= 2:
                        pool.wait_ge(turned, 8 * (b - 1))
                    pool.indirect_dma_start(kk[:, b % 2, :], None, k_rows, bass.IndirectOffsetOnAxis(ap=mem.row_no[:, b:b + 1], axis=0)).then_inc(k_loaded[b % 2], 16)

                def load_v(b):
                    if b >= 2:
                        pool.wait_ge(pv_done, b - 1)
                    pool.indirect_dma_start(vv[:, b % 2, :], None, v_rows, bass.IndirectOffsetOnAxis(ap=mem.row_no[:, b:b + 1], axis=0)).then_inc(v_loaded[b % 2], 16)

                load_k(0)
                load_k(1)
                nc.gpsimd.memset(own[:], 1.0).then_inc(made, 1)
                pool.wait_ge(made, 1)
                nc.gpsimd.affine_select(out=own[:], in_=own[:], compare_op=ALU.is_ge, fill=0.0, base=0, pattern=[[-32, 4], [-8, NKV]], channel_multiplier=1).then_inc(made, 1)
                pool.wait_ge(made, 2)
                nc.gpsimd.affine_select(out=own[:], in_=own[:], compare_op=ALU.is_ge, fill=0.0, base=7, pattern=[[32, 4], [8, NKV]], channel_multiplier=-1).then_inc(made, 1)
                load_v(0)
                load_v(1)
                load_k(2)
                load_k(3)
                load_k(4)
                load_k(5)
                for b in (2, 3, 4, 5):
                    load_v(b)
                load_k(6)
                load_k(7)
                load_v(6)
                load_v(7)
                for g in range(2):
                    pool.wait_ge(oT_kept, g + 1)
                    for b in range(4):
                        t0 = T + 16 * g + 4 * b
                        pool.dma_start(c.oT[:, t0:t0 + DS].rearrange("(h d) q -> d h q", d=HD), oT[:, g, 32 * b:32 * b + 32].rearrange("d (h q) -> d h q", h=NH)).then_inc(o_stored, 16)
                pool.wait_ge(o_stored, 128)

            @block.tensor
            def _(pe):
                for g in range(2):
                    for n, (k0, w) in enumerate(CHUNKS):
                        e = 5 * g + n
                        if e >= 2:
                            pe.wait_ge(mask_kept, e - 1)
                        nc.tensor.matmul(pss[e % 2][:, 0:w], mem.selT[:, g], mem.mask[:, k0:k0 + w], start=True, stop=True).then_inc(mask_full, 1)

                def turn(b):
                    pe.wait_ge(k_loaded[b % 2], 16 * (b // 2 + 1))
                    for t in range(NG):
                        for gh in range(2):
                            e = NG * b + t
                            if e >= 2:
                                pe.wait_ge(kept[gh], e - 1)
                            for s in range(4):
                                k = (4 * t + s) * 2 * P + gh * P
                                m = nc.tensor.transpose(pt[2 * gh + e % 2][:, s * P:(s + 1) * P], kk[:, b % 2, k:k + P], c.ident[:])
                            m.then_inc(turned, 1)

                def scores(b):
                    pe.wait_ge(kept[0], NG * (b + 1))
                    pe.wait_ge(kept[1], NG * (b + 1))
                    pe.wait_ge(new_loaded[b % 2], 16 * (b // 2 + 1))
                    p0 = 32 * (b % 4)
                    for n, (k0, w) in enumerate(CHUNKS):
                        e = 5 * b + n
                        if e >= 2:
                            pe.wait_ge(s_kept, e - 1)
                        for gh in range(2):
                            m = nc.tensor.matmul(pss[e % 2][p0:p0 + 32, 0:w], qbd[:, b, gh].rearrange("p h q -> p (h q)"), kT[:, b % 2, gh, k0:k0 + w],
                                                 start=(gh == 0), stop=(gh == 1))
                        m.then_inc(s_full, 1)

                def turn_probs(g):
                    pe.wait_ge(kept[0], NG * 4 * (g + 1))
                    pe.wait_ge(kept[1], NG * 4 * (g + 1))
                    pe.wait_ge(exp_done, g + 1)
                    p = sm[:, g, 0:2048].rearrange("r (p s) -> r s p", s=SLOTS)
                    for t in range(NG + 1):
                        if t == NG:
                            pe.wait_ge(p_kept[0], (NG // 2 + 1) * g + 1)
                            m = nc.tensor.transpose(pt[0][0:DS, 0:P], sm[:, g, 2048:LS], c.ident[:])
                        else:
                            for s in range(4):
                                m = nc.tensor.transpose(pt[t][:, s * P:(s + 1) * P], p[:, 4 * t + s, :], c.ident[:])
                        m.then_inc(p_turned, 1)

                def values(b):
                    g = b // 4
                    p0 = 32 * (b % 4)
                    pe.wait_ge(v_loaded[b % 2], 16 * (b // 2 + 1))
                    pe.wait_ge(p_kept[0], (NG // 2 + 1) * (g + 1))
                    pe.wait_ge(p_kept[1], NG // 2 * (g + 1))
                    if b == 4:
                        pe.wait_ge(o_ready, 1)
                    for s in range(SLOTS):
                        nc.tensor.matmul(po[p0:p0 + 32, 0:2 * P], pT[:, s, p0:p0 + 32], vv[:, b % 2, s * 2 * P:(s + 1) * 2 * P], start=(s == 0), stop=False)
                    nc.tensor.matmul(po[p0:p0 + 32, 0:2 * P], pT[0:DS, SLOTS, p0:p0 + 32], vnew[:, b, :], start=False, stop=True).then_inc(pv_done, 1)

                pe.wait_ge(q_loaded, 16 * NH)
                pe.wait_ge(mask_kept, 10)
                pe.wait_ge(v_new_loaded, 16)
                for g in range(2):
                    turn(4 * g)
                    for b in range(4 * g, 4 * g + 4):
                        if b % 4 < 3:
                            turn(b + 1)
                        scores(b)
                    turn_probs(g)
                    for b in range(4 * g, 4 * g + 4):
                        values(b)
                    pe.wait_ge(o_ready, g + 1)
                    if g:
                        pe.wait_ge(oT_kept, g)
                    nc.tensor.transpose(pot[0:HD, 0:P], o[:, g, :], c.ident[:]).then_inc(o_turned, 1)

            @block.scalar
            def _(act):
                for g in range(2):
                    for n, (k0, w) in enumerate(CHUNKS):
                        e = 5 * g + n
                        act.wait_ge(mask_full, e + 1)
                        nc.scalar.copy(masks[:, g, k0:k0 + w], pss[e % 2][:, 0:w]).then_inc(mask_kept, 1)
                for g in range(2):
                    for b in range(4 * g, 4 * g + 4):
                        if b >= 2:
                            act.wait_ge(s_full, 5 * (b - 1))
                        for t in range(NG):
                            e = NG * b + t
                            act.wait_ge(turned, 2 * e + 2)
                            out = kT[:, b % 2, 1, 0:2048].rearrange("d (p s) -> d s p", s=SLOTS)[:, 4 * t:4 * t + 4, :]
                            nc.scalar.copy(out, pt[2 + e % 2][:].rearrange("d (s p) -> d s p", s=4)).then_inc(kept[1], 1)
                    act.wait_ge(max_ready, g + 1)
                    nc.scalar.activation(sm[:, g], sm[:, g], ACT.Exp, bias=negmax[:, g:g + 1], scale=SM_SCALE, accum_out=total[:, g:g + 1]).then_inc(exp_done, 1)
                    if g:
                        act.wait_ge(pv_done, 4 * g)
                    for t in (2, 3):
                        act.wait_ge(p_turned, (NG + 1) * g + t + 1)
                        nc.scalar.copy(pT[:, 4 * t:4 * t + 4, :], pt[t][:].rearrange("p (s r) -> p s r", s=4)).then_inc(p_kept[1], 1)
                    act.wait_ge(o_turned, g + 1)
                    nc.scalar.copy(oT[:, g, :], pot[0:HD, 0:P]).then_inc(oT_kept, 1)

            @block.vector
            def _(dve):
                ch = Chain(dve, s_chain)
                ch.link(nc.vector.memset(qbd[:], 0.0))
                dve.sem_inc(zeroed, 1)
                dve.wait_ge(made, 3)
                ch.link(nc.vector.tensor_reduce(own_kv[:], own[:].rearrange("p b g -> p g b"), AX.X, ALU.add))
                dve.wait_ge(mask_kept, 10)

                def keep(b):
                    if b >= 2:
                        dve.wait_ge(s_full, 5 * (b - 1))
                    for t in range(NG):
                        e = NG * b + t
                        dve.wait_ge(turned, 2 * e + 1)
                        out = kT[:, b % 2, 0, 0:2048].rearrange("d (p s) -> d s p", s=SLOTS)[:, 4 * t:4 * t + 4, :]
                        nc.vector.tensor_copy(out, pt[e % 2][:].rearrange("d (s p) -> d s p", s=4)).then_inc(kept[0], 1)

                for g in range(2):
                    keep(4 * g)
                    for b in range(4 * g, 4 * g + 4):
                        if b % 4 < 3:
                            keep(b + 1)
                        p0 = 32 * (b % 4)
                        for n, (k0, w) in enumerate(CHUNKS):
                            dve.wait_ge(s_full, 5 * b + n + 1)
                            start = -3e38 if n == 0 else top[p0:p0 + 32, g, n - 1:n]
                            ch.link(nc.vector.tensor_tensor_reduce(sm[p0:p0 + 32, g, k0:k0 + w], pss[(5 * b + n) % 2][p0:p0 + 32, 0:w], masks[p0:p0 + 32, g, k0:k0 + w],
                                                                   1.0, start, ALU.add, ALU.max, top[p0:p0 + 32, g, n:n + 1]))
                            dve.sem_inc(s_kept, 1)
                    nc.vector.tensor_scalar(negmax[:, g:g + 1], top[:, g, len(CHUNKS) - 1:len(CHUNKS)], -SM_SCALE, None, ALU.mult).then_inc(max_ready, 1)
                    if g:
                        dve.wait_ge(pv_done, 4 * g)
                    for t in (0, 1, NG):
                        dve.wait_ge(p_turned, (NG + 1) * g + t + 1)
                        if t == NG:
                            nc.vector.tensor_copy(pT[0:DS, SLOTS, :], pt[0][0:DS, 0:P]).then_inc(p_kept[0], 1)
                        else:
                            nc.vector.tensor_copy(pT[:, 4 * t:4 * t + 4, :], pt[t][:].rearrange("p (s r) -> p s r", s=4)).then_inc(p_kept[0], 1)
                    ch.link(nc.vector.reciprocal(part[:, 0:1], total[:, g:g + 1]))
                    ch.link(nc.vector.tensor_scalar(part[:], own_kv[:], part[:, 0:1], None, ALU.mult))
                    dve.wait_ge(pv_done, 4 * g + 4)
                    ch.link(nc.vector.tensor_scalar(o[:, g, :], po[:, 0:HD], part[:, 0:1], None, ALU.mult))
                    for kv in range(1, NKV):
                        ch.link(nc.vector.scalar_tensor_tensor(o[:, g, :], po[:, kv * HD:(kv + 1) * HD], part[:, kv:kv + 1], o[:, g, :], ALU.mult, ALU.add))
                    dve.sem_inc(o_ready, 1)


def attend_samples(nc, c):
    with Phase(nc, "m_") as ph:
        mem = Ctx()
        mem.row_no = ph.sb("row_no", [P, DB], I32)
        mem.selT = ph.sb("selT", [S, 2, P])
        mem.mask = ph.sb("mask", [S, LS])
        sample_index(nc, c, mem)
        sample_attend(nc, c, mem)


NG, NE, EPG, F = 4, 32, 8, 256
NL = NG + NE
NTL = NT + 1
NBLK = -(-2 * TT // P) + NE


def tile_pairs(e):
    with e.Fori(0, NT // 2) as i:
        yield i, 0, 2 * i, P
        yield i, 1, 2 * i + 1, P
    yield NT // 2, 0, NT, S


def norm_conv(nc, c, yT):
    with Phase(nc, "n_") as ph:
        ct = ph.sb("ct", [P, 2, CB, P])
        yn = ph.sb("yn", [P, 2, CC])
        stats, mv, eps = ph.sb("stats", [P, 6]), ph.sb("mv", [P, 2, 2]), ph.sb("eps", [P, 2, 2])
        pa = [ph.ps(f"a{i}", [P, 512]) for i in range(2)]
        pb = [ph.ps(f"b{i}", [P, 512]) for i in range(2)]
        loaded = [ph.sem(f"loaded{i}") for i in range(2)]
        made, a_full, var_ready, rstd_ready, yn_ready, b_full, b_kept, s_chain, seen = (
            ph.sem(n) for n in ("made", "a_full", "var_ready", "rstd_ready", "yn_ready", "b_full", "b_kept", "chain", "seen"))
        with ph.block() as block:
            @block.sync
            def _(sp):
                for i, slot, t, n in tile_pairs(sp):
                    sp.wait_ge(a_full, t + 1)
                    sp.dma_start(ct[:, slot, :, 0:n], c.convT[:, bass.ds(t * P, n)].rearrange("(b p) t -> p b t", p=P)).then_inc(loaded[slot], 16)

            @block.tensor
            def _(pe):
                pe.sem_inc(a_full, 2)

                def rows(i, slot, t, n):
                    pe.wait_ge(loaded[slot], 16 * i + 16)
                    pe.wait_ge(yn_ready, t + 1)
                    for b in range(CB):
                        m = nc.tensor.transpose(pa[slot][0:n, b * P:(b + 1) * P], ct[:, slot, b, 0:n], c.ident[:])
                    m.then_inc(a_full, 1)

                def back(slot, t, n):
                    pe.wait_ge(yn_ready, t + 3)
                    pe.wait_ge(b_kept, t + 1)
                    for b in range(CB):
                        m = nc.tensor.transpose(pb[slot][:, b * P:b * P + n], yn[0:n, slot, b * P:(b + 1) * P], c.ident[0:n, 0:n])
                    m.then_inc(b_full, 1)

                with pe.Fori(0, NT // 2) as i:
                    rows(i, 0, 2 * i, P)
                    rows(i, 1, 2 * i + 1, P)
                    back(0, 2 * i, P)
                    back(1, 2 * i + 1, P)
                rows(NT // 2, 0, NT, S)
                back(0, NT, S)

            @block.gpsimd
            def _(pool):
                nc.gpsimd.memset(eps[:], -0.5).then_inc(made, 1)
                pool.wait_ge(made, 1)
                for i, slot, t, n in tile_pairs(pool):
                    pool.wait_ge(var_ready, t + 1)
                    nc.gpsimd.tensor_tensor(mv[0:n, slot, 1:2], mv[0:n, slot, 1:2], eps[0:n, 0, 0:1], ALU.pow).then_inc(rstd_ready, 1)

            @block.vector
            def _(dve):
                ch = Chain(dve, s_chain)
                dve.sem_inc(yn_ready, 2)
                for i, slot, t, n in tile_pairs(dve):
                    dve.wait_ge(a_full, t + 3)
                    ch.link(nc.vector.bn_stats(stats[0:n], pa[slot][0:n, :]))
                    ch.link(nc.vector.bn_aggr(mv[0:n, slot, :], stats[0:n]))
                    nc.vector.tensor_scalar(mv[0:n, slot, 1:2], mv[0:n, slot, 1:2], LN_EPS, None, ALU.add).then_inc(var_ready, 1)
                    dve.wait_ge(rstd_ready, t + 1)
                    dve.wait_ge(b_full, t + 1)
                    nc.vector.tensor_scalar(yn[0:n, slot, :], pa[slot][0:n, :], mv[0:n, slot, 0:1], mv[0:n, slot, 1:2], ALU.subtract, ALU.mult).then_inc(yn_ready, 1)
                    ch.restart()

            @block.scalar
            def _(act):
                act.sem_inc(b_kept, 2)
                act.sem_inc(b_full, 2)
                for i, slot, t, n in tile_pairs(act):
                    act.wait_ge(b_full, t + 3)
                    act.sem_inc(seen, 1)
                    for b in range(CB):
                        m = nc.scalar.activation(yT[:, b, bass.ds(t * P, n)], pb[slot][:, b * P:b * P + n], ACT.Silu,
                                                 scale=c.cols[:, VEC_LG + b:VEC_LG + b + 1], bias=c.cols[:, VEC_LB + b:VEC_LB + b + 1])
                    m.then_inc(b_kept, 1)


def mix(nc, c, yT, logits):
    with Phase(nc, "x2_") as ph:
        wc = ph.sb("wc", [P, CB, D])
        wa = ph.sb("wa", [P, CB, D])
        wo = ph.sb("wo", [P, KD, D])
        wr = ph.sb("wr", [P, KD, P])
        rb = ph.sb("rb", [P, NL])
        gain, bias = ph.sb("gain", [P, D]), ph.sb("bias", [P, D])
        oT = ph.sb("oT", [P, CB, 512])
        gates = ph.sb("gates", [P, 2 * KD, 512])
        t1, t2 = ph.sb("t1", [P, 512]), ph.sb("t2", [P, 512])
        mT = ph.sb("mT", [P, KD, 512])
        xt = ph.sb("xt", [P, 2, D])
        x1 = ph.sb("x1", [P, 2, D])
        x1T = ph.sb("x1T", [P, KD, P])
        stats, mv, eps = ph.sb("stats", [P, 2, 6]), ph.sb("mv", [P, 2]), ph.sb("eps", [P, 1])
        pA = [ph.ps(f"A{i}", [P, 512]) for i in range(2)]
        pB = [ph.ps(f"B{i}", [P, 512]) for i in range(2)]
        pC = ph.ps("C", [P, 2, 512])
        pX, pR = ph.ps("X", [P, 512]), ph.ps("R", [P, 512])
        w_loaded, o_weights, zeroed, made = (ph.sem(n) for n in ("w_loaded", "o_weights", "zeroed", "made"))
        o_loaded, g_loaded = ph.sem("o_loaded"), ph.sem("g_loaded")
        x_loaded = [ph.sem(f"x_loaded{i}") for i in range(2)]
        x1_stored = [ph.sem(f"x1_stored{i}") for i in range(2)]
        ab_full, m_done, c_full, c_kept, var_ready, rstd_ready, x1_ready, x_full, x_kept, r_full, r_kept, s_chain, seen = (
            ph.sem(n) for n in ("ab_full", "m_done", "c_full", "c_kept", "var_ready", "rstd_ready", "x1_ready", "x_full", "x_kept", "r_full", "r_kept",
                                "chain", "seen"))

        def blocks(e):
            with e.Fori(0, T // 512) as b:
                yield b, 512, [P] * 4
            yield T // 512, S, [S]

        with ph.block() as block:
            @block.sync
            def _(sp):
                sp.wait_ge(zeroed, 1)
                sp.dma_start(wc[:], c.inp["w_conv_out"][0].rearrange("(k p) n -> p k n", p=P)).then_inc(w_loaded, 16)
                sp.dma_start(wa[:], c.inp["w_attn_out"][0].rearrange("(k p) n -> p k n", p=P)).then_inc(w_loaded, 16)
                for b, n, tiles in blocks(sp):
                    sp.wait_ge(ab_full, 8 * b + 1)
                    sp.dma_start(oT[:, :, 0:n], c.oT[:, bass.ds(b * 512, n)].rearrange("(k p) t -> p k t", p=P)).then_inc(o_loaded, 16)
                    sp.wait_ge(m_done, 8 * b + 2)
                    sp.dma_start(gates[:, :, 0:n], c.featT[COL_G:N_IN, bass.ds(b * 512, n)].rearrange("(k p) t -> p k t", p=P)).then_inc(g_loaded, 16)
                    for s, r in enumerate(tiles):
                        sp.wait_ge(c_kept, 4 * b + (s + 1))
                        src = c.xp[bass.ds(b * 512 + s * P, P), :] if r == P else c.xs
                        sp.dma_start(xt[0:r, s % 2, :], src).then_inc(x_loaded[s % 2], 16)

            @block.gpsimd
            def _(pool):
                nc.gpsimd.memset(eps[:], -0.5).then_inc(made, 1)
                pool.wait_ge(made, 1)
                pool.dma_start(wo[:], c.inp["w_out"][0].rearrange("(k p) n -> p k n", p=P)).then_inc(o_weights, 16)
                pool.wait_ge(zeroed, 1)
                pool.dma_start(wr[:, :, 0:NG], c.inp["router_group_w"][0].rearrange("(k p) n -> p k n", p=P)).then_inc(o_weights, 16)
                pool.dma_start(wr[:, :, NG:NL], c.inp["router_expert_w"][0].rearrange("(k p) n -> p k n", p=P)).then_inc(o_weights, 16)
                pool.dma_start(rb[:, 0:NG], c.inp["router_group_b"].to_broadcast([P, NG])).then_inc(o_weights, 16)
                pool.dma_start(rb[:, NG:NL], c.inp["router_expert_b"].to_broadcast([P, NE])).then_inc(o_weights, 16)
                pool.dma_start(gain[:], c.inp["ln1_g"].to_broadcast([P, D])).then_inc(o_weights, 16)
                pool.dma_start(bias[:], c.inp["ln1_b"].to_broadcast([P, D])).then_inc(o_weights, 16)
                for b, n, tiles in blocks(pool):
                    for s, r in enumerate(tiles):
                        t = 4 * b + s
                        pool.wait_ge(var_ready, t + 1)
                        nc.gpsimd.tensor_tensor(mv[0:r, 1:2], mv[0:r, 1:2], eps[0:r], ALU.pow).then_inc(rstd_ready, 1)
                        pool.wait_ge(x1_ready, t + 1)
                        pool.sem_inc(seen, 1)
                        pool.dma_start(c.x1[bass.ds(b * 512 + s * P, r), :], x1[0:r, s % 2, :]).then_inc(x1_stored[s % 2], 16)
                pool.wait_ge(x1_stored[0], 16 * (NT // 2 + 1))
                pool.wait_ge(x1_stored[1], 16 * (NT // 2))

            @block.tensor
            def _(pe):
                pe.sem_inc(ab_full, 1)
                pe.wait_ge(w_loaded, 32)

                def branches(b, n):
                    pe.wait_ge(o_loaded, 16 * b + 16)
                    pe.wait_ge(c_full, 4 * b)
                    for f in range(KD):
                        pe.wait_ge(m_done, 8 * b + (f + 1))
                        for k in range(CB):
                            nc.tensor.matmul(pA[f % 2][:, 0:n], wc[:, k, f * P:(f + 1) * P], yT[:, k, bass.ds(b * 512, n)], start=(k == 0), stop=(k == CB - 1))
                        for k in range(CB):
                            m = nc.tensor.matmul(pB[f % 2][:, 0:n], wa[:, k, f * P:(f + 1) * P], oT[:, k, 0:n], start=(k == 0), stop=(k == CB - 1))
                        m.then_inc(ab_full, 1)

                def out(b, s, r):
                    pe.wait_ge(c_kept, 4 * b + (s + 2))
                    for h in range(2):
                        for k in range(KD):
                            m = nc.tensor.matmul(pC[0:r, h, :], mT[:, k, s * P:s * P + r], wo[:, k, h * 512:(h + 1) * 512], start=(k == 0), stop=(k == KD - 1))
                    m.then_inc(c_full, 1)

                def route(b, s, r):
                    t = 4 * b + s
                    pe.wait_ge(x1_ready, t + 1)
                    for h in range(2):
                        pe.wait_ge(x_kept, 2 * t + (h + 1))
                        for k in range(4):
                            m = nc.tensor.transpose(pX[:, k * P:k * P + r], x1[0:r, s % 2, (4 * h + k) * P:(4 * h + k + 1) * P], c.ident[0:r, 0:r])
                        m.then_inc(x_full, 1)
                    pe.wait_ge(x_kept, 2 * t + 3)
                    pe.wait_ge(r_kept, t + 1)
                    for k in range(KD):
                        m = nc.tensor.matmul(pR[0:r, 0:P], x1T[:, k, 0:r], wr[:, k, :], start=(k == 0), stop=(k == KD - 1))
                    m.then_inc(r_full, 1)

                for b, n, tiles in blocks(pe):
                    branches(b, n)
                    pe.wait_ge(m_done, 8 * b + 10)
                    pe.wait_ge(o_weights, 16 * 7)
                    for s, r in enumerate(tiles):
                        out(b, s, r)
                        if s:
                            route(b, s - 1, P)
                    route(b, len(tiles) - 1, tiles[-1])

            @block.scalar
            def _(act):
                act.sem_inc(x_kept, 1)
                for b, n, tiles in blocks(act):
                    for s, r in enumerate(tiles):
                        t = 4 * b + s
                        for h in range(2):
                            act.wait_ge(x_full, 2 * t + (h + 1))
                            if h == 0:
                                act.wait_ge(r_full, t)
                            nc.scalar.copy(x1T[:, 4 * h:4 * h + 4, 0:r], pX[:].rearrange("p (k t) -> p k t", k=4)[:, :, 0:r]).then_inc(x_kept, 1)

            @block.vector
            def _(dve):
                ch = Chain(dve, s_chain)
                ch.link(nc.vector.memset(wr[:], 0.0))
                ch.link(nc.vector.memset(logits[:], 0.0))
                dve.sem_inc(zeroed, 1)
                dve.sem_inc(m_done, 2)
                dve.sem_inc(c_kept, 2)
                dve.sem_inc(r_kept, 1)
                dve.wait_ge(o_weights, 16 * 7)
                ch.restart()
                for b, n, tiles in blocks(dve):
                    dve.wait_ge(g_loaded, 16 * b + 16)
                    for f in range(KD):
                        dve.wait_ge(ab_full, 8 * b + (f + 2))
                        if f == 0:
                            dve.wait_ge(c_full, 4 * b)
                        ch.mark(nc.vector.tensor_tensor(t1[:, 0:n], pA[f % 2][:, 0:n], gates[:, f, 0:n], ALU.mult))
                        ch.link(nc.vector.tensor_tensor(t2[:, 0:n], pB[f % 2][:, 0:n], gates[:, KD + f, 0:n], ALU.mult))
                        nc.vector.tensor_tensor(mT[:, f, 0:n], t1[:, 0:n], t2[:, 0:n], ALU.add).then_inc(m_done, 1)
                        dve.wait_ge(m_done, 8 * b + (f + 3))

                    def logit(s, r):
                        t = 4 * b + s
                        dve.wait_ge(r_full, t + 1)
                        dve.sem_inc(seen, 1)
                        at = logits[0:r, bass.ds(t, 1), :]
                        nc.vector.tensor_tensor(at, pR[0:r, 0:NL].rearrange("p (a l) -> p a l", a=1), rb[0:r].rearrange("p (a l) -> p a l", a=1), ALU.add).then_inc(r_kept, 1)

                    for s, r in enumerate(tiles):
                        t = 4 * b + s
                        dve.wait_ge(c_full, t + 1)
                        dve.wait_ge(x_loaded[s % 2], 32 * b + 16 * (s // 2 + 1))
                        dve.wait_ge(x1_stored[s % 2], 32 * b + 16 * (s // 2))
                        dve.wait_ge(x_full, 8 * b + 2 * max(s - 1, 0))
                        z, o = xt[0:r, s % 2, :], x1[0:r, s % 2, :]
                        ch.link(nc.vector.scalar_tensor_tensor(o, z, ALPHA, pC[0:r].rearrange("p h n -> p (h n)"), ALU.mult, ALU.add))
                        dve.sem_inc(c_kept, 1)
                        layer_norm(ch, nc, dve, o, r, stats, mv, gain, bias, var_ready, rstd_ready, t + 1)
                        dve.sem_inc(x1_ready, 1)
                        if s:
                            logit(s - 1, P)
                    logit(len(tiles) - 1, tiles[-1])
                    ch.restart()


def layer_norm(ch, nc, dve, o, r, stats, mv, gain, bias, var_ready, rstd_ready, nth):
    for h in range(2):
        ch.mark(nc.vector.bn_stats(stats[0:r, h, :], o[:, h * 512:(h + 1) * 512]))
    ch.sync()
    ch.link(nc.vector.bn_aggr(mv[0:r, :], stats[0:r].rearrange("p h s -> p (h s)")))
    nc.vector.tensor_scalar(mv[0:r, 1:2], mv[0:r, 1:2], LN_EPS, None, ALU.add).then_inc(var_ready, 1)
    dve.wait_ge(rstd_ready, nth)
    ch.link(nc.vector.tensor_scalar(o, o, mv[0:r, 0:1], mv[0:r, 1:2], ALU.subtract, ALU.mult))
    ch.link(nc.vector.tensor_tensor(o, o, gain[0:r, :], ALU.mult))
    ch.link(nc.vector.tensor_tensor(o, o, bias[0:r, :], ALU.add))


def first_of(ch, nc, one_hot, values, top, order, tmp, wide):
    n, m, w = wide
    ch.link(nc.vector.tensor_tensor(one_hot, values, top.to_broadcast([n, m, w]), ALU.is_equal))
    ch.link(nc.vector.tensor_tensor(one_hot, one_hot, order.to_broadcast([n, m, w]), ALU.mult))
    ch.link(nc.vector.tensor_reduce(tmp, one_hot, AX.X, ALU.max))
    ch.link(nc.vector.tensor_tensor(one_hot, one_hot, tmp.to_broadcast([n, m, w]), ALU.is_equal))


def route(nc, c, logits, gate, place, expert_of, weight_slot, is_new):
    with Phase(nc, "r_") as ph:
        order = ph.sb("order", [P, 1, NE])
        t1 = ph.sb("t1", [P, NTL, 1])
        top = ph.sb("top", [P, NTL, 1])
        goh = ph.sb("goh", [P, NTL, NG])
        el = ph.sb("el", [P, NTL, NE])
        oh = [ph.sb(f"oh{i}", [P, NTL, NE]) for i in range(2)]
        both = ph.sb("both", [P, NTL, NE])
        ex = ph.sb("ex", [P, NTL, NG])
        gsum = ph.sb("gsum", [P, NTL, 1])
        ratio = ph.sb("ratio", [P, NTL, 1])
        tops = ph.sb("tops", [P, 2, NTL, 1])
        below, ones = ph.sb("below", [P, P]), ph.sb("ones", [P, P])
        rank = ph.sb("rank", [P, NTL, NE])
        totals = ph.sb("totals", [P, NTL + 1, NE])
        blk_no = ph.sb("blk_no", [P, 1, NBLK])
        thr = ph.sb("thr", [P, NE, NTL])
        cmpa = ph.sb("cmpa", [P, NE, NTL])
        nblk, end, start = (ph.sb(n, [P, NE]) for n in ("nblk", "end", "start"))
        cmpb = ph.sb("cmpb", [1, NBLK, NE])
        exf, newf, slf = (ph.sb(n, [1, NBLK]) for n in ("exf", "newf", "slf"))
        placef = ph.sb("placef", [P, 2, NTL, 1])
        token = ph.sb("token", [P, NTL], I32)
        dummy = ph.sb("dummy", [P, NBLK], I32)
        zero = ph.sb("zero", [1, D])
        idx = ph.sb("idx", [P, 2, 1], I32)
        tok = ph.sb("tok", [P, 1], I32)
        pp = [ph.ps(f"p{i}", [P, 512]) for i in range(4)]
        made, made2, e_ready, e_done, m_ready, m_full, table_ready, place_ready, filled, copied, s_chain, seen = (
            ph.sem(n) for n in ("made", "made2", "e_ready", "e_done", "m_ready", "m_full", "table_ready", "place_ready", "filled", "copied", "chain", "seen"))
        scattered = [ph.sem(f"scattered{i}") for i in range(2)]
        with ph.block() as block:
            @block.gpsimd
            def _(pool):
                nc.gpsimd.iota(order[:], [[0, 1], [-1, NE]], base=NE, channel_multiplier=0, allow_small_or_imprecise_dtypes=True).then_inc(made, 1)
                nc.gpsimd.memset(ones[:], 1.0).then_inc(made, 1)
                nc.gpsimd.iota(thr[:], [[0, NE], [P, NTL]], base=0, channel_multiplier=0, allow_small_or_imprecise_dtypes=True).then_inc(made, 1)
                nc.gpsimd.iota(blk_no[:], [[0, 1], [1, NBLK]], base=0, channel_multiplier=0, allow_small_or_imprecise_dtypes=True).then_inc(made, 1)
                nc.gpsimd.iota(token[:], [[P, NTL]], base=0, channel_multiplier=1).then_inc(made, 1)
                nc.gpsimd.iota(dummy[:], [[0, NBLK]], base=TT, channel_multiplier=0).then_inc(made, 1)
                nc.gpsimd.memset(zero[:], 0.0).then_inc(made, 1)
                pool.wait_ge(made, 7)
                nc.gpsimd.affine_select(out=below[:], in_=ones[:], compare_op=ALU.is_gt, fill=0.0, base=0, pattern=[[1, P]], channel_multiplier=-1).then_inc(made, 1)
                pool.dma_start(c.slot_tok.rearrange("(p j) a -> p (j a)", p=P), dummy[:]).then_inc(filled, 16)
                pool.dma_start(c.x1[TT:TT + 1, :], zero[:]).then_inc(filled, 16)
                pool.wait_ge(filled, 32)
                pool.wait_ge(place_ready, 1)
                with pool.Fori(0, NT) as t:
                    nc.gpsimd.tensor_copy(tok[:], token[:, bass.ds(t, 1)]).then_inc(copied, 1)
                    for a in range(2):
                        nc.gpsimd.tensor_copy(idx[:, a, :], place[:, a, bass.ds(t, 1)]).then_inc(copied, 1)
                    pool.wait_ge(copied, 3 * t + 3)
                    pool.sem_inc(seen, 1)
                    for a in range(2):
                        pool.indirect_dma_start(c.slot_tok, bass.IndirectOffsetOnAxis(ap=idx[:, a, :], axis=0), tok[:], None).then_inc(scattered[a], 16)
                    pool.wait_ge(scattered[0], 16 * t + 16)
                    pool.wait_ge(scattered[1], 16 * t + 16)
                for a in range(2):
                    pool.indirect_dma_start(c.slot_tok, bass.IndirectOffsetOnAxis(ap=place[0:S, a, NT:NT + 1], axis=0), token[0:S, NT:NT + 1], None).then_inc(scattered[a], 16)
                for a in range(2):
                    pool.wait_ge(scattered[a], 16 * (NT + 1))

            @block.scalar
            def _(act):
                act.wait_ge(e_ready, 1)
                nc.scalar.activation(ex[:], ex[:], ACT.Exp).then_inc(e_done, 1)
                nc.scalar.activation(ratio[:], ratio[:], ACT.Exp).then_inc(e_done, 1)

            @block.tensor
            def _(pe):
                pe.wait_ge(m_ready, 1)
                pe.wait_ge(made, 8)
                flat = both[:].rearrange("p t e -> p (t e)")
                for k, w in enumerate((below, ones)):
                    nc.tensor.matmul(pp[2 * k][:], w[:], flat[:, 0:512], start=True, stop=True)
                    nc.tensor.matmul(pp[2 * k + 1][:, 0:NE], w[:], flat[:, 512:512 + NE], start=True, stop=True).then_inc(m_full, 1)

            @block.vector
            def _(dve):
                ch = Chain(dve, s_chain)
                lg, le = logits[:, :, 0:NG], logits[:, :, NG:NL]
                wide = (P, NTL, NE)
                dve.wait_ge(made, 6)
                ch.link(nc.vector.tensor_reduce(top[:], lg, AX.X, ALU.max))
                ch.link(nc.vector.tensor_tensor(ex[:], lg, top[:].to_broadcast([P, NTL, NG]), ALU.subtract))
                first_of(ch, nc, goh[:], lg, top[:], order[:, :, 0:NG], t1[:], (P, NTL, NG))
                ch.link(nc.vector.tensor_scalar(goh[:], goh[:], -1.0, BIG, ALU.add, ALU.mult))
                for g in range(NG):
                    ch.link(nc.vector.tensor_tensor(el[:, :, g * EPG:(g + 1) * EPG], le[:, :, g * EPG:(g + 1) * EPG], goh[:, :, g:g + 1].to_broadcast([P, NTL, EPG]), ALU.add))
                for a in range(2):
                    ch.link(nc.vector.tensor_reduce(tops[:, a], el[:], AX.X, ALU.max))
                    first_of(ch, nc, oh[a][:], el[:], tops[:, a], order[:], t1[:], wide)
                    if a == 0:
                        ch.link(nc.vector.scalar_tensor_tensor(el[:], oh[0][:], -BIG, el[:], ALU.mult, ALU.add))
                ch.link(nc.vector.tensor_tensor(ratio[:], tops[:, 1], tops[:, 0], ALU.subtract))
                dve.sem_inc(e_ready, 1)
                ch.link(nc.vector.tensor_tensor(both[:], oh[0][:], oh[1][:], ALU.add))
                ch.mark(nc.vector.memset(both[S:2 * S, NT, :], 0.0))
                ch.link(nc.vector.memset(both[2 * S:P, NT, :], 0.0))
                dve.sem_inc(m_ready, 1)
                dve.wait_ge(e_done, 2)
                ch.link(nc.vector.tensor_reduce(gsum[:], ex[:], AX.X, ALU.add))
                ch.link(nc.vector.tensor_scalar(t1[:], ratio[:], 1.0, None, ALU.add))
                ch.link(nc.vector.tensor_tensor(gsum[:], gsum[:], t1[:], ALU.mult))
                ch.link(nc.vector.reciprocal(gate[:, 0], gsum[:, :, 0]))
                ch.link(nc.vector.tensor_tensor(gate[:, 1], gate[:, 0], ratio[:, :, 0], ALU.mult))
                dve.wait_ge(m_full, 2)
                rf, tf = rank[:].rearrange("p t e -> p (t e)"), totals[:, 1:NTL + 1, :].rearrange("p t e -> p (t e)")
                for dst, k in ((rf, 0), (tf, 1)):
                    ch.mark(nc.vector.tensor_copy(dst[:, 0:512], pp[2 * k][:]))
                    ch.mark(nc.vector.tensor_copy(dst[:, 512:512 + NE], pp[2 * k + 1][:, 0:NE]))
                ch.link(nc.vector.memset(totals[:, 0, :], 0.0))
                for t in range(1, NTL + 1):
                    ch.link(nc.vector.tensor_tensor(totals[:, t, :], totals[:, t, :], totals[:, t - 1, :], ALU.add))
                ch.link(nc.vector.tensor_tensor(rank[:], rank[:], totals[:, 0:NTL, :], ALU.add))
                cnt = totals[:, NTL, :].rearrange("p (e a) -> p e a", a=1)
                ch.link(nc.vector.tensor_tensor(cmpa[:], cnt.to_broadcast([P, NE, NTL]), thr[:], ALU.is_gt))
                ch.link(nc.vector.tensor_reduce(nblk[:], cmpa[:], AX.X, ALU.add))
                ch.link(nc.vector.tensor_tensor_scan(end[:], nblk[:], nblk[:], 0.0, ALU.add, ALU.max))
                ch.link(nc.vector.tensor_tensor(start[:], end[:], nblk[:], ALU.subtract))
                ch.link(nc.vector.tensor_scalar(start[:], start[:], float(P), None, ALU.mult))
                ch.link(nc.vector.tensor_tensor(rank[:], rank[:], start[:].rearrange("p (a e) -> p a e", a=1).to_broadcast([P, NTL, NE]), ALU.add))
                for a in range(2):
                    ch.link(nc.vector.tensor_tensor(el[:], oh[a][:], rank[:], ALU.mult))
                    ch.link(nc.vector.tensor_reduce(placef[:, a], el[:], AX.X, ALU.add))
                    ch.link(nc.vector.tensor_copy(place[:, a, :], placef[:, a, :, 0]))
                dve.sem_inc(place_ready, 1)
                b3 = blk_no[0:1].rearrange("p a b -> p b a").to_broadcast([1, NBLK, NE])
                ch.link(nc.vector.tensor_tensor(cmpb[:], end[0:1].rearrange("p (a e) -> p a e", a=1).to_broadcast([1, NBLK, NE]), b3, ALU.is_le))
                ch.link(nc.vector.tensor_reduce(exf[:], cmpb[:], AX.X, ALU.add))
                ch.link(nc.vector.tensor_scalar(exf[:], exf[:], float(NE - 1), None, ALU.min))
                ch.mark(nc.vector.memset(newf[:, 0:1], 1.0))
                ch.link(nc.vector.tensor_tensor(newf[:, 1:NBLK], exf[:, 1:NBLK], exf[:, 0:NBLK - 1], ALU.not_equal))
                ch.link(nc.vector.tensor_tensor_scan(slf[:], newf[:], newf[:], 0.0, ALU.add, ALU.max))
                ch.link(nc.vector.tensor_copy(weight_slot[:], slf[:]))
                ch.link(nc.vector.tensor_scalar(weight_slot[:], weight_slot[:], WS - 1, None, ALU.bitwise_and))
                ch.mark(nc.vector.tensor_copy(expert_of[:], exf[:]))
                ch.link(nc.vector.tensor_copy(is_new[:], newf[:]))


WS = 4


def experts(nc, c, expert_of, weight_slot, is_new):
    with Phase(nc, "e_") as ph:
        wgu = ph.sb("wgu", [P, WS, KD, 2 * F])
        wd = ph.sb("wd", [P, WS, 2, D])
        xg = ph.sb("xg", [P, 2, D])
        xT = ph.sb("xT", [P, 2, KD, P])
        sg = ph.sb("sg", [P, F])
        hh = ph.sb("hh", [P, F])
        hT = ph.sb("hT", [P, 2, P])
        y = ph.sb("y", [P, 2, D])
        ids = ph.sb("ids", [P, NBLK], I32)
        idx = ph.sb("idx", [P, 2, 1], I32)
        pX = [ph.ps(f"X{i}", [P, 512]) for i in range(2)]
        pG = [ph.ps(f"G{i}", [P, 512]) for i in range(2)]
        pH = ph.ps("H", [P, 512])
        pY = [ph.ps(f"Y{i}", [P, 512]) for i in range(2)]
        w_loaded = [ph.sem(f"w_loaded{i}") for i in range(WS)]
        x_loaded = [ph.sem(f"x_loaded{i}") for i in range(2)]
        y_stored = [ph.sem(f"y_stored{i}") for i in range(2)]
        ids_loaded, copied, x_turned, x_kept, gu_full, sg_done, h_done, h_turned, h_kept, y_full, y_kept, s_done, seen, wdone = (
            ph.sem(n) for n in ("ids_loaded", "copied", "x_turned", "x_kept", "gu_full", "sg_done", "h_done", "h_turned", "h_kept", "y_full", "y_kept",
                                "block_done", "seen", "w_issued"))

        def steps(e):
            with e.Fori(0, NBLK // 2) as i:
                yield i, 0, 2 * i
                yield i, 1, 2 * i + 1
            yield NBLK // 2, 0, NBLK - 1

        with ph.block() as block:
            @block.sync
            def _(sp):
                wg_h, wu_h = (c.inp[n][0].rearrange("e (p k) f -> p e k f", k=KD) for n in ("w_gate", "w_up"))
                wd_h = c.inp["w_down"][0].rearrange("e (p k) d -> p e k d", k=2)
                def load(turn, a):
                    j = turn * WS + a
                    sp.wait_ge(s_done, j + 1)
                    e = sp.value_load(expert_of[0:1, bass.ds(j, 1)], min_val=0, max_val=NE - 1)
                    s = sp.value_load(weight_slot[0:1, bass.ds(j, 1)], min_val=0, max_val=WS - 1)
                    n = sp.value_load(is_new[0:1, bass.ds(j, 1)], min_val=0, max_val=1)
                    for dst, src in ((wgu[:, bass.ds(s, 1), :, 0:F], wg_h), (wgu[:, bass.ds(s, 1), :, F:2 * F], wu_h), (wd[:, bass.ds(s, 1)], wd_h)):
                        sp.dma_start(dst, src[:, bass.ds(e, 1)], cond=n).then_inc(w_loaded[a], 16)

                def store(i, slot, j):
                    sp.wait_ge(y_kept, 2 * j + 4)
                    sp.dma_start(c.yb[bass.ds(j * P, P), :], y[:, slot, :]).then_inc(y_stored[slot], 16)

                for a in range(WS):
                    load(0, a)
                turns = (NBLK - WS) // WS
                with sp.Fori(0, turns) as i:
                    for a in range(WS):
                        store(2 * i + a // 2, a % 2, i * WS + a)
                        load(i + 1, a)
                for j in range(turns * WS, NBLK):
                    store(j // 2, j % 2, j)
                    if j + WS < NBLK:
                        load((j + WS) // WS, (j + WS) % WS)
                sp.wait_ge(y_stored[0], 16 * (NBLK // 2 + 1))
                sp.wait_ge(y_stored[1], 16 * (NBLK // 2))

            @block.gpsimd
            def _(pool):
                pool.dma_start(ids[:], c.slot_tok.rearrange("(j p) a -> p (j a)", p=P), allow_slow_non_contiguous=True).then_inc(ids_loaded, 16)
                pool.wait_ge(ids_loaded, 16)
                for i, slot, j in steps(pool):
                    pool.wait_ge(x_loaded[slot], 16 * i)
                    pool.sem_inc(seen, 1)
                    nc.gpsimd.tensor_copy(idx[:, slot, :], ids[:, bass.ds(j, 1)]).then_inc(copied, 1)
                    pool.wait_ge(copied, j + 1)
                    pool.wait_ge(x_turned, 2 * j + 2)
                    pool.sem_inc(seen, 1)
                    pool.indirect_dma_start(xg[:, slot, :], None, c.x1, bass.IndirectOffsetOnAxis(ap=idx[:, slot, :], axis=0)).then_inc(x_loaded[slot], 16)

            @block.tensor
            def _(pe):
                pe.sem_inc(x_turned, 4)
                pe.sem_inc(s_done, WS)
                pe.sem_inc(gu_full, 2)

                def turn(i, slot, j):
                    pe.wait_ge(x_loaded[slot], 16 * i + 16)
                    for h in range(2):
                        pe.wait_ge(x_kept, 2 * j + (h + 1))
                        for k in range(4):
                            m = nc.tensor.transpose(pX[h][:, k * P:(k + 1) * P], xg[:, slot, 4 * h + k:D:KD], c.ident[:])
                        m.then_inc(x_turned, 1)

                def up(slot, j, s, turn, a):
                    pe.wait_ge(x_kept, 2 * j + 4)
                    pe.wait_ge(w_loaded[a], 48 * turn + 48)
                    pe.wait_ge(h_done, j + 1)
                    pe.sem_inc(seen, 1)
                    for k in range(KD):
                        m = nc.tensor.matmul(pG[slot][:], xT[:, slot, k, :], wgu[:, bass.ds(s, 1), k, :].rearrange("p a f -> p (a f)"), start=(k == 0), stop=(k == KD - 1))
                    m.then_inc(gu_full, 1)

                def down(slot, j, s):
                    pe.wait_ge(h_done, j + 3)
                    for k in range(2):
                        m = nc.tensor.transpose(pH[:, k * P:(k + 1) * P], hh[:, k:F:2], c.ident[:])
                    m.then_inc(h_turned, 1)
                    pe.wait_ge(h_kept, j + 1)
                    for h in range(2):
                        pe.wait_ge(y_kept, 2 * j + (h + 1))
                        pe.sem_inc(seen, 1)
                        for k in range(2):
                            m = nc.tensor.matmul(pY[h][:], hT[:, k, :], wd[:, bass.ds(s, 1), k, h * 512:(h + 1) * 512].rearrange("p a f -> p (a f)"), start=(k == 0), stop=(k == 1))
                        m.then_inc(y_full, 1)
                    pe.wait_ge(y_full, 2 * j + 2)
                    pe.sem_inc(s_done, 1)

                def group(i, n):
                    s = [pe.value_load(weight_slot[0:1, bass.ds(i * WS + a, 1)], min_val=0, max_val=WS - 1) for a in range(n)]
                    turn(2 * i, 0, i * WS)
                    for a in range(n):
                        slot, j = a % 2, i * WS + a
                        if a + 1 < n:
                            turn(2 * i + (a + 1) // 2, (a + 1) % 2, j + 1)
                        up(slot, j, s[a], i, a)
                        down(slot, j, s[a])

                with pe.Fori(0, NBLK // WS) as i:
                    group(i, WS)
                assert NBLK % WS == 1
                group(NBLK // WS, 1)

            @block.scalar
            def _(act):
                act.sem_inc(x_kept, 2)
                act.sem_inc(y_kept, 2)

                def keep_x(slot, j):
                    act.wait_ge(gu_full, j + 1)
                    for h in range(2):
                        act.wait_ge(x_turned, 2 * j + (h + 5))
                        nc.scalar.copy(xT[:, slot, 4 * h:4 * h + 4, :], pX[h][:].rearrange("p (k t) -> p k t", k=4)).then_inc(x_kept, 1)

                def rest(slot, j):
                    act.wait_ge(gu_full, j + 3)
                    act.wait_ge(h_done, j + 2)
                    nc.scalar.activation(sg[:], pG[slot][:, 0:F], ACT.Silu).then_inc(sg_done, 1)
                    act.wait_ge(y_full, 2 * j + 2)
                    nc.scalar.copy(y[:, slot, 512:D], pY[1][:]).then_inc(y_kept, 1)

                def group(i, n):
                    keep_x(0, i * WS)
                    for a in range(n):
                        if a + 1 < n:
                            keep_x((a + 1) % 2, i * WS + a + 1)
                        act.wait_ge(y_stored[a % 2], 32 * i + 16 * (a // 2))
                        rest(a % 2, i * WS + a)

                with act.Fori(0, NBLK // WS) as i:
                    group(i, WS)
                group(NBLK // WS, 1)

            @block.vector
            def _(dve):
                dve.sem_inc(h_done, 2)
                for i, slot, j in steps(dve):
                    dve.wait_ge(sg_done, j + 1)
                    dve.wait_ge(h_turned, j)
                    nc.vector.tensor_tensor(hh[:], sg[:], pG[slot][:, F:2 * F], ALU.mult).then_inc(h_done, 1)
                    dve.wait_ge(h_turned, j + 1)
                    dve.wait_ge(y_full, 2 * j)
                    nc.vector.tensor_copy(hT[:], pH[:, 0:2 * P].rearrange("p (k t) -> p k t", k=2)).then_inc(h_kept, 1)
                    dve.wait_ge(y_full, 2 * j + 1)
                    dve.wait_ge(y_stored[slot], 16 * i)
                    nc.vector.tensor_copy(y[:, slot, 0:512], pY[0][:]).then_inc(y_kept, 1)


def combine(nc, c, gate, place):
    with Phase(nc, "o_") as ph:
        gain, bias = ph.sb("gain", [P, D]), ph.sb("bias", [P, D])
        x1 = ph.sb("x1", [P, 2, D])
        ye = ph.sb("ye", [P, 2, 2, D])
        z = ph.sb("z", [P, 2, D])
        idx = ph.sb("idx", [P, 2, 2], I32)
        gnow = ph.sb("gnow", [P, 2, 1])
        stats, mv, eps = ph.sb("stats", [P, 2, 6]), ph.sb("mv", [P, 2]), ph.sb("eps", [P, 1])
        g_loaded, made, copied, var_ready, rstd_ready, z_first, z_ready, s_chain, seen = (
            ph.sem(n) for n in ("g_loaded", "made", "copied", "var_ready", "rstd_ready", "z_first", "z_ready", "chain", "seen"))
        x_loaded = [ph.sem(f"x_loaded{i}") for i in range(2)]
        y_loaded = [ph.sem(f"y_loaded{i}") for i in range(2)]
        z_stored = [ph.sem(f"z_stored{i}") for i in range(2)]
        with ph.block() as block:
            @block.sync
            def _(sp):
                sp.dma_start(gain[:], c.inp["ln2_g"].to_broadcast([P, D])).then_inc(g_loaded, 16)
                sp.dma_start(bias[:], c.inp["ln2_b"].to_broadcast([P, D])).then_inc(g_loaded, 16)
                for i, slot, t, n in tile_pairs(sp):
                    sp.wait_ge(z_first, t + 1)
                    sp.dma_start(x1[0:n, slot, :], c.x1[bass.ds(t * P, n), :]).then_inc(x_loaded[slot], 16)

            @block.scalar
            def _(act):
                for i, slot, t, n in tile_pairs(act):
                    act.wait_ge(z_ready, t + 1)
                    dst = c.out["y_prompt"][0, bass.ds(t * P, P), :] if n == P else c.out["y_sample"].rearrange("b s d -> (b s) d")
                    act.dma_start(dst, z[0:n, slot, :]).then_inc(z_stored[slot], 16)
                act.wait_ge(z_stored[0], 16 * (NT // 2 + 1))
                act.wait_ge(z_stored[1], 16 * (NT // 2))

            @block.gpsimd
            def _(pool):
                nc.gpsimd.memset(eps[:], -0.5).then_inc(made, 1)
                pool.wait_ge(made, 1)

                def gather(i, slot, t, n):
                    pool.wait_ge(y_loaded[slot], 32 * i)
                    pool.sem_inc(seen, 1)
                    nc.gpsimd.tensor_copy(idx[:, slot, :].rearrange("p (a b) -> p a b", b=1), place[:, :, bass.ds(t, 1)]).then_inc(copied, 1)
                    pool.wait_ge(copied, t + 1)
                    pool.wait_ge(z_first, t + 1)
                    pool.sem_inc(seen, 1)
                    for a in range(2):
                        pool.indirect_dma_start(ye[0:n, slot, a, :], None, c.yb, bass.IndirectOffsetOnAxis(ap=idx[0:n, slot, a:a + 1], axis=0)).then_inc(y_loaded[slot], 16)

                def power(t, n):
                    pool.wait_ge(var_ready, t + 1)
                    nc.gpsimd.tensor_tensor(mv[0:n, 1:2], mv[0:n, 1:2], eps[0:n], ALU.pow).then_inc(rstd_ready, 1)

                gather(0, 0, 0, P)
                gather(0, 1, 1, P)
                with pool.Fori(0, NT // 2 - 1) as i:
                    power(2 * i, P)
                    gather(i + 1, 0, 2 * i + 2, P)
                    power(2 * i + 1, P)
                    gather(i + 1, 1, 2 * i + 3, P)
                power(NT - 2, P)
                gather(NT // 2, 0, NT, S)
                power(NT - 1, P)
                power(NT, S)

            @block.vector
            def _(dve):
                ch = Chain(dve, s_chain)
                dve.sem_inc(z_first, 2)
                dve.wait_ge(g_loaded, 32)
                for i, slot, t, n in tile_pairs(dve):
                    ch.link(nc.vector.tensor_copy(gnow[:], gate[:, :, bass.ds(t, 1)]))
                    dve.wait_ge(x_loaded[slot], 16 * i + 16)
                    dve.wait_ge(y_loaded[slot], 32 * i + 32)
                    dve.wait_ge(z_stored[slot], 16 * i)
                    o = z[0:n, slot, :]
                    ch.link(nc.vector.tensor_scalar(o, x1[0:n, slot, :], ALPHA, None, ALU.mult))
                    for a in range(2):
                        ch.link(nc.vector.scalar_tensor_tensor(o, ye[0:n, slot, a, :], gnow[0:n, a], o, ALU.mult, ALU.add))
                    dve.sem_inc(z_first, 1)
                    layer_norm(ch, nc, dve, o, n, stats, mv, gain, bias, var_ready, rstd_ready, t + 1)
                    dve.sem_inc(z_ready, 1)
                    ch.restart()


INPUTS = ["x_prompt", "x_sample", "cache_k", "cache_v", "cache_kidx", "state_conv", "page_table", "w_in", "b_in",
          "conv_w", "conv_b", "conv_ln_g", "conv_ln_b", "w_conv_out", "w_attn_out", "w_out", "ln1_g", "ln1_b",
          "router_group_w", "router_group_b", "router_expert_w", "router_expert_b", "w_gate", "w_up", "w_down",
          "ln2_g", "ln2_b"]
OUTPUTS = [("y_prompt", (1, T, D)), ("y_sample", (DB, DS, D)), ("k_prompt", (1, 1, T, NKV, HD)), ("v_prompt", (1, 1, T, NKV, HD)),
           ("ki_prompt", (1, 1, T, HD)), ("conv_prompt", (1, 1, HIST, CC)), ("k_sample", (1, DB, DS, NKV, HD)),
           ("v_sample", (1, DB, DS, NKV, HD)), ("ki_sample", (1, DB, DS, HD)), ("conv_sample", (1, DB, HIST, CC))]


def build(nc, inp, out, upto=99, skip=()):
    c = Ctx()
    c.inp, c.out = inp, out
    c.xp = inp["x_prompt"][0]
    c.xs = inp["x_sample"].rearrange("b s d -> (b s) d")
    c.featT = nc.dram_tensor("featT", (N_IN, TT), F32).ap()
    c.oT = nc.dram_tensor("oT", (CC, TT), F32).ap()
    c.x1 = nc.dram_tensor("x1", (TT + 1, D), F32).ap()
    c.slot_tok = nc.dram_tensor("slot_tok", (NBLK * P, 1), I32).ap()
    c.yb = nc.dram_tensor("yb", (NBLK * P, D), F32).ap()
    c.convT = nc.dram_tensor("convT", (CC, TT), F32).ap()
    with Phase(nc, "g_") as g:
        c.ident = g.sb("ident", [P, P])
        c.cols = g.sb("cols", [P, VEC_N])
        constants(nc, c)
        with Phase(nc, "x_") as ph:
            xT = ph.sb("xT", [P, KD, TT])
            taps = ph.sb("taps", [P, CB, TAPS])
            turn_input(nc, c, xT, c.cols, taps)
            if upto >= 2:
                project(nc, c, xT, c.cols, taps)
        with Phase(nc, "a_") as ph:
            kT = ph.sb("kT", [P, 2, T])
            kiT = ph.sb("kiT", [P, T])
            v_tok = ph.sb("v_tok", [P, NT, 2 * P])
            wi_tok = ph.sb("wi_tok", [P, NT + 1, NIH])
            if upto >= 3:
                keep_keys(nc, c, kT, kiT, v_tok, wi_tok)
            if upto >= 4 and 4 not in skip:
                attend_prompt(nc, c, kT, kiT, v_tok, wi_tok)
        if upto >= 5:
            attend_samples(nc, c)
        with Phase(nc, "b_") as ph:
            logits = ph.sb("logits", [P, NTL, NL])
            gate = ph.sb("gate", [P, 2, NTL])
            place = ph.sb("place", [P, 2, NTL], I32)
            expert_of, weight_slot, is_new = (ph.sb(n, [1, NBLK], I32) for n in ("expert_of", "weight_slot", "is_new"))
            with Phase(nc, "y_") as ph2:
                yT = ph2.sb("yT", [P, CB, TT])
                if upto >= 6:
                    norm_conv(nc, c, yT)
                if upto >= 7:
                    mix(nc, c, yT, logits)
            if upto >= 8:
                route(nc, c, logits, gate, place, expert_of, weight_slot, is_new)
            if upto >= 9:
                experts(nc, c, expert_of, weight_slot, is_new)
            if upto >= 10:
                combine(nc, c, gate, place)


def kernel(**inputs):
    import numpy as _np
    import concourse.bacc as _bacc
    from concourse import mybir as _mybir
    from concourse.bass_utils import run_bass_kernel_spmd as _run

    nc = _bacc.Bacc("TRN2", target_bir_lowering=False, num_devices=1)
    arrays, inp = {}, {}
    for name in INPUTS:
        a = _np.ascontiguousarray(inputs[name])
        arrays[f"in_{name}_dram"] = a
        inp[name] = nc.dram_tensor(f"in_{name}_dram", a.shape, _mybir.dt.from_np(a.dtype), kind="ExternalInput").ap()
    out = {name: nc.dram_tensor(f"out_{name}_dram", shape, _mybir.dt.float32, kind="ExternalOutput").ap() for name, shape in OUTPUTS}
    build(nc, inp, out)
    r = _run(nc, [arrays], core_ids=[0])
    return tuple(r.results[0][f"out_{name}_dram"] for name, _ in OUTPUTS)
```

```python
from contextlib import ExitStack

import concourse.bass as bass
from concourse import mybir

F32 = mybir.dt.float32
I32 = mybir.dt.int32
ALU = mybir.AluOpType
ACT = mybir.ActivationFunctionType
AX = mybir.AxisListType

P = 128
D = 1024
KD = D // P
T = 2048
DB, DS = 8, 4
S = DB * DS
TT = T + S
NT = T // P
CC = 512
CB = CC // P
TAPS = 31
HIST = TAPS - 1
NH, NKV, HD = 8, 4, 64
NIH = 8
TOPK = 256
N_IN = 4680
COL_Q, COL_K, COL_V, COL_QI, COL_KI, COL_WI, COL_G = 1024, 1536, 1792, 2048, 2560, 2624, 2632
LN_EPS = 1e-5
ALPHA = 2.0 ** 0.25

VEC_BIN, VEC_CB, VEC_LG, VEC_LB, VEC_N = 0, 37, 41, 45, 49
KI_BLK = 20
KI_ROWS = COL_G - KI_BLK * P



class Chain:

    def __init__(self, eng, sem):
        self.eng, self.sem, self.count = eng, sem, 0

    def link(self, ins):
        self.count += 1
        ins.then_inc(self.sem, 1)
        self.eng.wait_ge(self.sem, self.count)

    def mark(self, ins):
        self.count += 1
        ins.then_inc(self.sem, 1)

    def sync(self):
        self.eng.wait_ge(self.sem, self.count)

    def restart(self):
        if self.count:
            self.eng.wait_ge(self.sem, self.count)
            self.eng.sem_clear(self.sem)
            self.count = 0


class Phase:

    def __init__(self, nc, tag):
        self.nc, self.tag, self.ctx, self.sems = nc, tag, ExitStack(), []

    def __enter__(self):
        self.ctx.__enter__()
        return self

    def __exit__(self, *e):
        if self.sems:
            self.nc.clear_and_free_semaphores(self.sems)
            self.nc.all_engine_barrier()
        return self.ctx.__exit__(*e)

    def sb(self, name, shape, dt=F32):
        return self.ctx.enter_context(self.nc.sbuf_tensor(self.tag + name, shape, dt))

    def ps(self, name, shape, dt=F32):
        return self.ctx.enter_context(self.nc.psum_tensor(self.tag + "ps_" + name, shape, dt))

    def sem(self, name):
        self.sems.append(self.nc.alloc_semaphore(self.tag + name))
        return self.sems[-1]

    def block(self):
        return self.nc.Block()


def constants(nc, c):
    with Phase(nc, "c_") as ph:
        made = ph.sem("made")
        with ph.block() as block:
            @block.gpsimd
            def _(pool):
                nc.gpsimd.memset(c.ident[:], 0.0).then_inc(made, 1)
                pool.wait_ge(made, 1)
                nc.gpsimd.affine_select(out=c.ident[:], in_=c.ident[:], compare_op=ALU.not_equal, fill=1.0,
                                        base=0, pattern=[[-1, P]], channel_multiplier=1).then_inc(made, 1)
                pool.wait_ge(made, 2)


HALVES = [(0, T // 2, 2), (T // 2, T // 2 + S, 3)]
HALF = max(n for _, n, _ in HALVES)
F32R = mybir.dt.float32r


def turn_input(nc, c, half, x_hi, x_lo, cols, taps):
    first, tokens, _ = HALVES[half]
    full = tokens // P
    with Phase(nc, f"t{half}_") as ph:
        xt = ph.sb("xt", [P, 2, D])
        vec = ph.sb("vec", [VEC_N, P])
        tap_rows = ph.sb("tap_rows", [TAPS, CC])
        acc = [ph.ps(f"acc{i}", [P, 4, P]) for i in range(4)]
        pv = ph.ps("pv", [P, 512])
        x_loaded = [ph.sem(f"x_loaded{i}") for i in range(2)]
        vec_zero, vec_loaded, vec_turned, vec_kept = (ph.sem(n) for n in ("vec_zero", "vec_loaded", "vec_turned", "vec_kept"))
        turned, hi_done, kept, seen_act, seen_dve = (ph.sem(n) for n in ("turned", "hi_done", "kept", "seen_act", "seen_dve"))

        def pairs(e):
            with e.Fori(0, full // 2) as i:
                yield i, 0, P
                yield i, 1, P
            if tokens % P:
                yield full // 2, 0, S

        with ph.block() as block:
            @block.sync
            def _(sp):
                if half == 0:
                    sp.wait_ge(vec_zero, 1)
                    for row, name in ((VEC_CB, "conv_b"), (VEC_LG, "conv_ln_g"), (VEC_LB, "conv_ln_b")):
                        sp.dma_start(vec[row:row + CB, :], c.inp[name][0].rearrange("(b f) -> b f", f=P)).then_inc(vec_loaded, 16)
                    b_in = c.inp["b_in"]
                    sp.dma_start(vec[0:KI_BLK, :], b_in[0, 0:KI_BLK * P].rearrange("(b f) -> b f", f=P)).then_inc(vec_loaded, 16)
                    sp.dma_start(vec[KI_BLK:KI_BLK + 1, 0:KI_ROWS], b_in[0:1, KI_BLK * P:COL_G]).then_inc(vec_loaded, 16)
                    sp.dma_start(vec[KI_BLK + 1:VEC_CB, :], b_in[0, COL_G:N_IN].rearrange("(b f) -> b f", f=P)).then_inc(vec_loaded, 16)
                    sp.dma_start(tap_rows[:], c.inp["conv_w"][0]).then_inc(vec_loaded, 16)
                for i, slot, n in pairs(sp):
                    sp.wait_ge(kept, 4 * i + 2 * slot + 2)
                    src = c.xp[bass.ds((2 * i + slot) * P + first, P), :] if n == P else c.xs
                    sp.dma_start(xt[0:n, slot, :], src).then_inc(x_loaded[slot], 16)

            @block.tensor
            def _(pe):
                for i, slot, n in pairs(pe):
                    pe.wait_ge(x_loaded[slot], 16 * i + 16)
                    pe.wait_ge(kept, 4 * i + 2 * slot + 2)
                    for h in range(2):
                        for k in range(4):
                            f = (4 * h + k) * P
                            t = nc.tensor.transpose(acc[2 * slot + h][:, k, 0:n], xt[0:n, slot, f:f + P], c.ident[0:n, 0:n])
                        t.then_inc(turned, 1)
                if half == 0:
                    pe.wait_ge(vec_loaded, 112)
                    nc.tensor.transpose(pv[:, 0:VEC_N], vec[:], c.ident[0:VEC_N, 0:VEC_N])
                    for b in range(CB):
                        t = nc.tensor.transpose(pv[:, 64 + 32 * b:64 + 32 * b + TAPS], tap_rows[:, b * P:(b + 1) * P], c.ident[0:TAPS, 0:TAPS])
                    t.then_inc(vec_turned, 1)

            @block.scalar
            def _(act):
                for i, slot, n in pairs(act):
                    for h in range(2):
                        act.wait_ge(turned, 4 * i + 2 * slot + h + 1)
                        act.sem_inc(seen_act, 1)
                        at = bass.ds((2 * i + slot) * P, n)
                        nc.scalar.copy(x_hi[:, 4 * h:4 * h + 4, at], acc[2 * slot + h][:, :, 0:n]).then_inc(hi_done, 1)

            @block.vector
            def _(dve):
                if half == 0:
                    nc.vector.memset(vec[:], 0.0).then_inc(vec_zero, 1)
                dve.sem_inc(kept, 4)
                for i, slot, n in pairs(dve):
                    for h in range(2):
                        dve.wait_ge(hi_done, 4 * i + 2 * slot + h + 1)
                        dve.sem_inc(seen_dve, 1)
                        at = bass.ds((2 * i + slot) * P, n)
                        nc.vector.tensor_tensor(x_lo[:, 4 * h:4 * h + 4, at], acc[2 * slot + h][:, :, 0:n], x_hi[:, 4 * h:4 * h + 4, at].bitcast(F32),
                                                ALU.subtract).then_inc(kept, 1)
                if half == 0:
                    dve.wait_ge(vec_turned, 1)
                    nc.vector.tensor_copy(cols[:], pv[:, 0:VEC_N]).then_inc(vec_kept, 1)
                    nc.vector.tensor_copy(taps[:], pv[:, 64:64 + 32 * CB].rearrange("p (b t) -> p b t", b=CB)[:, :, 0:TAPS]).then_inc(vec_kept, 1)
                    dve.wait_ge(vec_kept, 2)


def project(nc, c, half, x_hi, x_lo, cols, taps, uh):
    first, tokens, NTB = HALVES[half]
    width = tokens // NTB
    prompt = min(tokens, T - first)
    samples = tokens - prompt
    with Phase(nc, f"p{half}_") as ph:
        w = ph.sb("w", [P, 2, KD, P])
        w_hi, w_lo = (ph.sb(n, [P, 2, KD, P], F32R) for n in ("w_hi", "w_lo"))
        stage = ph.sb("stage", [P, 2, HALF])
        glu = ph.sb("glu", [P, 2, HALF])
        conv = ph.sb("conv", [P, CB, HALF])
        ush = ph.sb("ush", [P, CB, DB, HIST + DS])
        hist_rows = ph.sb("hist_rows", [120, 2, CC])
        bias = ph.sb("bias", [P, 2])
        acc = [[ph.ps(f"acc{s}_{i}", [P, 512]) for i in range(NTB)] for s in range(2)]
        ph_h = ph.ps("hist", [P, 512])
        w_loaded = [ph.sem(f"w_loaded{i}") for i in range(2)]
        w_split = [ph.sem(f"w_split{i}") for i in range(2)]
        split_used = [ph.sem(f"split_used{i}") for i in range(2)]
        stored = [ph.sem(f"stored{i}") for i in range(2)]
        acc_full, acc_kept, glu_done, conv_done, u_stored, hi_done, seen, seen_act = (
            ph.sem(n) for n in ("acc_full", "acc_kept", "glu_done", "conv_done", "u_stored", "hi_done", "seen", "seen_act"))
        h_loaded, h_turned, h_kept, s_chain, bias_kept = (ph.sem(n) for n in ("h_loaded", "h_turned", "h_kept", "chain", "bias_kept"))

        def steps(e):
            with e.Fori(0, CB) as i:
                yield 2 * i, i, 0, i, i * P, P, "ca"
                yield 2 * i + 1, i, 1, i + CB, i * P + CC, P, "cb"
            with e.Fori(0, 6) as i:
                yield 2 * i + 8, i + 4, 0, 2 * i + 8, i * (2 * P) + 8 * P, P, "plain"
                yield 2 * i + 9, i + 4, 1, 2 * i + 9, i * (2 * P) + 9 * P, P, "plain"
            yield 20, 10, 0, KI_BLK, KI_BLK * P, KI_ROWS, "plain"
            with e.Fori(0, 8) as i:
                yield 2 * i + 21, i + 10, 1, 2 * i + 21, i * (2 * P) + COL_G, P, "gate"
                yield 2 * i + 22, i + 11, 0, 2 * i + 22, i * (2 * P) + COL_G + P, P, "gate"

        with ph.block() as block:
            @block.sync
            def _(sp):
                if samples:
                    for r in range(2):
                        sp.dma_start(hist_rows[:, r, :], c.inp["state_conv"][0, 4 * r:4 * r + 4].rearrange("b h c -> (b h) c")).then_inc(h_loaded, 16)
                w_in = c.inp["w_in"][0].rearrange("(k p) n -> p k n", p=P)
                for s, use, slot, blk, col, rows, kind in steps(sp):
                    sp.wait_ge(w_split[slot], use + 1)
                    sp.dma_start(w[:, slot, :, 0:rows], w_in[:, :, bass.ds(col, rows)]).then_inc(w_loaded[slot], 16)

            @block.gpsimd
            def _(pool):
                for slot in range(2):
                    pool.sem_inc(w_split[slot], 1)
                for s, use, slot, blk, col, rows, kind in steps(pool):
                    pool.wait_ge(w_loaded[slot], 16 * use + 16)
                    pool.wait_ge(split_used[slot], use + 1)
                    pool.sem_inc(seen, 1)
                    nc.gpsimd.tensor_copy(w_hi[:, slot], w[:, slot]).then_inc(hi_done, 1)
                    pool.wait_ge(hi_done, s + 1)
                    pool.sem_inc(seen, 1)
                    nc.gpsimd.tensor_tensor(w_lo[:, slot], w[:, slot], w_hi[:, slot].bitcast(F32), ALU.subtract).then_inc(w_split[slot], 1)
                pool.wait_ge(glu_done, 2 * CB)
                pool.dma_start(c.featT[0:CC, first:first + prompt].rearrange("(b p) t -> p b t", p=P), uh[:, :, HIST + first:HIST + first + prompt]).then_inc(u_stored, 16)
                if samples:
                    for b in range(CB):
                        pool.dma_start(c.featT[b * P:(b + 1) * P, T:TT].rearrange("p (b t) -> p b t", b=DB), ush[:, b, :, HIST:HIST + DS]).then_inc(u_stored, 16)
                pool.wait_ge(conv_done, CB)
                pool.dma_start(c.convT[:, first:first + tokens].rearrange("(b p) t -> p b t", p=P), conv[:, :, 0:tokens]).then_inc(u_stored, 16)
                pool.wait_ge(u_stored, 16 * (2 + (CB if samples else 0)))

            @block.tensor
            def _(pe):
                pe.sem_inc(split_used[0], 1)
                pe.sem_inc(split_used[1], 1)
                if samples:
                    pe.wait_ge(h_loaded, 32)
                    for b in range(CB):
                        for r in range(2):
                            if r == 0 and b > 0:
                                pe.wait_ge(h_kept, b)
                            t = nc.tensor.transpose(ph_h[:, r * 120:r * 120 + 120], hist_rows[:, r, b * P:(b + 1) * P], c.ident[0:120, 0:120])
                        t.then_inc(h_turned, 1)
                for s, use, slot, blk, col, rows, kind in steps(pe):
                    pe.wait_ge(w_split[slot], use + 2)
                    for tb in range(NTB):
                        at = slice(tb * width, (tb + 1) * width)
                        pe.wait_ge(acc_kept, NTB * s + (tb + 1))
                        for k in range(KD):
                            for n, (wp, xp) in enumerate(((w_hi, x_hi), (w_hi, x_lo), (w_lo, x_hi))):
                                m = nc.tensor.matmul(acc[slot][tb][0:rows, 0:width], wp[:, slot, k, 0:rows], xp[:, k, at],
                                                     start=(k == 0 and n == 0), stop=(k == KD - 1 and n == 2))
                        m.then_inc(acc_full, 1)
                    pe.wait_ge(acc_full, NTB * s + NTB)
                    pe.sem_inc(split_used[slot], 1)

            @block.scalar
            def _(act):
                act.sem_inc(acc_kept, 2 * NTB)
                for s, use, slot, blk, col, rows, kind in steps(act):
                    nc.scalar.copy(bias[:, slot:slot + 1], cols[:, bass.ds(blk, 1)]).then_inc(bias_kept, 1)
                    act.wait_ge(bias_kept, s + 1)
                    if kind == "ca":
                        act.wait_ge(glu_done, 2 * blk)
                    if kind in ("plain", "gate"):
                        act.wait_ge(stored[slot], (use - 4) * 16)
                    out = glu if kind in ("ca", "cb") else stage
                    func = ACT.Sigmoid if kind in ("cb", "gate") else ACT.Identity
                    for tb in range(NTB):
                        act.wait_ge(acc_full, NTB * s + (tb + 1))
                        nc.scalar.activation(out[0:rows, slot, tb * width:(tb + 1) * width], acc[slot][tb][0:rows, 0:width], func,
                                             bias=bias[0:rows, slot:slot + 1]).then_inc(acc_kept, 1)
                    if kind in ("plain", "gate"):
                        act.wait_ge(acc_kept, NTB * s + 3 * NTB)
                        act.dma_start(c.featT[bass.ds(col, rows), first:first + tokens], stage[0:rows, slot, 0:tokens]).then_inc(stored[slot], 16)
                act.wait_ge(stored[0], 16 * (7 + 8))
                act.wait_ge(stored[1], 16 * (6 + 8))

            @block.vector
            def _(dve):
                ch = Chain(dve, s_chain)
                if half == 0:
                    ch.mark(nc.vector.memset(uh[:, :, 0:HIST], 0.0))
                if samples:
                    for b in range(CB):
                        dve.wait_ge(h_turned, b + 1)
                        nc.vector.tensor_copy(ush[:, b, :, 0:HIST], ph_h[:, 0:240].rearrange("p (b h) -> p b h", b=DB)).then_inc(h_kept, 1)
                with dve.Fori(0, CB) as i:
                    dve.wait_ge(acc_kept, 2 * NTB * i + 4 * NTB)
                    nc.vector.tensor_tensor(uh[:, bass.ds(i, 1), HIST + first:HIST + first + prompt], glu[:, 0:1, 0:prompt], glu[:, 1:2, 0:prompt], ALU.mult).then_inc(glu_done, 1)
                    if samples:
                        g1, g2 = (glu[:, n:n + 1, prompt:tokens].rearrange("p a (b t) -> p a b t", b=DB) for n in range(2))
                        nc.vector.tensor_tensor(ush[:, bass.ds(i, 1), :, HIST:HIST + DS], g1, g2, ALU.mult).then_inc(glu_done, 1)
                    else:
                        dve.sem_inc(glu_done, 1)
                dve.wait_ge(glu_done, 2 * CB)
                ch.sync()
                if samples:
                    dve.wait_ge(h_kept, CB)
                for b in range(CB):
                    out, outs = conv[:, b, 0:prompt], conv[:, b, prompt:tokens].rearrange("p (b t) -> p b t", b=DB) if samples else None
                    for tap in range(TAPS):
                        wt = taps[:, b, tap:tap + 1]
                        pairs = [(out, uh[:, b, first + tap:first + tap + prompt])]
                        if samples:
                            pairs.append((outs, ush[:, b, :, tap:tap + DS]))
                        ch.sync()
                        for dst, src in pairs:
                            if tap == 0:
                                ch.mark(nc.vector.tensor_scalar(dst, src, wt, cols[:, VEC_CB + b:VEC_CB + b + 1], ALU.mult, ALU.add))
                            else:
                                ch.mark(nc.vector.scalar_tensor_tensor(dst, src, wt, dst, ALU.mult, ALU.add))
                    ch.sync()
                    dve.sem_inc(conv_done, 1)


def keep_keys(nc, c, kT, kiT, v_tok, wi_tok):
    with Phase(nc, "k_") as ph:
        st = ph.sb("st", [P, 2, 4, P])
        sti = ph.sb("sti", [KI_ROWS, 2, P])
        ulast = ph.sb("ulast", [P, CB, HIST + S])
        utok = ph.sb("utok", [HIST + S, CC])
        k_tok = ph.sb("k_tok", [P, NT + 1, 2 * P])
        vs_tok = ph.sb("vs_tok", [S, 2 * P])
        ki_tok = ph.sb("ki_tok", [P, NT + 1, HD])
        kv = [ph.ps(f"kv{i}", [P, 512]) for i in range(2)]
        kw = [ph.ps(f"kw{i}", [P, 512]) for i in range(2)]
        pu = ph.ps("pu", [P, 512])
        keys_loaded, turned, kv_kept, ki_kept, u_loaded, u_turned, u_kept, saved = (
            ph.sem(n) for n in ("keys_loaded", "turned", "kv_kept", "ki_kept", "u_loaded", "u_turned", "u_kept", "saved"))
        loaded = [ph.sem(f"loaded{i}") for i in range(2)]

        def tiles(e):
            with e.Fori(0, NT // 2) as i:
                yield i, 0, P
                yield i, 1, P
            yield NT // 2, 0, S

        with ph.block() as block:
            @block.sync
            def _(sp):
                for i, slot, n in tiles(sp):
                    sp.wait_ge(turned, 2 * i + slot + 1)
                    t0 = (2 * i + slot) * P
                    sp.dma_start(st[:, slot, :, 0:n], c.featT[COL_K:COL_QI, bass.ds(t0, n)].rearrange("(b p) t -> p b t", p=P)).then_inc(loaded[slot], 16)
                    sp.dma_start(sti[:, slot, 0:n], c.featT[COL_KI:COL_G, bass.ds(t0, n)]).then_inc(loaded[slot], 16)
                out = c.out
                sp.wait_ge(kv_kept, 2 * (NT + 1) + 4)
                sp.wait_ge(ki_kept, NT + 1 + 2)
                sp.dma_start(out["k_prompt"][0, 0].rearrange("(i p) h d -> p i (h d)", p=P), k_tok[:, 0:NT]).then_inc(saved, 16)
                sp.dma_start(out["k_sample"][0].rearrange("b s h d -> (b s) (h d)"), k_tok[0:S, NT]).then_inc(saved, 16)
                sp.dma_start(out["v_prompt"][0, 0].rearrange("(i p) h d -> p i (h d)", p=P), v_tok[:]).then_inc(saved, 16)
                sp.dma_start(out["v_sample"][0].rearrange("b s h d -> (b s) (h d)"), vs_tok[:]).then_inc(saved, 16)
                sp.dma_start(out["ki_prompt"][0, 0].rearrange("(i p) d -> p i d", p=P), ki_tok[:, 0:NT]).then_inc(saved, 16)
                sp.dma_start(out["ki_sample"][0].rearrange("b s d -> (b s) d"), ki_tok[0:S, NT]).then_inc(saved, 16)
                sp.wait_ge(saved, 96)

            @block.gpsimd
            def _(pool):
                out = c.out
                pool.dma_start(kT[:], c.featT[COL_K:COL_V, 0:T].rearrange("(b p) t -> p b t", p=P)).then_inc(keys_loaded, 16)
                pool.dma_start(kiT[0:HD], c.featT[COL_KI:COL_WI, 0:T]).then_inc(keys_loaded, 16)
                pool.dma_start(ulast[:], c.featT[0:CC, T - HIST:TT].rearrange("(b p) t -> p b t", p=P)).then_inc(u_loaded, 16)
                pool.dma_start(out["conv_sample"][0, :, 0:HIST - DS], c.inp["state_conv"][0, :, DS:HIST]).then_inc(keys_loaded, 16)
                pool.wait_ge(u_kept, 1)
                pool.dma_start(out["conv_prompt"][0, 0], utok[0:HIST]).then_inc(keys_loaded, 16)
                for b in range(DB):
                    pool.dma_start(out["conv_sample"][0, b, HIST - DS:HIST], utok[HIST + b * DS:HIST + b * DS + DS]).then_inc(keys_loaded, 16)
                pool.wait_ge(keys_loaded, 16 * (4 + DB))

            @block.tensor
            def _(pe):
                pe.sem_inc(turned, 2)
                for i, slot, n in tiles(pe):
                    t = 2 * i + slot
                    pe.wait_ge(loaded[slot], 32 * i + 32)
                    pe.wait_ge(kv_kept, 2 * t + 2)
                    for b in range(4):
                        nc.tensor.transpose(kv[slot][0:n, b * P:(b + 1) * P], st[:, slot, b, 0:n], c.ident[:])
                    pe.wait_ge(ki_kept, t + 1)
                    nc.tensor.transpose(kw[slot][0:n, 0:KI_ROWS], sti[:, slot, 0:n], c.ident[0:KI_ROWS, 0:KI_ROWS]).then_inc(turned, 1)
                pe.wait_ge(u_loaded, 16)
                for b in range(CB):
                    u = nc.tensor.transpose(pu[0:HIST + S, b * P:(b + 1) * P], ulast[:, b, :], c.ident[:])
                u.then_inc(u_turned, 1)

            @block.scalar
            def _(act):
                act.sem_inc(kv_kept, 4)
                for i, slot, n in tiles(act):
                    t = 2 * i + slot
                    act.wait_ge(turned, t + 3)
                    act.nop()
                    nc.scalar.copy(k_tok[0:n, bass.ds(t, 1), :], kv[slot][0:n, 0:2 * P].rearrange("p (a c) -> p a c", a=1)).then_inc(kv_kept, 1)
                    v_out = v_tok[0:n, bass.ds(t, 1), :] if n == P else vs_tok[:].rearrange("p (a c) -> p a c", a=1)
                    nc.scalar.copy(v_out, kv[slot][0:n, 2 * P:4 * P].rearrange("p (a c) -> p a c", a=1)).then_inc(kv_kept, 1)

            @block.vector
            def _(dve):
                dve.sem_inc(ki_kept, 2)
                for i, slot, n in tiles(dve):
                    t = 2 * i + slot
                    dve.wait_ge(turned, t + 3)
                    nc.vector.tensor_copy(ki_tok[0:n, bass.ds(t, 1), :], kw[slot][0:n, 0:HD].rearrange("p (a c) -> p a c", a=1))
                    nc.vector.tensor_scalar(wi_tok[0:n, bass.ds(t, 1), :], kw[slot][0:n, HD:KI_ROWS].rearrange("p (a c) -> p a c", a=1),
                                            float(NIH) ** -0.5, None, ALU.mult).then_inc(ki_kept, 1)
                dve.wait_ge(u_turned, 1)
                nc.vector.tensor_copy(utok[:], pu[0:HIST + S, :]).then_inc(u_kept, 1)


ROUNDS = 28
BIG = 1e30
NQ = 4
IDX_SCALE = float(HD) ** -0.5
SM_SCALE = float(HD) ** -0.5


class ThresholdMemory:

    def __init__(self, ph, n, rows=P):
        self.low, self.width, self.mid, self.count, self.step, self.high, self.top, self.need = (
            ph.sb(f"th_{x}", [rows, n]) for x in ("low", "width", "mid", "count", "step", "high", "top", "need"))


def search_start(ch, eng, th):
    ch.link(eng.tensor_tensor(th.width[:], th.top[:], th.low[:], ALU.subtract))
    ch.link(eng.tensor_scalar(th.width[:], th.width[:], 1.0, 1e-30, ALU.mult, ALU.add))
    ch.link(eng.tensor_tensor(th.mid[:], th.low[:], th.width[:], ALU.add))


def search_round(ch, eng, th, parts):
    for a, b, bound, compare in parts:
        ch.mark(eng.tensor_scalar(th.step[:, a:b], th.count[:, a:b], bound, None, compare))
    ch.sync()
    ch.link(eng.tensor_tensor(th.step[:], th.step[:], th.width[:], ALU.mult))
    ch.mark(eng.tensor_tensor(th.low[:], th.low[:], th.step[:], ALU.add))
    ch.link(eng.tensor_scalar(th.width[:], th.width[:], 0.5, None, ALU.mult))
    ch.link(eng.tensor_tensor(th.mid[:], th.low[:], th.width[:], ALU.add))


def search_end(ch, eng, th):
    ch.link(eng.tensor_scalar(th.width[:], th.width[:], 8.0, None, ALU.mult))
    ch.link(eng.tensor_tensor(th.high[:], th.low[:], th.width[:], ALU.add))


def select_stage(stage, ch, nc, score, low, high, need, sure, edge, run):
    if stage == 0:
        ch.link(nc.vector.tensor_scalar(sure, score, high, None, ALU.is_gt, ALU.add, accum_out=need))
    elif stage == 1:
        ch.mark(nc.vector.tensor_scalar(need, need, -1.0, float(TOPK), ALU.mult, ALU.add))
        ch.link(nc.vector.scalar_tensor_tensor(edge, score, low, sure, ALU.is_ge, ALU.subtract))
    elif stage == 2:
        ch.link(nc.vector.tensor_tensor_scan(run, edge, edge, 0.0, ALU.add, ALU.max))
    elif stage == 3:
        ch.link(nc.vector.scalar_tensor_tensor(edge, run, need, edge, ALU.is_le, ALU.mult))
    elif stage == 4:
        ch.link(nc.vector.scalar_tensor_tensor(sure, edge, -1.0, sure, ALU.add, ALU.add))
    else:
        ch.link(nc.vector.tensor_scalar(score, sure, BIG, None, ALU.mult))


SELECT_STAGES = 6


def select_row_tile(ch, nc, *args):
    for stage in range(SELECT_STAGES):
        select_stage(stage, ch, nc, *args)


def attend_prompt_step(nc, c, mem, cls):
    nxt = cls + 1
    has_next, here = nxt < NT // NQ, cls >= 0
    last_class = here and not has_next
    LN = 512 * (nxt + 1)
    next_units = [(u, min(u + 1024, LN)) for u in range(0, LN, 1024)]
    DOTS = NIH * len(next_units)
    QN, Q0 = 512 * nxt, 512 * cls
    th = mem.th
    if has_next:
        sc_next = mem.sc[nxt % 2]
    if here:
        L = 512 * nxt
        G = nxt
        sc = mem.sc[cls % 2]
        units = [(u, min(u + 1024, L)) for u in range(0, L, 1024)]
        U = len(units)
        TG = 8 * G + 2
    RH = NH - 1
    assert RH * NQ == ROUNDS
    with Phase(nc, f"a{nxt}_") as ph:
        qi_loaded = [ph.sem(f"qi_loaded{i}") for i in range(2)]
        q_loaded = [ph.sem(f"q_loaded{i}") for i in range(2)]
        dots_full, dots_kept, relu_used, qi_used = (
            ph.sem(n) for n in ("dots_full", "dots_kept", "relu_used", "qi_used"))
        bracket_ready, mid_ready, dve_counted, act_counted, p_chain = (
            ph.sem(n) for n in ("bracket_ready", "mid_ready", "dve_counted", "act_counted", "pool_chain"))
        s_full, s_kept, max_ready, exp_done, t_done, t_full, t_kept, pv_done, o_done, ot_full, o_stored = (
            ph.sem(n) for n in ("s_full", "s_kept", "max_ready", "exp_done", "t_done", "t_full", "t_kept", "pv_done",
                                "o_done", "ot_full", "o_stored"))
        s_chain, seen, seen_pool = ph.sem("chain"), ph.sem("seen"), ph.sem("seen_pool")

        def tiles(e):
            with e.Fori(0, NQ // 2) as i:
                yield i, 0, 2 * i
                yield i, 1, 2 * i + 1

        with ph.block() as block:
            @block.sync
            def _(sp):
                if has_next:
                    for i, slot, j in tiles(sp):
                        sp.wait_ge(qi_used, j + 1)
                        sp.dma_start(mem.qi_st[0:HD, slot], c.featT[COL_QI:COL_KI, bass.ds(j * P + QN, P)].rearrange("(h d) t -> d h t", d=HD)).then_inc(qi_loaded[slot], 16)
                if here:
                    for i, slot, j in tiles(sp):
                        sp.wait_ge(pv_done, 8 * j + 2)
                        for gl in range(2):
                            for gh in range(2):
                                r0 = COL_Q + (2 * gh + gl) * P
                                sp.dma_start(mem.q_st[gl * HD:(gl + 1) * HD, slot, 4 * gh + 2 * gl:4 * gh + 2 * gl + 2], c.featT[r0:r0 + P, bass.ds(j * P + Q0, P)].rearrange("(r d) t -> d r t", d=HD)).then_inc(q_loaded[slot], 16)

            @block.tensor
            def _(pe):
                if has_next:
                    pe.sem_inc(qi_used, 2)
                    for i, slot, j in tiles(pe):
                        pe.wait_ge(qi_loaded[slot], 16 * i + 16)
                        for u, (a, b) in enumerate(next_units):
                            for h in range(NIH):
                                pe.wait_ge(dots_kept, j * DOTS + (NIH * u + h + 1))
                                for k in range(a, b, 512):
                                    m = nc.tensor.matmul(mem.ps_s[h % 2][:, k - a:k - a + 512], mem.qi_st[:, slot, h, :],
                                                         mem.kiT[:, k:k + 512], start=True, stop=True)
                                m.then_inc(dots_full, 1)
                        pe.wait_ge(dots_full, j * DOTS + DOTS)
                        pe.sem_inc(qi_used, 1)
                    pe.wait_ge(dots_kept, DOTS * NQ + 2)
                if not here:
                    return
                pe.sem_inc(t_done, 2)
                pe.sem_inc(pv_done, 2)
                for i, slot, j in tiles(pe):
                    pe.wait_ge(q_loaded[slot], 64 * i + 64)

                    def scores(h):
                        for u, (a, b) in enumerate(units):
                            n = h * U + u
                            pe.wait_ge(s_kept, j * (8 * U) + (n + 1))
                            for k in range(a, b, 512):
                                m = nc.tensor.matmul(mem.ps_s[n % 2][:, k - a:k - a + 512], mem.q_st[:, slot, h, :],
                                                     mem.kT[:, h // 4, k:k + 512], start=True, stop=True)
                            m.then_inc(s_full, 1)

                    def turn(h):
                        pe.wait_ge(exp_done, 8 * j + (h + 1))
                        for g in range(G):
                            n = h * G + g
                            pe.wait_ge(t_kept, j * TG + (n + 1))
                            for b in range(4):
                                k = 4 * g + b
                                m = nc.tensor.transpose(mem.ps_t[n % 2][:, b * P:(b + 1) * P], mem.sm[:, h % 2, k * P:(k + 1) * P], c.ident[:])
                            m.then_inc(t_full, 1)
                        pe.wait_ge(t_full, j * TG + (h + 1) * G)
                        pe.sem_inc(t_done, 1)

                    def values(h):
                        pe.wait_ge(o_done, 8 * j + (h + 1))
                        pe.wait_ge(t_kept, j * TG + ((h + 1) * G + 2))
                        for k in range(4 * G):
                            m = nc.tensor.matmul(mem.ps_o[h % 2][:, 0:P], mem.pT[:, h % 2, k, :],
                                                 mem.v_tok[:, k, (h // 4) * P:(h // 4 + 1) * P], start=(k == 0), stop=(k == 4 * G - 1))
                        m.then_inc(pv_done, 1)

                    scores(0)
                    for h in range(NH):
                        if h + 1 < NH:
                            scores(h + 1)
                        turn(h)
                        if h:
                            values(h - 1)
                    values(NH - 1)
                    pe.wait_ge(o_done, 8 * j + 10)
                    for n in range(2):
                        pe.wait_ge(t_kept, j * TG + (8 * G + n + 1))
                        for b in range(2):
                            m = nc.tensor.transpose(mem.ps_t[n][:, b * P:(b + 1) * P], mem.o_sb[:, (2 * n + b) * P:(2 * n + b + 1) * P], c.ident[:])
                        m.then_inc(t_full, 1)
                    pe.wait_ge(t_full, j * TG + TG)
                    pe.sem_inc(ot_full, 1)

            @block.scalar
            def _(act):
                if has_next:
                    act.sem_inc(dots_kept, 2)
                    for i, slot, j in tiles(act):
                        for u, (a, b) in enumerate(next_units):
                            for h in range(NIH):
                                n = NIH * u + h + 1
                                act.wait_ge(dots_full, j * DOTS + n)
                                act.wait_ge(relu_used, j * DOTS + n)
                                nc.scalar.activation(mem.relu[:, h % 2, 0:b - a], mem.ps_s[h % 2][:, 0:b - a], ACT.Relu, scale=IDX_SCALE).then_inc(dots_kept, 1)
                if not here:
                    return
                act.sem_inc(t_kept, 2)
                for i, slot, j in tiles(act):
                    for h in range(NH):
                        act.wait_ge(max_ready, 8 * j + (h + 1))
                        nc.scalar.activation(mem.sm[:, h % 2, 0:L], mem.sm[:, h % 2, 0:L], ACT.Exp, bias=mem.negmax[:, h:h + 1],
                                             scale=SM_SCALE, accum_out=mem.total[:, h:h + 1]).then_inc(exp_done, 1)
                        act.wait_ge(pv_done, 8 * j + (h + 1))
                        for g in range(G):
                            act.wait_ge(t_full, j * TG + (h * G + g + 1))
                            nc.scalar.copy(mem.pT[:, h % 2, 4 * g:4 * g + 4, :], mem.ps_t[(h * G + g) % 2][:].rearrange("p (b q) -> p b q", b=4)).then_inc(t_kept, 1)
                        if has_next and h < RH:
                            act.wait_ge(mid_ready, RH * j + (h + 1))
                            for t in (2, 3):
                                act.wait_ge(act_counted, (2 * RH) * j + (2 * h + t - 2))
                                nc.scalar.activation(mem.junk_act[:, 0:LN], sc_next[:, t, 0:LN], ACT.Sign, bias=th.mid[:, t:t + 1], scale=-1.0,
                                                     accum_out=th.count[:, t:t + 1]).then_inc(act_counted, 1)
                    act.wait_ge(o_stored, 16 * j)
                    for n in range(2):
                        act.wait_ge(t_full, j * TG + (8 * G + n + 1))
                        nc.scalar.copy(mem.oT_st[:, 2 * n:2 * n + 2, :], mem.ps_t[n][:, 0:2 * P].rearrange("p (b q) -> p b q", b=2)).then_inc(t_kept, 1)
                    act.wait_ge(t_kept, j * TG + (TG + 2))
                    act.dma_start(c.oT[:, bass.ds(j * P + Q0, P)].rearrange("(b p) t -> p b t", p=P), mem.oT_st[:]).then_inc(o_stored, 16)
                act.wait_ge(o_stored, 16 * NQ)

            @block.vector
            def _(dve):
                ch = Chain(dve, s_chain)

                def index_sums(j):
                    ch.link(nc.vector.tensor_copy(mem.wi_now[:], mem.wi_tok[:, bass.ds(j + NQ * nxt, 1), :]))
                    for u, (a, b) in enumerate(next_units):
                        at = sc_next[:, bass.ds(j, 1), a:b]
                        for h in range(NIH):
                            dve.wait_ge(dots_kept, j * DOTS + (NIH * u + h + 3))
                            src, w = mem.relu[:, h % 2:h % 2 + 1, 0:b - a], mem.wi_now[:, 0, h:h + 1]
                            if h == 0:
                                ch.link(nc.vector.tensor_scalar(at, src, w, None, ALU.mult))
                            else:
                                ch.link(nc.vector.scalar_tensor_tensor(at, src, w, at, ALU.mult, ALU.add))
                            dve.sem_inc(relu_used, 1)
                    row = sc_next[:, bass.ds(j, 1), 0:LN]
                    last = sc_next[:, bass.ds(j, 1), LN - 512:LN]
                    late = mem.sm[:, 0:1, 0:512]
                    ch.mark(nc.vector.tensor_reduce(th.low[:, bass.ds(j, 1)], row, AX.X, ALU.min))
                    ch.link(nc.vector.tensor_scalar(late, mem.key_no[:], mem.query_no[:, bass.ds(j, 1)], -BIG, ALU.is_gt, ALU.mult))
                    ch.link(nc.vector.tensor_tensor(last, last, late, ALU.add))
                    ch.link(nc.vector.tensor_reduce(th.top[:, bass.ds(j, 1)], row, AX.X, ALU.max))

                def count(t):
                    return nc.vector.tensor_scalar(mem.junk_dve[:, t * LN:(t + 1) * LN], sc_next[:, t, 0:LN], th.mid[:, t:t + 1], None, ALU.is_ge, ALU.add,
                                                   accum_out=th.count[:, t:t + 1])

                def select(j, stages, buffers):
                    score = sc[:, bass.ds(j, 1), 0:L].rearrange("p a k -> p (a k)")
                    for stage in stages:
                        select_stage(stage, ch, nc, score, mem.bounds[:, 0:1], mem.bounds[:, 1:2], mem.bounds[:, 2:3],
                                     *(b[:, 0:L] for b in buffers))

                def keep_bounds(j):
                    ch.mark(nc.vector.tensor_copy(mem.bounds[:, 0:1], th.low[:, bass.ds(j, 1)]))
                    ch.link(nc.vector.tensor_copy(mem.bounds[:, 1:2], th.high[:, bass.ds(j, 1)]))

                if has_next:
                    dve.sem_inc(relu_used, 2)
                    for i, slot, j in tiles(dve):
                        if here:
                            keep_bounds(j)
                            select(j, range(SELECT_STAGES), (mem.sm[:, 0], mem.sm[:, 1], mem.pT[:, 0].rearrange("p k q -> p (k q)")))
                        index_sums(j)
                        ch.restart()
                    if here:
                        dve.sem_inc(bracket_ready, 1)
                if not here:
                    search_start(ch, nc.vector, th)
                    ch.restart()
                    with dve.Fori(0, ROUNDS):
                        for t in range(NQ):
                            ch.mark(count(t))
                        ch.sync()
                        search_round(ch, nc.vector, th, [(0, NQ, TOPK - 0.5, ALU.is_ge)])
                        ch.restart()
                    search_end(ch, nc.vector, th)
                else:
                    dve.sem_inc(s_kept, 2)
                    dve.sem_inc(o_done, 2)
                    free = mem.sc[nxt % 2]
                    free = [free[:].rearrange("p t k -> p (t k)")[:, n * T:(n + 1) * T] for n in range(3)]
                    if last_class:
                        keep_bounds(0)
                        select(0, range(SELECT_STAGES), free)
                        ch.restart()

                    def tile(i, slot, j):
                        def invert(h):
                            dve.wait_ge(exp_done, 8 * j + (h + 1))
                            ch.mark(nc.vector.reciprocal(mem.inv[:, h:h + 1], mem.total[:, h:h + 1]))

                        def normalise(h):
                            ch.sync()
                            dve.wait_ge(pv_done, 8 * j + (h + 3))
                            if h == 0:
                                dve.wait_ge(ot_full, j)
                            at = (h // 2 % 2) * HD
                            nc.vector.tensor_scalar(mem.o_sb[:, h * HD:(h + 1) * HD], mem.ps_o[h % 2][:, at:at + HD], mem.inv[:, h:h + 1], None,
                                                    ALU.mult).then_inc(o_done, 1)

                        for h in range(NH):
                            dve.wait_ge(t_done, 8 * j + (h + 1))
                            for u, (a, b) in enumerate(units):
                                n = h * U + u
                                dve.wait_ge(s_full, j * (8 * U) + (n + 1))
                                dve.sem_inc(seen, 1)
                                start = -3e38 if u == 0 else mem.max2[:, u - 1:u]
                                mask = sc[:, j, a:b]
                                ch.link(nc.vector.tensor_tensor_reduce(mem.sm[:, h % 2, a:b], mem.ps_s[n % 2][:, 0:b - a], mask, 1.0, start,
                                                                       ALU.add, ALU.max, mem.max2[:, u:u + 1]))
                                dve.sem_inc(s_kept, 1)
                            if h == 0:
                                dve.wait_ge(exp_done, 8 * j)
                            nc.vector.tensor_scalar(mem.negmax[:, h:h + 1], mem.max2[:, U - 1:U], -SM_SCALE, None, ALU.mult).then_inc(max_ready, 1)
                            dve.wait_ge(max_ready, 8 * j + (h + 1))
                            if h >= 2:
                                invert(h - 2)
                            if has_next:
                                if h < RH:
                                    dve.wait_ge(mid_ready, RH * j + (h + 1))
                                    dve.sem_inc(seen, 1)
                                    count(0).then_inc(dve_counted, 1)
                            elif j < NQ - 1 and 1 <= h <= SELECT_STAGES:
                                if h == 1:
                                    keep_bounds(j + 1)
                                select(j + 1, (h - 1,), free)
                            if h >= 2:
                                normalise(h - 2)
                            if has_next and h < RH:
                                count(1).then_inc(dve_counted, 1)
                        for h in (NH - 2, NH - 1):
                            invert(h)
                            normalise(h)
                        ch.restart()

                    for j in range(NQ):
                        tile(j // 2, j % 2, j)
            @block.gpsimd
            def _(pool):
                if not (here and has_next):
                    return
                ch = Chain(pool, p_chain)
                pool.wait_ge(bracket_ready, 1)
                search_start(ch, nc.gpsimd, th)
                ch.restart()
                pool.sem_inc(mid_ready, 1)
                with pool.Fori(0, ROUNDS) as r:
                    pool.wait_ge(dve_counted, 2 * r + 2)
                    pool.wait_ge(act_counted, 2 * r + 2)
                    pool.sem_inc(seen_pool, 1)
                    search_round(ch, nc.gpsimd, th, [(0, 2, TOPK - 0.5, ALU.is_ge), (2, NQ, LN - 2 * TOPK + 0.5, ALU.is_le)])
                    ch.restart()
                    pool.sem_inc(mid_ready, 1)
                search_end(ch, nc.gpsimd, th)


def attend_prompt(nc, c, kT, kiT, v_tok, wi_tok):
    with Phase(nc, "q_") as ph:
        mem = Ctx()
        mem.kT, mem.kiT, mem.v_tok, mem.wi_tok = kT, kiT, v_tok, wi_tok
        mem.th = ThresholdMemory(ph, NQ)
        mem.qi_st = ph.sb("qi_st", [P, 2, NIH, P])
        mem.q_st = ph.sb("q_st", [P, 2, NH, P])
        mem.wi_now = ph.sb("wi_now", [P, 1, NIH])
        mem.sc = [ph.sb("sc0", [P, NQ, T - 512]), ph.sb("sc1", [P, NQ, T])]
        mem.relu = ph.sb("relu", [P, 2, 1024])
        mem.key_no = ph.sb("key_no", [P, 512])
        mem.query_no = ph.sb("query_no", [P, NQ])
        mem.junk_act = ph.sb("junk_act", [P, T], mybir.dt.bfloat16)
        mem.junk_dve = ph.sb("junk_dve", [P, 2 * T], mybir.dt.bfloat16)
        mem.bounds = ph.sb("bounds", [P, 4])
        mem.sm = ph.sb("sm", [P, 2, T])
        mem.max2, mem.negmax, mem.total, mem.inv = (ph.sb(n, [P, w]) for n, w in (("max2", 2), ("negmax", NH), ("total", NH), ("inv", NH)))
        mem.pT = ph.sb("pT", [P, 2, NT, P])
        mem.o_sb = ph.sb("o_sb", [P, NH * HD])
        mem.oT_st = ph.sb("oT_st", [P, 4, P])
        mem.ps_s = [ph.ps(f"s{i}", [P, 1024]) for i in range(2)]
        mem.ps_t = [ph.ps(f"t{i}", [P, 512]) for i in range(2)]
        mem.ps_o = [ph.ps(f"o{i}", [P, 512]) for i in range(2)]
        made = ph.sem("made")
        with ph.block() as block:
            @block.vector
            def _(dve):
                nc.vector.memset(mem.q_st[:], 0.0)
                nc.vector.memset(mem.qi_st[:], 0.0)
                nc.vector.memset(kiT[HD:P], 0.0)

            @block.gpsimd
            def _(pool):
                nc.gpsimd.iota(mem.key_no[:], [[1, 512]], base=0, channel_multiplier=0, allow_small_or_imprecise_dtypes=True).then_inc(made, 1)
                nc.gpsimd.iota(mem.query_no[:], [[P, NQ]], base=0, channel_multiplier=1, allow_small_or_imprecise_dtypes=True).then_inc(made, 1)
                pool.wait_ge(made, 2)
        for cls in range(-1, NT // NQ):
            attend_prompt_step(nc, c, mem, cls)


class Ctx:
    pass


LS = 2048 + DS
CHUNKS = [(i * 512, 512) for i in range(4)] + [(2048, DS)]
SLOTS = 16
N_PAGES, PAGE = 16, 128


def sample_index(nc, c, mem):
    with Phase(nc, "i_") as ph:
        page_of = ph.sb("page_of", [P, DB], I32)
        part = ph.sb("part", [P, 1], I32)
        fl = ph.sb("fl", [P, DB])
        partf = ph.sb("partf", [P, 1])
        kid = ph.sb("kid", [P, 2, SLOTS * HD])
        kiT = ph.sb("kiT", [P, 2, LS])
        qis = ph.sb("qis", [P, DB, NIH, DS])
        dots = ph.sb("dots", [P, 2, LS])
        wcol = ph.sb("wcol", [P, 2])
        wsel = ph.sb("wsel", [P, 2, S])
        sc = mem.mask
        sure, edge, run = (ph.sb(n, [S, LS]) for n in ("sure", "edge", "run"))
        junk = ph.sb("junk", [S, LS], mybir.dt.bfloat16)
        newpos = ph.sb("newpos", [S, DS])
        qmod = ph.sb("qmod", [S, 1])
        bounds = ph.sb("bounds", [S, 1])
        th = ThresholdMemory(ph, 1, S)
        pt = [ph.ps(f"t{i}", [P, 512]) for i in range(2)]
        pd = [ph.ps(f"d{i}", [P, 512]) for i in range(2)]
        pc = [ph.ps(f"c{i}", [P, 512]) for i in range(2)]
        table_loaded, rows_ready, zeroed, made, q_loaded, w_loaded = (ph.sem(n) for n in ("table_loaded", "rows_ready", "zeroed", "made", "q_loaded", "w_loaded"))
        kid_loaded = [ph.sem(f"kid_loaded{i}") for i in range(2)]
        new_loaded = [ph.sem(f"new_loaded{i}") for i in range(2)]
        turned, keys_kept, dots_full, dots_kept, sel_turned, sel_ready, sum_full, sum_kept, s_chain = (
            ph.sem(n) for n in ("turned", "keys_kept", "dots_full", "dots_kept", "sel_turned", "sel_ready", "sum_full", "sum_kept", "chain"))
        with ph.block() as block:
            @block.sync
            def _(sp):
                table = c.inp["page_table"].rearrange("b (g a) -> g a b", a=1)
                for g in range(N_PAGES):
                    sp.dma_start(page_of[8 * g:8 * g + 8, :], table[g].to_broadcast([8, DB]), allow_slow_non_contiguous=True).then_inc(table_loaded, 16)
                sp.wait_ge(zeroed, 1)
                for h in range(NIH):
                    sp.dma_start(qis[0:HD, :, h, :], c.featT[COL_QI + h * HD:COL_QI + (h + 1) * HD, T:TT].rearrange("d (b q) -> d b q", b=DB)).then_inc(q_loaded, 16)
                for g in range(2):
                    for b in range(4):
                        sp.dma_start(wcol[32 * b:32 * b + 32, g:g + 1], c.featT[COL_WI:COL_G, T + 4 * (4 * g + b):T + 4 * (4 * g + b) + 4],
                                     allow_slow_non_contiguous=True).then_inc(w_loaded, 16)
                for b in range(DB):
                    if b >= 2:
                        sp.wait_ge(dots_full, 5 * (b - 1))
                    sp.dma_start(kiT[0:HD, b % 2, 2048:LS], c.featT[COL_KI:COL_WI, T + DS * b:T + DS * b + DS], allow_slow_non_contiguous=True).then_inc(new_loaded[b % 2], 16)

            @block.gpsimd
            def _(pool):
                nc.gpsimd.iota(part[:], [[0, 1]], base=0, channel_multiplier=1).then_inc(made, 1)
                nc.gpsimd.iota(newpos[:], [[1, DS]], base=0, channel_multiplier=0, allow_small_or_imprecise_dtypes=True).then_inc(made, 1)
                nc.gpsimd.memset(mem.selT[:], 0.0).then_inc(made, 1)
                pool.wait_ge(made, 3)
                for g in range(2):
                    v = mem.selT[:, g].rearrange("r (b h q) -> r b h q", b=4, h=NIH)
                    nc.gpsimd.affine_select(out=v, in_=v, compare_op=ALU.not_equal, fill=1.0, base=-16 * g,
                                            pattern=[[-4, 4], [0, NIH], [-1, DS]], channel_multiplier=1).then_inc(made, 1)
                pool.wait_ge(rows_ready, 1)
                pool_rows = c.inp["cache_kidx"][0].rearrange("n (a s) d -> (n a) (s d)", s=SLOTS)
                for b in range(DB):
                    if b >= 2:
                        pool.wait_ge(turned, 4 * (b - 1))
                    pool.indirect_dma_start(kid[:, b % 2, :], None, pool_rows, bass.IndirectOffsetOnAxis(ap=mem.row_no[:, b:b + 1], axis=0)).then_inc(kid_loaded[b % 2], 16)

            @block.tensor
            def _(pe):
                def turn(b):
                    pe.wait_ge(kid_loaded[b % 2], 16 * (b // 2 + 1))
                    for t in range(4):
                        e = 4 * b + t
                        if e >= 2:
                            pe.wait_ge(keys_kept, e - 1)
                        for s in range(4):
                            k = 4 * t + s
                            m = nc.tensor.transpose(pt[e % 2][0:HD, s * P:(s + 1) * P], kid[:, b % 2, k * HD:(k + 1) * HD], c.ident[:])
                        m.then_inc(turned, 1)

                turn(0)
                pe.wait_ge(q_loaded, 16 * NIH)
                for b in range(DB):
                    if b + 1 < DB:
                        turn(b + 1)
                    pe.wait_ge(keys_kept, 4 * (b + 1))
                    pe.wait_ge(new_loaded[b % 2], 16 * (b // 2 + 1))
                    for n, (k0, w) in enumerate(CHUNKS):
                        e = 5 * b + n
                        if e >= 2:
                            pe.wait_ge(dots_kept, e - 1)
                        p0 = 32 * (b % 4)
                        nc.tensor.matmul(pd[e % 2][p0:p0 + 32, 0:w], qis[:, b].rearrange("d h q -> d (h q)"), kiT[:, b % 2, k0:k0 + w], start=True, stop=True).then_inc(dots_full, 1)
                pe.wait_ge(made, 5)
                for g in range(2):
                    m = nc.tensor.transpose(pt[g][:, 0:S], mem.selT[:, g], c.ident[0:S, 0:S])
                m.then_inc(sel_turned, 1)
                pe.wait_ge(sel_ready, 2)
                pe.wait_ge(dots_kept, 5 * DB)
                for n, (k0, w) in enumerate(CHUNKS):
                    if n >= 2:
                        pe.wait_ge(sum_kept, n - 1)
                    for g in range(2):
                        m = nc.tensor.matmul(pc[n % 2][0:S, 0:w], wsel[:, g, :], dots[:, g, k0:k0 + w], start=(g == 0), stop=(g == 1))
                    m.then_inc(sum_full, 1)

            @block.scalar
            def _(act):
                for b in range(DB):
                    p0 = 32 * (b % 4)
                    for n, (k0, w) in enumerate(CHUNKS):
                        e = 5 * b + n
                        act.wait_ge(dots_full, e + 1)
                        nc.scalar.activation(dots[p0:p0 + 32, b // 4, k0:k0 + w], pd[e % 2][p0:p0 + 32, 0:w], ACT.Relu, scale=IDX_SCALE).then_inc(dots_kept, 1)

            @block.vector
            def _(dve):
                ch = Chain(dve, s_chain)
                ch.mark(nc.vector.memset(qis[:], 0.0))
                ch.mark(nc.vector.memset(kiT[:], 0.0))
                ch.sync()
                dve.sem_inc(zeroed, 1)
                dve.wait_ge(table_loaded, 16 * N_PAGES)
                dve.wait_ge(made, 2)
                ch.mark(nc.vector.tensor_copy(fl[:], page_of[:]))
                ch.link(nc.vector.tensor_scalar(part[:], part[:], 7, None, ALU.bitwise_and))
                ch.link(nc.vector.tensor_copy(partf[:], part[:]))
                ch.link(nc.vector.tensor_scalar(mem.row_no[:], fl[:], 8.0, partf[:], ALU.mult, ALU.add))
                dve.sem_inc(rows_ready, 1)
                ch.link(nc.vector.tensor_scalar(part[0:S], part[0:S], 3, None, ALU.bitwise_and))
                ch.link(nc.vector.tensor_copy(qmod[:], part[0:S]))
                for b in range(DB):
                    if b >= 2:
                        dve.wait_ge(dots_full, 5 * (b - 1))
                    for t in range(4):
                        e = 4 * b + t
                        dve.wait_ge(turned, e + 1)
                        out = kiT[0:HD, b % 2, 0:2048].rearrange("d (p s) -> d s p", s=SLOTS)[:, 4 * t:4 * t + 4, :]
                        nc.vector.tensor_copy(out, pt[e % 2][0:HD, :].rearrange("d (s p) -> d s p", s=4)).then_inc(keys_kept, 1)
                dve.wait_ge(sel_turned, 1)
                dve.wait_ge(w_loaded, 128)
                for g in range(2):
                    nc.vector.tensor_scalar(wsel[:, g, :], pt[g][:, 0:S], wcol[:, g:g + 1], float(NIH) ** -0.5, ALU.mult, ALU.mult).then_inc(sel_ready, 1)
                for n, (k0, w) in enumerate(CHUNKS):
                    dve.wait_ge(sum_full, n + 1)
                    nc.vector.tensor_copy(sc[:, k0:k0 + w], pc[n % 2][0:S, 0:w]).then_inc(sum_kept, 1)
                dve.wait_ge(sum_kept, len(CHUNKS))
                ch.link(nc.vector.tensor_reduce(th.low[:], sc[:], AX.X, ALU.min))
                ch.link(nc.vector.tensor_scalar(newpos[:], newpos[:], qmod[:], -BIG, ALU.is_gt, ALU.mult))
                ch.link(nc.vector.tensor_tensor(sc[:, 2048:LS], sc[:, 2048:LS], newpos[:], ALU.add))
                ch.link(nc.vector.tensor_reduce(th.top[:], sc[:], AX.X, ALU.max))
                search_start(ch, nc.vector, th)
                ch.restart()
                with dve.Fori(0, ROUNDS):
                    ch.link(nc.vector.tensor_scalar(junk[:], sc[:], th.mid[:], None, ALU.is_ge, ALU.add, accum_out=th.count[:]))
                    search_round(ch, nc.vector, th, [(0, 1, TOPK - 0.5, ALU.is_ge)])
                    ch.restart()
                search_end(ch, nc.vector, th)
                select_row_tile(ch, nc, mem.mask[:], th.low[:], th.high[:], bounds[:], sure[:], edge[:], run[:])


def sample_attend(nc, c, mem):
    with Phase(nc, "s_") as ph:
        masks = ph.sb("masks", [P, 2, LS])
        sm = ph.sb("sm", [P, 2, LS])
        kk = ph.sb("kk", [P, 2, SLOTS * 2 * P])
        vv = ph.sb("vv", [P, 2, SLOTS * 2 * P])
        kT = ph.sb("kT", [P, 2, 2, LS])
        pT = ph.sb("pT", [P, SLOTS + 1, P])
        qbd = ph.sb("qbd", [P, DB, 2, NH, DS])
        vnew = ph.sb("vnew", [DS, DB, 2 * P])
        own = ph.sb("own", [P, 4, NKV])
        own_kv = ph.sb("own_kv", [P, NKV])
        part = ph.sb("part", [P, NKV])
        top = ph.sb("top", [P, 2, len(CHUNKS)])
        negmax, total = ph.sb("negmax", [P, 2]), ph.sb("total", [P, 2])
        o = ph.sb("o", [P, 2, HD])
        oT = ph.sb("oT", [HD, 2, P])
        pt = [ph.ps(f"t{i}", [P, 512]) for i in range(4)]
        pss = [ph.ps(f"s{i}", [P, 512]) for i in range(2)]
        po = ph.ps("o", [P, 512])
        pot = ph.ps("ot", [P, 512])
        zeroed, q_loaded, made, v_new_loaded = (ph.sem(n) for n in ("zeroed", "q_loaded", "made", "v_new_loaded"))
        k_loaded = [ph.sem(f"k_loaded{i}") for i in range(2)]
        v_loaded = [ph.sem(f"v_loaded{i}") for i in range(2)]
        new_loaded = [ph.sem(f"new_loaded{i}") for i in range(2)]
        mask_full, mask_kept, turned, s_full, s_kept, max_ready, exp_done, p_turned, pv_done, o_ready, o_turned, oT_kept, o_stored = (
            ph.sem(n) for n in ("mask_full", "mask_kept", "turned", "s_full", "s_kept", "max_ready", "exp_done", "p_turned", "pv_done", "o_ready",
                                "o_turned", "oT_kept", "o_stored"))
        kept = [ph.sem(f"kept{i}") for i in range(2)]
        p_kept = [ph.sem(f"p_kept{i}") for i in range(2)]
        s_chain = ph.sem("chain")
        NG = SLOTS // 4
        with ph.block() as block:
            @block.sync
            def _(sp):
                sp.wait_ge(zeroed, 1)
                for h in range(NH):
                    g = h // 2
                    p0 = (g % 2) * HD
                    sp.dma_start(qbd[p0:p0 + HD, :, g // 2, h, :], c.featT[COL_Q + h * HD:COL_Q + (h + 1) * HD, T:TT].rearrange("d (b q) -> d b q", b=DB)).then_inc(q_loaded, 16)
                sp.dma_start(vnew[:], c.out["v_sample"][0].rearrange("b q h d -> q b (h d)")).then_inc(v_new_loaded, 16)
                for b in range(DB):
                    if b >= 2:
                        sp.wait_ge(s_full, 5 * (b - 1))
                    sp.dma_start(kT[:, b % 2, :, 2048:LS], c.featT[COL_K:COL_V, T + DS * b:T + DS * b + DS].rearrange("(g p) t -> p g t", p=P),
                                 allow_slow_non_contiguous=True).then_inc(new_loaded[b % 2], 16)

            @block.gpsimd
            def _(pool):
                k_rows = c.inp["cache_k"][0].rearrange("n (a s) h d -> (n a) (s h d)", s=SLOTS)
                v_rows = c.inp["cache_v"][0].rearrange("n (a s) h d -> (n a) (s h d)", s=SLOTS)

                def load_k(b):
                    if b >= 2:
                        pool.wait_ge(turned, 8 * (b - 1))
                    pool.indirect_dma_start(kk[:, b % 2, :], None, k_rows, bass.IndirectOffsetOnAxis(ap=mem.row_no[:, b:b + 1], axis=0)).then_inc(k_loaded[b % 2], 16)

                def load_v(b):
                    if b >= 2:
                        pool.wait_ge(pv_done, b - 1)
                    pool.indirect_dma_start(vv[:, b % 2, :], None, v_rows, bass.IndirectOffsetOnAxis(ap=mem.row_no[:, b:b + 1], axis=0)).then_inc(v_loaded[b % 2], 16)

                load_k(0)
                load_k(1)
                nc.gpsimd.memset(own[:], 1.0).then_inc(made, 1)
                pool.wait_ge(made, 1)
                nc.gpsimd.affine_select(out=own[:], in_=own[:], compare_op=ALU.is_ge, fill=0.0, base=0, pattern=[[-32, 4], [-8, NKV]], channel_multiplier=1).then_inc(made, 1)
                pool.wait_ge(made, 2)
                nc.gpsimd.affine_select(out=own[:], in_=own[:], compare_op=ALU.is_ge, fill=0.0, base=7, pattern=[[32, 4], [8, NKV]], channel_multiplier=-1).then_inc(made, 1)
                load_v(0)
                load_v(1)
                load_k(2)
                load_k(3)
                load_k(4)
                load_k(5)
                for b in (2, 3, 4, 5):
                    load_v(b)
                load_k(6)
                load_k(7)
                load_v(6)
                load_v(7)
                for g in range(2):
                    pool.wait_ge(oT_kept, g + 1)
                    for b in range(4):
                        t0 = T + 16 * g + 4 * b
                        pool.dma_start(c.oT[:, t0:t0 + DS].rearrange("(h d) q -> d h q", d=HD), oT[:, g, 32 * b:32 * b + 32].rearrange("d (h q) -> d h q", h=NH)).then_inc(o_stored, 16)
                pool.wait_ge(o_stored, 128)

            @block.tensor
            def _(pe):
                for g in range(2):
                    for n, (k0, w) in enumerate(CHUNKS):
                        e = 5 * g + n
                        if e >= 2:
                            pe.wait_ge(mask_kept, e - 1)
                        nc.tensor.matmul(pss[e % 2][:, 0:w], mem.selT[:, g], mem.mask[:, k0:k0 + w], start=True, stop=True).then_inc(mask_full, 1)

                def turn(b):
                    pe.wait_ge(k_loaded[b % 2], 16 * (b // 2 + 1))
                    for t in range(NG):
                        for gh in range(2):
                            e = NG * b + t
                            if e >= 2:
                                pe.wait_ge(kept[gh], e - 1)
                            for s in range(4):
                                k = (4 * t + s) * 2 * P + gh * P
                                m = nc.tensor.transpose(pt[2 * gh + e % 2][:, s * P:(s + 1) * P], kk[:, b % 2, k:k + P], c.ident[:])
                            m.then_inc(turned, 1)

                def scores(b):
                    pe.wait_ge(kept[0], NG * (b + 1))
                    pe.wait_ge(kept[1], NG * (b + 1))
                    pe.wait_ge(new_loaded[b % 2], 16 * (b // 2 + 1))
                    p0 = 32 * (b % 4)
                    for n, (k0, w) in enumerate(CHUNKS):
                        e = 5 * b + n
                        if e >= 2:
                            pe.wait_ge(s_kept, e - 1)
                        for gh in range(2):
                            m = nc.tensor.matmul(pss[e % 2][p0:p0 + 32, 0:w], qbd[:, b, gh].rearrange("p h q -> p (h q)"), kT[:, b % 2, gh, k0:k0 + w],
                                                 start=(gh == 0), stop=(gh == 1))
                        m.then_inc(s_full, 1)

                def turn_probs(g):
                    pe.wait_ge(kept[0], NG * 4 * (g + 1))
                    pe.wait_ge(kept[1], NG * 4 * (g + 1))
                    pe.wait_ge(exp_done, g + 1)
                    p = sm[:, g, 0:2048].rearrange("r (p s) -> r s p", s=SLOTS)
                    for t in range(NG + 1):
                        if t == NG:
                            pe.wait_ge(p_kept[0], (NG // 2 + 1) * g + 1)
                            m = nc.tensor.transpose(pt[0][0:DS, 0:P], sm[:, g, 2048:LS], c.ident[:])
                        else:
                            for s in range(4):
                                m = nc.tensor.transpose(pt[t][:, s * P:(s + 1) * P], p[:, 4 * t + s, :], c.ident[:])
                        m.then_inc(p_turned, 1)

                def values(b):
                    g = b // 4
                    p0 = 32 * (b % 4)
                    pe.wait_ge(v_loaded[b % 2], 16 * (b // 2 + 1))
                    pe.wait_ge(p_kept[0], (NG // 2 + 1) * (g + 1))
                    pe.wait_ge(p_kept[1], NG // 2 * (g + 1))
                    if b == 4:
                        pe.wait_ge(o_ready, 1)
                    for s in range(SLOTS):
                        nc.tensor.matmul(po[p0:p0 + 32, 0:2 * P], pT[:, s, p0:p0 + 32], vv[:, b % 2, s * 2 * P:(s + 1) * 2 * P], start=(s == 0), stop=False)
                    nc.tensor.matmul(po[p0:p0 + 32, 0:2 * P], pT[0:DS, SLOTS, p0:p0 + 32], vnew[:, b, :], start=False, stop=True).then_inc(pv_done, 1)

                pe.wait_ge(q_loaded, 16 * NH)
                pe.wait_ge(mask_kept, 10)
                pe.wait_ge(v_new_loaded, 16)
                for g in range(2):
                    turn(4 * g)
                    for b in range(4 * g, 4 * g + 4):
                        if b % 4 < 3:
                            turn(b + 1)
                        scores(b)
                    turn_probs(g)
                    for b in range(4 * g, 4 * g + 4):
                        values(b)
                    pe.wait_ge(o_ready, g + 1)
                    if g:
                        pe.wait_ge(oT_kept, g)
                    nc.tensor.transpose(pot[0:HD, 0:P], o[:, g, :], c.ident[:]).then_inc(o_turned, 1)

            @block.scalar
            def _(act):
                for g in range(2):
                    for n, (k0, w) in enumerate(CHUNKS):
                        e = 5 * g + n
                        act.wait_ge(mask_full, e + 1)
                        nc.scalar.copy(masks[:, g, k0:k0 + w], pss[e % 2][:, 0:w]).then_inc(mask_kept, 1)
                for g in range(2):
                    for b in range(4 * g, 4 * g + 4):
                        if b >= 2:
                            act.wait_ge(s_full, 5 * (b - 1))
                        for t in range(NG):
                            e = NG * b + t
                            act.wait_ge(turned, 2 * e + 2)
                            out = kT[:, b % 2, 1, 0:2048].rearrange("d (p s) -> d s p", s=SLOTS)[:, 4 * t:4 * t + 4, :]
                            nc.scalar.copy(out, pt[2 + e % 2][:].rearrange("d (s p) -> d s p", s=4)).then_inc(kept[1], 1)
                    act.wait_ge(max_ready, g + 1)
                    nc.scalar.activation(sm[:, g], sm[:, g], ACT.Exp, bias=negmax[:, g:g + 1], scale=SM_SCALE, accum_out=total[:, g:g + 1]).then_inc(exp_done, 1)
                    if g:
                        act.wait_ge(pv_done, 4 * g)
                    for t in (2, 3):
                        act.wait_ge(p_turned, (NG + 1) * g + t + 1)
                        nc.scalar.copy(pT[:, 4 * t:4 * t + 4, :], pt[t][:].rearrange("p (s r) -> p s r", s=4)).then_inc(p_kept[1], 1)
                    act.wait_ge(o_turned, g + 1)
                    nc.scalar.copy(oT[:, g, :], pot[0:HD, 0:P]).then_inc(oT_kept, 1)

            @block.vector
            def _(dve):
                ch = Chain(dve, s_chain)
                ch.link(nc.vector.memset(qbd[:], 0.0))
                dve.sem_inc(zeroed, 1)
                dve.wait_ge(made, 3)
                ch.link(nc.vector.tensor_reduce(own_kv[:], own[:].rearrange("p b g -> p g b"), AX.X, ALU.add))
                dve.wait_ge(mask_kept, 10)

                def keep(b):
                    if b >= 2:
                        dve.wait_ge(s_full, 5 * (b - 1))
                    for t in range(NG):
                        e = NG * b + t
                        dve.wait_ge(turned, 2 * e + 1)
                        out = kT[:, b % 2, 0, 0:2048].rearrange("d (p s) -> d s p", s=SLOTS)[:, 4 * t:4 * t + 4, :]
                        nc.vector.tensor_copy(out, pt[e % 2][:].rearrange("d (s p) -> d s p", s=4)).then_inc(kept[0], 1)

                for g in range(2):
                    keep(4 * g)
                    for b in range(4 * g, 4 * g + 4):
                        if b % 4 < 3:
                            keep(b + 1)
                        p0 = 32 * (b % 4)
                        for n, (k0, w) in enumerate(CHUNKS):
                            dve.wait_ge(s_full, 5 * b + n + 1)
                            start = -3e38 if n == 0 else top[p0:p0 + 32, g, n - 1:n]
                            ch.link(nc.vector.tensor_tensor_reduce(sm[p0:p0 + 32, g, k0:k0 + w], pss[(5 * b + n) % 2][p0:p0 + 32, 0:w], masks[p0:p0 + 32, g, k0:k0 + w],
                                                                   1.0, start, ALU.add, ALU.max, top[p0:p0 + 32, g, n:n + 1]))
                            dve.sem_inc(s_kept, 1)
                    nc.vector.tensor_scalar(negmax[:, g:g + 1], top[:, g, len(CHUNKS) - 1:len(CHUNKS)], -SM_SCALE, None, ALU.mult).then_inc(max_ready, 1)
                    if g:
                        dve.wait_ge(pv_done, 4 * g)
                    for t in (0, 1, NG):
                        dve.wait_ge(p_turned, (NG + 1) * g + t + 1)
                        if t == NG:
                            nc.vector.tensor_copy(pT[0:DS, SLOTS, :], pt[0][0:DS, 0:P]).then_inc(p_kept[0], 1)
                        else:
                            nc.vector.tensor_copy(pT[:, 4 * t:4 * t + 4, :], pt[t][:].rearrange("p (s r) -> p s r", s=4)).then_inc(p_kept[0], 1)
                    ch.link(nc.vector.reciprocal(part[:, 0:1], total[:, g:g + 1]))
                    ch.link(nc.vector.tensor_scalar(part[:], own_kv[:], part[:, 0:1], None, ALU.mult))
                    dve.wait_ge(pv_done, 4 * g + 4)
                    ch.link(nc.vector.tensor_scalar(o[:, g, :], po[:, 0:HD], part[:, 0:1], None, ALU.mult))
                    for kv in range(1, NKV):
                        ch.link(nc.vector.scalar_tensor_tensor(o[:, g, :], po[:, kv * HD:(kv + 1) * HD], part[:, kv:kv + 1], o[:, g, :], ALU.mult, ALU.add))
                    dve.sem_inc(o_ready, 1)


def attend_samples(nc, c):
    with Phase(nc, "m_") as ph:
        mem = Ctx()
        mem.row_no = ph.sb("row_no", [P, DB], I32)
        mem.selT = ph.sb("selT", [S, 2, P])
        mem.mask = ph.sb("mask", [S, LS])
        sample_index(nc, c, mem)
        sample_attend(nc, c, mem)


NG, NE, EPG, F = 4, 32, 8, 256
NL = NG + NE
NTL = NT + 1
NBLK = -(-2 * TT // P) + NE


def tile_pairs(e):
    with e.Fori(0, NT // 2) as i:
        yield i, 0, 2 * i, P
        yield i, 1, 2 * i + 1, P
    yield NT // 2, 0, NT, S


def norm_conv(nc, c, yT):
    with Phase(nc, "n_") as ph:
        ct = ph.sb("ct", [P, 2, CB, P])
        yn = ph.sb("yn", [P, 2, CC])
        stats, mv, eps = ph.sb("stats", [P, 6]), ph.sb("mv", [P, 2, 2]), ph.sb("eps", [P, 2, 2])
        pa = [ph.ps(f"a{i}", [P, 512]) for i in range(2)]
        pb = [ph.ps(f"b{i}", [P, 512]) for i in range(2)]
        loaded = [ph.sem(f"loaded{i}") for i in range(2)]
        made, a_full, var_ready, rstd_ready, yn_ready, b_full, b_kept, s_chain, seen = (
            ph.sem(n) for n in ("made", "a_full", "var_ready", "rstd_ready", "yn_ready", "b_full", "b_kept", "chain", "seen"))
        with ph.block() as block:
            @block.sync
            def _(sp):
                for i, slot, t, n in tile_pairs(sp):
                    sp.wait_ge(a_full, t + 1)
                    sp.dma_start(ct[:, slot, :, 0:n], c.convT[:, bass.ds(t * P, n)].rearrange("(b p) t -> p b t", p=P)).then_inc(loaded[slot], 16)

            @block.tensor
            def _(pe):
                pe.sem_inc(a_full, 2)

                def rows(i, slot, t, n):
                    pe.wait_ge(loaded[slot], 16 * i + 16)
                    pe.wait_ge(yn_ready, t + 1)
                    for b in range(CB):
                        m = nc.tensor.transpose(pa[slot][0:n, b * P:(b + 1) * P], ct[:, slot, b, 0:n], c.ident[:])
                    m.then_inc(a_full, 1)

                def back(slot, t, n):
                    pe.wait_ge(yn_ready, t + 3)
                    pe.wait_ge(b_kept, t + 1)
                    for b in range(CB):
                        m = nc.tensor.transpose(pb[slot][:, b * P:b * P + n], yn[0:n, slot, b * P:(b + 1) * P], c.ident[0:n, 0:n])
                    m.then_inc(b_full, 1)

                with pe.Fori(0, NT // 2) as i:
                    rows(i, 0, 2 * i, P)
                    rows(i, 1, 2 * i + 1, P)
                    back(0, 2 * i, P)
                    back(1, 2 * i + 1, P)
                rows(NT // 2, 0, NT, S)
                back(0, NT, S)

            @block.gpsimd
            def _(pool):
                nc.gpsimd.memset(eps[:], -0.5).then_inc(made, 1)
                pool.wait_ge(made, 1)
                for i, slot, t, n in tile_pairs(pool):
                    pool.wait_ge(var_ready, t + 1)
                    nc.gpsimd.tensor_tensor(mv[0:n, slot, 1:2], mv[0:n, slot, 1:2], eps[0:n, 0, 0:1], ALU.pow).then_inc(rstd_ready, 1)

            @block.vector
            def _(dve):
                ch = Chain(dve, s_chain)
                dve.sem_inc(yn_ready, 2)
                for i, slot, t, n in tile_pairs(dve):
                    dve.wait_ge(a_full, t + 3)
                    ch.link(nc.vector.bn_stats(stats[0:n], pa[slot][0:n, :]))
                    ch.link(nc.vector.bn_aggr(mv[0:n, slot, :], stats[0:n]))
                    nc.vector.tensor_scalar(mv[0:n, slot, 1:2], mv[0:n, slot, 1:2], LN_EPS, None, ALU.add).then_inc(var_ready, 1)
                    dve.wait_ge(rstd_ready, t + 1)
                    dve.wait_ge(b_full, t + 1)
                    nc.vector.tensor_scalar(yn[0:n, slot, :], pa[slot][0:n, :], mv[0:n, slot, 0:1], mv[0:n, slot, 1:2], ALU.subtract, ALU.mult).then_inc(yn_ready, 1)
                    ch.restart()

            @block.scalar
            def _(act):
                act.sem_inc(b_kept, 2)
                act.sem_inc(b_full, 2)
                for i, slot, t, n in tile_pairs(act):
                    act.wait_ge(b_full, t + 3)
                    act.sem_inc(seen, 1)
                    for b in range(CB):
                        m = nc.scalar.activation(yT[:, b, bass.ds(t * P, n)], pb[slot][:, b * P:b * P + n], ACT.Silu,
                                                 scale=c.cols[:, VEC_LG + b:VEC_LG + b + 1], bias=c.cols[:, VEC_LB + b:VEC_LB + b + 1])
                    m.then_inc(b_kept, 1)


def mix(nc, c, yT, logits):
    with Phase(nc, "x2_") as ph:
        wc = ph.sb("wc", [P, CB, D])
        wa = ph.sb("wa", [P, CB, D])
        wo = ph.sb("wo", [P, KD, D])
        wr = ph.sb("wr", [P, KD, P])
        rb = ph.sb("rb", [P, NL])
        gain, bias = ph.sb("gain", [P, D]), ph.sb("bias", [P, D])
        oT = ph.sb("oT", [P, CB, 512])
        gates = ph.sb("gates", [P, 2 * KD, 512])
        t1, t2 = ph.sb("t1", [P, 512]), ph.sb("t2", [P, 512])
        mT = ph.sb("mT", [P, KD, 512])
        xt = ph.sb("xt", [P, 2, D])
        x1 = ph.sb("x1", [P, 2, D])
        x1T = ph.sb("x1T", [P, KD, P])
        stats, mv, eps = ph.sb("stats", [P, 2, 6]), ph.sb("mv", [P, 2]), ph.sb("eps", [P, 1])
        pA = [ph.ps(f"A{i}", [P, 512]) for i in range(2)]
        pB = [ph.ps(f"B{i}", [P, 512]) for i in range(2)]
        pC = ph.ps("C", [P, 2, 512])
        pX, pR = ph.ps("X", [P, 512]), ph.ps("R", [P, 512])
        w_loaded, o_weights, zeroed, made = (ph.sem(n) for n in ("w_loaded", "o_weights", "zeroed", "made"))
        o_loaded, g_loaded = ph.sem("o_loaded"), ph.sem("g_loaded")
        x_loaded = [ph.sem(f"x_loaded{i}") for i in range(2)]
        x1_stored = [ph.sem(f"x1_stored{i}") for i in range(2)]
        ab_full, m_done, c_full, c_kept, var_ready, rstd_ready, x1_ready, x_full, x_kept, r_full, r_kept, s_chain, seen = (
            ph.sem(n) for n in ("ab_full", "m_done", "c_full", "c_kept", "var_ready", "rstd_ready", "x1_ready", "x_full", "x_kept", "r_full", "r_kept",
                                "chain", "seen"))

        def blocks(e):
            with e.Fori(0, T // 512) as b:
                yield b, 512, [P] * 4
            yield T // 512, S, [S]

        with ph.block() as block:
            @block.sync
            def _(sp):
                sp.wait_ge(zeroed, 1)
                sp.dma_start(wc[:], c.inp["w_conv_out"][0].rearrange("(k p) n -> p k n", p=P)).then_inc(w_loaded, 16)
                sp.dma_start(wa[:], c.inp["w_attn_out"][0].rearrange("(k p) n -> p k n", p=P)).then_inc(w_loaded, 16)
                for b, n, tiles in blocks(sp):
                    sp.wait_ge(ab_full, 8 * b + 1)
                    sp.dma_start(oT[:, :, 0:n], c.oT[:, bass.ds(b * 512, n)].rearrange("(k p) t -> p k t", p=P)).then_inc(o_loaded, 16)
                    sp.wait_ge(m_done, 8 * b + 2)
                    sp.dma_start(gates[:, :, 0:n], c.featT[COL_G:N_IN, bass.ds(b * 512, n)].rearrange("(k p) t -> p k t", p=P)).then_inc(g_loaded, 16)
                    for s, r in enumerate(tiles):
                        sp.wait_ge(c_kept, 4 * b + (s + 1))
                        src = c.xp[bass.ds(b * 512 + s * P, P), :] if r == P else c.xs
                        sp.dma_start(xt[0:r, s % 2, :], src).then_inc(x_loaded[s % 2], 16)

            @block.gpsimd
            def _(pool):
                nc.gpsimd.memset(eps[:], -0.5).then_inc(made, 1)
                pool.wait_ge(made, 1)
                pool.dma_start(wo[:], c.inp["w_out"][0].rearrange("(k p) n -> p k n", p=P)).then_inc(o_weights, 16)
                pool.wait_ge(zeroed, 1)
                pool.dma_start(wr[:, :, 0:NG], c.inp["router_group_w"][0].rearrange("(k p) n -> p k n", p=P)).then_inc(o_weights, 16)
                pool.dma_start(wr[:, :, NG:NL], c.inp["router_expert_w"][0].rearrange("(k p) n -> p k n", p=P)).then_inc(o_weights, 16)
                pool.dma_start(rb[:, 0:NG], c.inp["router_group_b"].to_broadcast([P, NG])).then_inc(o_weights, 16)
                pool.dma_start(rb[:, NG:NL], c.inp["router_expert_b"].to_broadcast([P, NE])).then_inc(o_weights, 16)
                pool.dma_start(gain[:], c.inp["ln1_g"].to_broadcast([P, D])).then_inc(o_weights, 16)
                pool.dma_start(bias[:], c.inp["ln1_b"].to_broadcast([P, D])).then_inc(o_weights, 16)
                for b, n, tiles in blocks(pool):
                    for s, r in enumerate(tiles):
                        t = 4 * b + s
                        pool.wait_ge(var_ready, t + 1)
                        nc.gpsimd.tensor_tensor(mv[0:r, 1:2], mv[0:r, 1:2], eps[0:r], ALU.pow).then_inc(rstd_ready, 1)
                        pool.wait_ge(x1_ready, t + 1)
                        pool.sem_inc(seen, 1)
                        pool.dma_start(c.x1[bass.ds(b * 512 + s * P, r), :], x1[0:r, s % 2, :]).then_inc(x1_stored[s % 2], 16)
                pool.wait_ge(x1_stored[0], 16 * (NT // 2 + 1))
                pool.wait_ge(x1_stored[1], 16 * (NT // 2))

            @block.tensor
            def _(pe):
                pe.sem_inc(ab_full, 1)
                pe.wait_ge(w_loaded, 32)

                def branches(b, n):
                    pe.wait_ge(o_loaded, 16 * b + 16)
                    pe.wait_ge(c_full, 4 * b)
                    for f in range(KD):
                        pe.wait_ge(m_done, 8 * b + (f + 1))
                        for k in range(CB):
                            nc.tensor.matmul(pA[f % 2][:, 0:n], wc[:, k, f * P:(f + 1) * P], yT[:, k, bass.ds(b * 512, n)], start=(k == 0), stop=(k == CB - 1))
                        for k in range(CB):
                            m = nc.tensor.matmul(pB[f % 2][:, 0:n], wa[:, k, f * P:(f + 1) * P], oT[:, k, 0:n], start=(k == 0), stop=(k == CB - 1))
                        m.then_inc(ab_full, 1)

                def out(b, s, r):
                    pe.wait_ge(c_kept, 4 * b + (s + 2))
                    for h in range(2):
                        for k in range(KD):
                            m = nc.tensor.matmul(pC[0:r, h, :], mT[:, k, s * P:s * P + r], wo[:, k, h * 512:(h + 1) * 512], start=(k == 0), stop=(k == KD - 1))
                    m.then_inc(c_full, 1)

                def route(b, s, r):
                    t = 4 * b + s
                    pe.wait_ge(x1_ready, t + 1)
                    for h in range(2):
                        pe.wait_ge(x_kept, 2 * t + (h + 1))
                        for k in range(4):
                            m = nc.tensor.transpose(pX[:, k * P:k * P + r], x1[0:r, s % 2, (4 * h + k) * P:(4 * h + k + 1) * P], c.ident[0:r, 0:r])
                        m.then_inc(x_full, 1)
                    pe.wait_ge(x_kept, 2 * t + 3)
                    pe.wait_ge(r_kept, t + 1)
                    for k in range(KD):
                        m = nc.tensor.matmul(pR[0:r, 0:P], x1T[:, k, 0:r], wr[:, k, :], start=(k == 0), stop=(k == KD - 1))
                    m.then_inc(r_full, 1)

                for b, n, tiles in blocks(pe):
                    branches(b, n)
                    pe.wait_ge(m_done, 8 * b + 10)
                    pe.wait_ge(o_weights, 16 * 7)
                    for s, r in enumerate(tiles):
                        out(b, s, r)
                        if s:
                            route(b, s - 1, P)
                    route(b, len(tiles) - 1, tiles[-1])

            @block.scalar
            def _(act):
                act.sem_inc(x_kept, 1)
                for b, n, tiles in blocks(act):
                    for s, r in enumerate(tiles):
                        t = 4 * b + s
                        for h in range(2):
                            act.wait_ge(x_full, 2 * t + (h + 1))
                            if h == 0:
                                act.wait_ge(r_full, t)
                            nc.scalar.copy(x1T[:, 4 * h:4 * h + 4, 0:r], pX[:].rearrange("p (k t) -> p k t", k=4)[:, :, 0:r]).then_inc(x_kept, 1)

            @block.vector
            def _(dve):
                ch = Chain(dve, s_chain)
                ch.link(nc.vector.memset(wr[:], 0.0))
                ch.link(nc.vector.memset(logits[:], 0.0))
                dve.sem_inc(zeroed, 1)
                dve.sem_inc(m_done, 2)
                dve.sem_inc(c_kept, 2)
                dve.sem_inc(r_kept, 1)
                dve.wait_ge(o_weights, 16 * 7)
                ch.restart()
                for b, n, tiles in blocks(dve):
                    dve.wait_ge(g_loaded, 16 * b + 16)
                    for f in range(KD):
                        dve.wait_ge(ab_full, 8 * b + (f + 2))
                        if f == 0:
                            dve.wait_ge(c_full, 4 * b)
                        ch.mark(nc.vector.tensor_tensor(t1[:, 0:n], pA[f % 2][:, 0:n], gates[:, f, 0:n], ALU.mult))
                        ch.link(nc.vector.tensor_tensor(t2[:, 0:n], pB[f % 2][:, 0:n], gates[:, KD + f, 0:n], ALU.mult))
                        nc.vector.tensor_tensor(mT[:, f, 0:n], t1[:, 0:n], t2[:, 0:n], ALU.add).then_inc(m_done, 1)
                        dve.wait_ge(m_done, 8 * b + (f + 3))

                    def logit(s, r):
                        t = 4 * b + s
                        dve.wait_ge(r_full, t + 1)
                        dve.sem_inc(seen, 1)
                        at = logits[0:r, bass.ds(t, 1), :]
                        nc.vector.tensor_tensor(at, pR[0:r, 0:NL].rearrange("p (a l) -> p a l", a=1), rb[0:r].rearrange("p (a l) -> p a l", a=1), ALU.add).then_inc(r_kept, 1)

                    for s, r in enumerate(tiles):
                        t = 4 * b + s
                        dve.wait_ge(c_full, t + 1)
                        dve.wait_ge(x_loaded[s % 2], 32 * b + 16 * (s // 2 + 1))
                        dve.wait_ge(x1_stored[s % 2], 32 * b + 16 * (s // 2))
                        dve.wait_ge(x_full, 8 * b + 2 * max(s - 1, 0))
                        z, o = xt[0:r, s % 2, :], x1[0:r, s % 2, :]
                        ch.link(nc.vector.scalar_tensor_tensor(o, z, ALPHA, pC[0:r].rearrange("p h n -> p (h n)"), ALU.mult, ALU.add))
                        dve.sem_inc(c_kept, 1)
                        layer_norm(ch, nc, dve, o, r, stats, mv, gain, bias, var_ready, rstd_ready, t + 1)
                        dve.sem_inc(x1_ready, 1)
                        if s:
                            logit(s - 1, P)
                    logit(len(tiles) - 1, tiles[-1])
                    ch.restart()


def layer_norm(ch, nc, dve, o, r, stats, mv, gain, bias, var_ready, rstd_ready, nth):
    for h in range(2):
        ch.mark(nc.vector.bn_stats(stats[0:r, h, :], o[:, h * 512:(h + 1) * 512]))
    ch.sync()
    ch.link(nc.vector.bn_aggr(mv[0:r, :], stats[0:r].rearrange("p h s -> p (h s)")))
    nc.vector.tensor_scalar(mv[0:r, 1:2], mv[0:r, 1:2], LN_EPS, None, ALU.add).then_inc(var_ready, 1)
    dve.wait_ge(rstd_ready, nth)
    ch.link(nc.vector.tensor_scalar(o, o, mv[0:r, 0:1], mv[0:r, 1:2], ALU.subtract, ALU.mult))
    ch.link(nc.vector.tensor_tensor(o, o, gain[0:r, :], ALU.mult))
    ch.link(nc.vector.tensor_tensor(o, o, bias[0:r, :], ALU.add))


def first_of(ch, nc, one_hot, values, top, order, tmp, wide):
    n, m, w = wide
    ch.link(nc.vector.tensor_tensor(one_hot, values, top.to_broadcast([n, m, w]), ALU.is_equal))
    ch.link(nc.vector.tensor_tensor(one_hot, one_hot, order.to_broadcast([n, m, w]), ALU.mult))
    ch.link(nc.vector.tensor_reduce(tmp, one_hot, AX.X, ALU.max))
    ch.link(nc.vector.tensor_tensor(one_hot, one_hot, tmp.to_broadcast([n, m, w]), ALU.is_equal))


def route(nc, c, logits, gate, place, expert_of, weight_slot, is_new):
    with Phase(nc, "r_") as ph:
        order = ph.sb("order", [P, 1, NE])
        t1 = ph.sb("t1", [P, NTL, 1])
        top = ph.sb("top", [P, NTL, 1])
        goh = ph.sb("goh", [P, NTL, NG])
        el = ph.sb("el", [P, NTL, NE])
        oh = [ph.sb(f"oh{i}", [P, NTL, NE]) for i in range(2)]
        both = ph.sb("both", [P, NTL, NE])
        ex = ph.sb("ex", [P, NTL, NG])
        gsum = ph.sb("gsum", [P, NTL, 1])
        ratio = ph.sb("ratio", [P, NTL, 1])
        tops = ph.sb("tops", [P, 2, NTL, 1])
        below, ones = ph.sb("below", [P, P]), ph.sb("ones", [P, P])
        rank = ph.sb("rank", [P, NTL, NE])
        totals = ph.sb("totals", [P, NTL + 1, NE])
        blk_no = ph.sb("blk_no", [P, 1, NBLK])
        thr = ph.sb("thr", [P, NE, NTL])
        cmpa = ph.sb("cmpa", [P, NE, NTL])
        nblk, end, start = (ph.sb(n, [P, NE]) for n in ("nblk", "end", "start"))
        cmpb = ph.sb("cmpb", [1, NBLK, NE])
        exf, newf, slf = (ph.sb(n, [1, NBLK]) for n in ("exf", "newf", "slf"))
        placef = ph.sb("placef", [P, 2, NTL, 1])
        token = ph.sb("token", [P, NTL], I32)
        dummy = ph.sb("dummy", [P, NBLK], I32)
        zero = ph.sb("zero", [1, D])
        idx = ph.sb("idx", [P, 2, 1], I32)
        tok = ph.sb("tok", [P, 1], I32)
        pp = [ph.ps(f"p{i}", [P, 512]) for i in range(4)]
        made, e_ready, e_done, m_ready, m_full, place_ready, filled, copied, s_chain, seen = (
            ph.sem(n) for n in ("made", "e_ready", "e_done", "m_ready", "m_full", "place_ready", "filled", "copied", "chain", "seen"))
        scattered = [ph.sem(f"scattered{i}") for i in range(2)]
        with ph.block() as block:
            @block.gpsimd
            def _(pool):
                nc.gpsimd.iota(order[:], [[0, 1], [-1, NE]], base=NE, channel_multiplier=0, allow_small_or_imprecise_dtypes=True).then_inc(made, 1)
                nc.gpsimd.memset(ones[:], 1.0).then_inc(made, 1)
                nc.gpsimd.iota(thr[:], [[0, NE], [P, NTL]], base=0, channel_multiplier=0, allow_small_or_imprecise_dtypes=True).then_inc(made, 1)
                nc.gpsimd.iota(blk_no[:], [[0, 1], [1, NBLK]], base=0, channel_multiplier=0, allow_small_or_imprecise_dtypes=True).then_inc(made, 1)
                nc.gpsimd.iota(token[:], [[P, NTL]], base=0, channel_multiplier=1).then_inc(made, 1)
                nc.gpsimd.iota(dummy[:], [[0, NBLK]], base=TT, channel_multiplier=0).then_inc(made, 1)
                nc.gpsimd.memset(zero[:], 0.0).then_inc(made, 1)
                pool.wait_ge(made, 7)
                nc.gpsimd.affine_select(out=below[:], in_=ones[:], compare_op=ALU.is_gt, fill=0.0, base=0, pattern=[[1, P]], channel_multiplier=-1).then_inc(made, 1)
                pool.dma_start(c.slot_tok.rearrange("(p j) a -> p (j a)", p=P), dummy[:]).then_inc(filled, 16)
                pool.dma_start(c.x1[TT:TT + 1, :], zero[:]).then_inc(filled, 16)
                pool.wait_ge(filled, 32)
                pool.wait_ge(place_ready, 1)
                with pool.Fori(0, NT) as t:
                    nc.gpsimd.tensor_copy(tok[:], token[:, bass.ds(t, 1)]).then_inc(copied, 1)
                    for a in range(2):
                        nc.gpsimd.tensor_copy(idx[:, a, :], place[:, a, bass.ds(t, 1)]).then_inc(copied, 1)
                    pool.wait_ge(copied, 3 * t + 3)
                    pool.sem_inc(seen, 1)
                    for a in range(2):
                        pool.indirect_dma_start(c.slot_tok, bass.IndirectOffsetOnAxis(ap=idx[:, a, :], axis=0), tok[:], None).then_inc(scattered[a], 16)
                    pool.wait_ge(scattered[0], 16 * t + 16)
                    pool.wait_ge(scattered[1], 16 * t + 16)
                for a in range(2):
                    pool.indirect_dma_start(c.slot_tok, bass.IndirectOffsetOnAxis(ap=place[0:S, a, NT:NT + 1], axis=0), token[0:S, NT:NT + 1], None).then_inc(scattered[a], 16)
                for a in range(2):
                    pool.wait_ge(scattered[a], 16 * (NT + 1))

            @block.scalar
            def _(act):
                act.wait_ge(e_ready, 1)
                nc.scalar.activation(ex[:], ex[:], ACT.Exp).then_inc(e_done, 1)
                nc.scalar.activation(ratio[:], ratio[:], ACT.Exp).then_inc(e_done, 1)

            @block.tensor
            def _(pe):
                pe.wait_ge(m_ready, 1)
                pe.wait_ge(made, 8)
                flat = both[:].rearrange("p t e -> p (t e)")
                for k, w in enumerate((below, ones)):
                    nc.tensor.matmul(pp[2 * k][:], w[:], flat[:, 0:512], start=True, stop=True)
                    nc.tensor.matmul(pp[2 * k + 1][:, 0:NE], w[:], flat[:, 512:512 + NE], start=True, stop=True).then_inc(m_full, 1)

            @block.vector
            def _(dve):
                ch = Chain(dve, s_chain)
                lg, le = logits[:, :, 0:NG], logits[:, :, NG:NL]
                wide = (P, NTL, NE)
                dve.wait_ge(made, 6)
                ch.link(nc.vector.tensor_reduce(top[:], lg, AX.X, ALU.max))
                ch.link(nc.vector.tensor_tensor(ex[:], lg, top[:].to_broadcast([P, NTL, NG]), ALU.subtract))
                first_of(ch, nc, goh[:], lg, top[:], order[:, :, 0:NG], t1[:], (P, NTL, NG))
                ch.link(nc.vector.tensor_scalar(goh[:], goh[:], -1.0, BIG, ALU.add, ALU.mult))
                for g in range(NG):
                    ch.link(nc.vector.tensor_tensor(el[:, :, g * EPG:(g + 1) * EPG], le[:, :, g * EPG:(g + 1) * EPG], goh[:, :, g:g + 1].to_broadcast([P, NTL, EPG]), ALU.add))
                for a in range(2):
                    ch.link(nc.vector.tensor_reduce(tops[:, a], el[:], AX.X, ALU.max))
                    first_of(ch, nc, oh[a][:], el[:], tops[:, a], order[:], t1[:], wide)
                    if a == 0:
                        ch.link(nc.vector.scalar_tensor_tensor(el[:], oh[0][:], -BIG, el[:], ALU.mult, ALU.add))
                ch.link(nc.vector.tensor_tensor(ratio[:], tops[:, 1], tops[:, 0], ALU.subtract))
                dve.sem_inc(e_ready, 1)
                ch.link(nc.vector.tensor_tensor(both[:], oh[0][:], oh[1][:], ALU.add))
                ch.mark(nc.vector.memset(both[S:2 * S, NT, :], 0.0))
                ch.link(nc.vector.memset(both[2 * S:P, NT, :], 0.0))
                dve.sem_inc(m_ready, 1)
                dve.wait_ge(e_done, 2)
                ch.link(nc.vector.tensor_reduce(gsum[:], ex[:], AX.X, ALU.add))
                ch.link(nc.vector.tensor_scalar(t1[:], ratio[:], 1.0, None, ALU.add))
                ch.link(nc.vector.tensor_tensor(gsum[:], gsum[:], t1[:], ALU.mult))
                ch.link(nc.vector.reciprocal(gate[:, 0], gsum[:, :, 0]))
                ch.link(nc.vector.tensor_tensor(gate[:, 1], gate[:, 0], ratio[:, :, 0], ALU.mult))
                dve.wait_ge(m_full, 2)
                rf, tf = rank[:].rearrange("p t e -> p (t e)"), totals[:, 1:NTL + 1, :].rearrange("p t e -> p (t e)")
                for dst, k in ((rf, 0), (tf, 1)):
                    ch.mark(nc.vector.tensor_copy(dst[:, 0:512], pp[2 * k][:]))
                    ch.mark(nc.vector.tensor_copy(dst[:, 512:512 + NE], pp[2 * k + 1][:, 0:NE]))
                ch.link(nc.vector.memset(totals[:, 0, :], 0.0))
                for t in range(1, NTL + 1):
                    ch.link(nc.vector.tensor_tensor(totals[:, t, :], totals[:, t, :], totals[:, t - 1, :], ALU.add))
                ch.link(nc.vector.tensor_tensor(rank[:], rank[:], totals[:, 0:NTL, :], ALU.add))
                cnt = totals[:, NTL, :].rearrange("p (e a) -> p e a", a=1)
                ch.link(nc.vector.tensor_tensor(cmpa[:], cnt.to_broadcast([P, NE, NTL]), thr[:], ALU.is_gt))
                ch.link(nc.vector.tensor_reduce(nblk[:], cmpa[:], AX.X, ALU.add))
                ch.link(nc.vector.tensor_tensor_scan(end[:], nblk[:], nblk[:], 0.0, ALU.add, ALU.max))
                ch.link(nc.vector.tensor_tensor(start[:], end[:], nblk[:], ALU.subtract))
                ch.link(nc.vector.tensor_scalar(start[:], start[:], float(P), None, ALU.mult))
                ch.link(nc.vector.tensor_tensor(rank[:], rank[:], start[:].rearrange("p (a e) -> p a e", a=1).to_broadcast([P, NTL, NE]), ALU.add))
                for a in range(2):
                    ch.link(nc.vector.tensor_tensor(el[:], oh[a][:], rank[:], ALU.mult))
                    ch.link(nc.vector.tensor_reduce(placef[:, a], el[:], AX.X, ALU.add))
                    ch.link(nc.vector.tensor_copy(place[:, a, :], placef[:, a, :, 0]))
                dve.sem_inc(place_ready, 1)
                b3 = blk_no[0:1].rearrange("p a b -> p b a").to_broadcast([1, NBLK, NE])
                ch.link(nc.vector.tensor_tensor(cmpb[:], end[0:1].rearrange("p (a e) -> p a e", a=1).to_broadcast([1, NBLK, NE]), b3, ALU.is_le))
                ch.link(nc.vector.tensor_reduce(exf[:], cmpb[:], AX.X, ALU.add))
                ch.link(nc.vector.tensor_scalar(exf[:], exf[:], float(NE - 1), None, ALU.min))
                ch.mark(nc.vector.memset(newf[:, 0:1], 1.0))
                ch.link(nc.vector.tensor_tensor(newf[:, 1:NBLK], exf[:, 1:NBLK], exf[:, 0:NBLK - 1], ALU.not_equal))
                ch.link(nc.vector.tensor_tensor_scan(slf[:], newf[:], newf[:], 0.0, ALU.add, ALU.max))
                ch.link(nc.vector.tensor_copy(weight_slot[:], slf[:]))
                ch.link(nc.vector.tensor_scalar(weight_slot[:], weight_slot[:], WS - 1, None, ALU.bitwise_and))
                ch.mark(nc.vector.tensor_copy(expert_of[:], exf[:]))
                ch.link(nc.vector.tensor_copy(is_new[:], newf[:]))


WS = 4


def experts(nc, c, expert_of, weight_slot, is_new):
    with Phase(nc, "e_") as ph:
        wgu = ph.sb("wgu", [P, WS, KD, 2 * F])
        wd = ph.sb("wd", [P, WS, 2, D])
        xg = ph.sb("xg", [P, 2, D])
        xT = ph.sb("xT", [P, 2, KD, P])
        sg = ph.sb("sg", [P, F])
        hh = ph.sb("hh", [P, F])
        hT = ph.sb("hT", [P, 2, P])
        y = ph.sb("y", [P, 2, D])
        ids = ph.sb("ids", [P, NBLK], I32)
        idx = ph.sb("idx", [P, 2, 1], I32)
        pX = [ph.ps(f"X{i}", [P, 512]) for i in range(2)]
        pG = [ph.ps(f"G{i}", [P, 512]) for i in range(2)]
        pH = ph.ps("H", [P, 512])
        pY = [ph.ps(f"Y{i}", [P, 512]) for i in range(2)]
        w_loaded = [ph.sem(f"w_loaded{i}") for i in range(WS)]
        x_loaded = [ph.sem(f"x_loaded{i}") for i in range(2)]
        y_stored = [ph.sem(f"y_stored{i}") for i in range(2)]
        ids_loaded, copied, x_turned, x_kept, gu_full, sg_done, h_done, h_turned, h_kept, y_full, s_done, seen = (
            ph.sem(n) for n in ("ids_loaded", "copied", "x_turned", "x_kept", "gu_full", "sg_done", "h_done", "h_turned", "h_kept", "y_full", "block_done", "seen"))
        y_kept = [ph.sem(f"y_kept{i}") for i in range(2)]

        def steps(e):
            with e.Fori(0, NBLK // 2) as i:
                yield i, 0, 2 * i
                yield i, 1, 2 * i + 1
            yield NBLK // 2, 0, NBLK - 1

        with ph.block() as block:
            @block.sync
            def _(sp):
                wg_h, wu_h = (c.inp[n][0].rearrange("e (p k) f -> p e k f", k=KD) for n in ("w_gate", "w_up"))
                wd_h = c.inp["w_down"][0].rearrange("e (p k) d -> p e k d", k=2)
                def load(turn, a):
                    j = turn * WS + a
                    sp.wait_ge(s_done, j + 1)
                    e = sp.value_load(expert_of[0:1, bass.ds(j, 1)], min_val=0, max_val=NE - 1)
                    s = sp.value_load(weight_slot[0:1, bass.ds(j, 1)], min_val=0, max_val=WS - 1)
                    n = sp.value_load(is_new[0:1, bass.ds(j, 1)], min_val=0, max_val=1)
                    for dst, src in ((wgu[:, bass.ds(s, 1), :, 0:F], wg_h), (wgu[:, bass.ds(s, 1), :, F:2 * F], wu_h), (wd[:, bass.ds(s, 1)], wd_h)):
                        sp.dma_start(dst, src[:, bass.ds(e, 1)], cond=n).then_inc(w_loaded[a], 16)

                def store(i, slot, j):
                    sp.wait_ge(y_kept[0], j + 2)
                    sp.wait_ge(y_kept[1], j + 2)
                    sp.dma_start(c.yb[bass.ds(j * P, P), :], y[:, slot, :]).then_inc(y_stored[slot], 16)

                for a in range(WS):
                    load(0, a)
                turns = (NBLK - WS) // WS
                with sp.Fori(0, turns) as i:
                    for a in range(WS):
                        store(2 * i + a // 2, a % 2, i * WS + a)
                        load(i + 1, a)
                for j in range(turns * WS, NBLK):
                    store(j // 2, j % 2, j)
                    if j + WS < NBLK:
                        load((j + WS) // WS, (j + WS) % WS)
                sp.wait_ge(y_stored[0], 16 * (NBLK // 2 + 1))
                sp.wait_ge(y_stored[1], 16 * (NBLK // 2))

            @block.gpsimd
            def _(pool):
                pool.dma_start(ids[:], c.slot_tok.rearrange("(j p) a -> p (j a)", p=P), allow_slow_non_contiguous=True).then_inc(ids_loaded, 16)
                pool.wait_ge(ids_loaded, 16)
                for i, slot, j in steps(pool):
                    pool.wait_ge(x_loaded[slot], 16 * i)
                    pool.sem_inc(seen, 1)
                    nc.gpsimd.tensor_copy(idx[:, slot, :], ids[:, bass.ds(j, 1)]).then_inc(copied, 1)
                    pool.wait_ge(copied, j + 1)
                    pool.wait_ge(x_turned, 2 * j + 2)
                    pool.sem_inc(seen, 1)
                    pool.indirect_dma_start(xg[:, slot, :], None, c.x1, bass.IndirectOffsetOnAxis(ap=idx[:, slot, :], axis=0)).then_inc(x_loaded[slot], 16)

            @block.tensor
            def _(pe):
                pe.sem_inc(x_turned, 4)
                pe.sem_inc(s_done, WS)
                pe.sem_inc(gu_full, 2)

                def turn(i, slot, j):
                    pe.wait_ge(x_loaded[slot], 16 * i + 16)
                    for h in range(2):
                        pe.wait_ge(x_kept, 2 * j + (h + 1))
                        for k in range(4):
                            m = nc.tensor.transpose(pX[h][:, k * P:(k + 1) * P], xg[:, slot, 4 * h + k:D:KD], c.ident[:])
                        m.then_inc(x_turned, 1)

                def up(slot, j, s, turn, a):
                    pe.wait_ge(x_kept, 2 * j + 4)
                    pe.wait_ge(w_loaded[a], 48 * turn + 48)
                    pe.wait_ge(h_done, j + 1)
                    pe.sem_inc(seen, 1)
                    for k in range(KD):
                        m = nc.tensor.matmul(pG[slot][:], xT[:, slot, k, :], wgu[:, bass.ds(s, 1), k, :].rearrange("p a f -> p (a f)"), start=(k == 0), stop=(k == KD - 1))
                    m.then_inc(gu_full, 1)

                def turn_hidden(j):
                    pe.wait_ge(h_done, j + 3)
                    pe.wait_ge(h_kept, j)
                    for k in range(2):
                        m = nc.tensor.transpose(pH[:, k * P:(k + 1) * P], hh[:, k:F:2], c.ident[:])
                    m.then_inc(h_turned, 1)

                def down(j, s):
                    pe.wait_ge(h_kept, j + 1)
                    for h in range(2):
                        pe.wait_ge(y_kept[h], j + 1)
                        pe.sem_inc(seen, 1)
                        for k in range(2):
                            m = nc.tensor.matmul(pY[h][:], hT[:, k, :], wd[:, bass.ds(s, 1), k, h * 512:(h + 1) * 512].rearrange("p a f -> p (a f)"), start=(k == 0), stop=(k == 1))
                        m.then_inc(y_full, 1)
                    pe.wait_ge(y_full, 2 * j + 2)
                    pe.sem_inc(s_done, 1)

                def group(i, n, last):
                    s = [pe.value_load(weight_slot[0:1, bass.ds(i * WS + a, 1)], min_val=0, max_val=WS - 1) for a in range(n + (not last))]
                    for a in range(n):
                        j = i * WS + a
                        if a + 1 < n or not last:
                            up((a + 1) % 2, j + 1, s[a + 1], i + (a + 1) // WS, (a + 1) % WS)
                        turn_hidden(j)
                        if a + 2 < n or not last:
                            turn(2 * i + (a + 2) // 2, a % 2, j + 2)
                        down(j, s[a])

                turn(0, 0, 0)
                up(0, 0, pe.value_load(weight_slot[0:1, 0:1], min_val=0, max_val=WS - 1), 0, 0)
                turn(0, 1, 1)
                with pe.Fori(0, NBLK // WS - 1) as i:
                    group(i, WS, False)
                assert NBLK % WS == 1
                group(NBLK // WS - 1, WS + 1, True)

            @block.scalar
            def _(act):
                act.sem_inc(x_kept, 2)
                act.sem_inc(y_kept[1], 1)

                def keep_x(slot, j):
                    act.wait_ge(gu_full, j + 1)
                    for h in range(2):
                        act.wait_ge(x_turned, 2 * j + (h + 5))
                        nc.scalar.copy(xT[:, slot, 4 * h:4 * h + 4, :], pX[h][:].rearrange("p (k t) -> p k t", k=4)).then_inc(x_kept, 1)

                def silu(slot, j):
                    act.wait_ge(gu_full, j + 3)
                    act.wait_ge(h_done, j + 2)
                    nc.scalar.activation(sg[:], pG[slot][:, 0:F], ACT.Silu).then_inc(sg_done, 1)

                def keep_y(slot, uses, j):
                    act.wait_ge(y_stored[slot], 16 * uses)
                    act.wait_ge(y_full, 2 * j + 2)
                    nc.scalar.copy(y[:, slot, 512:D], pY[1][:]).then_inc(y_kept[1], 1)

                def group(i, n, last):
                    for a in range(n):
                        j = i * WS + a
                        if a + 1 < n or not last:
                            silu((a + 1) % 2, j + 1)
                        if a + 2 < n or not last:
                            keep_x(a % 2, j + 2)
                        keep_y(a % 2, 2 * i + a // 2, j)

                keep_x(0, 0)
                silu(0, 0)
                keep_x(1, 1)
                with act.Fori(0, NBLK // WS - 1) as i:
                    group(i, WS, False)
                group(NBLK // WS - 1, WS + 1, True)

            @block.vector
            def _(dve):
                dve.sem_inc(h_done, 2)
                dve.sem_inc(y_kept[0], 1)

                def gated(slot, j):
                    dve.wait_ge(sg_done, j + 1)
                    dve.wait_ge(h_turned, j)
                    nc.vector.tensor_tensor(hh[:], sg[:], pG[slot][:, F:2 * F], ALU.mult).then_inc(h_done, 1)

                def keep(i, slot, j, last=False):
                    dve.wait_ge(h_turned, j + 1)
                    dve.wait_ge(y_full, 2 * j)
                    nc.vector.tensor_copy(hT[:], pH[:, 0:2 * P].rearrange("p (k t) -> p k t", k=2)).then_inc(h_kept, 1)
                    if not last:
                        gated(1 - slot, j + 1)
                    dve.wait_ge(y_full, 2 * j + 1)
                    dve.wait_ge(y_stored[slot], 16 * i)
                    nc.vector.tensor_copy(y[:, slot, 0:512], pY[0][:]).then_inc(y_kept[0], 1)

                gated(0, 0)
                with dve.Fori(0, NBLK // 2) as i:
                    keep(i, 0, 2 * i)
                    keep(i, 1, 2 * i + 1)
                keep(NBLK // 2, 0, NBLK - 1, last=True)


def combine(nc, c, gate, place):
    with Phase(nc, "o_") as ph:
        gain, bias = ph.sb("gain", [P, D]), ph.sb("bias", [P, D])
        x1 = ph.sb("x1", [P, 2, D])
        ye = ph.sb("ye", [P, 2, 2, D])
        z = ph.sb("z", [P, 2, D])
        idx = ph.sb("idx", [P, 2, 2], I32)
        gnow = ph.sb("gnow", [P, 2, 1])
        stats, mv, eps = ph.sb("stats", [P, 2, 6]), ph.sb("mv", [P, 2]), ph.sb("eps", [P, 1])
        g_loaded, made, copied, var_ready, rstd_ready, z_first, z_ready, s_chain, seen = (
            ph.sem(n) for n in ("g_loaded", "made", "copied", "var_ready", "rstd_ready", "z_first", "z_ready", "chain", "seen"))
        x_loaded = [ph.sem(f"x_loaded{i}") for i in range(2)]
        y_loaded = [ph.sem(f"y_loaded{i}") for i in range(2)]
        z_stored = [ph.sem(f"z_stored{i}") for i in range(2)]
        with ph.block() as block:
            @block.sync
            def _(sp):
                sp.dma_start(gain[:], c.inp["ln2_g"].to_broadcast([P, D])).then_inc(g_loaded, 16)
                sp.dma_start(bias[:], c.inp["ln2_b"].to_broadcast([P, D])).then_inc(g_loaded, 16)
                for i, slot, t, n in tile_pairs(sp):
                    sp.wait_ge(z_first, t + 1)
                    sp.dma_start(x1[0:n, slot, :], c.x1[bass.ds(t * P, n), :]).then_inc(x_loaded[slot], 16)

            @block.scalar
            def _(act):
                for i, slot, t, n in tile_pairs(act):
                    act.wait_ge(z_ready, t + 1)
                    dst = c.out["y_prompt"][0, bass.ds(t * P, P), :] if n == P else c.out["y_sample"].rearrange("b s d -> (b s) d")
                    act.dma_start(dst, z[0:n, slot, :]).then_inc(z_stored[slot], 16)
                act.wait_ge(z_stored[0], 16 * (NT // 2 + 1))
                act.wait_ge(z_stored[1], 16 * (NT // 2))

            @block.gpsimd
            def _(pool):
                nc.gpsimd.memset(eps[:], -0.5).then_inc(made, 1)
                pool.wait_ge(made, 1)

                def gather(i, slot, t, n):
                    pool.wait_ge(y_loaded[slot], 32 * i)
                    pool.sem_inc(seen, 1)
                    nc.gpsimd.tensor_copy(idx[:, slot, :].rearrange("p (a b) -> p a b", b=1), place[:, :, bass.ds(t, 1)]).then_inc(copied, 1)
                    pool.wait_ge(copied, t + 1)
                    pool.wait_ge(z_first, t + 1)
                    pool.sem_inc(seen, 1)
                    for a in range(2):
                        pool.indirect_dma_start(ye[0:n, slot, a, :], None, c.yb, bass.IndirectOffsetOnAxis(ap=idx[0:n, slot, a:a + 1], axis=0)).then_inc(y_loaded[slot], 16)

                def power(t, n):
                    pool.wait_ge(var_ready, t + 1)
                    nc.gpsimd.tensor_tensor(mv[0:n, 1:2], mv[0:n, 1:2], eps[0:n], ALU.pow).then_inc(rstd_ready, 1)

                gather(0, 0, 0, P)
                gather(0, 1, 1, P)
                with pool.Fori(0, NT // 2 - 1) as i:
                    power(2 * i, P)
                    gather(i + 1, 0, 2 * i + 2, P)
                    power(2 * i + 1, P)
                    gather(i + 1, 1, 2 * i + 3, P)
                power(NT - 2, P)
                gather(NT // 2, 0, NT, S)
                power(NT - 1, P)
                power(NT, S)

            @block.vector
            def _(dve):
                ch = Chain(dve, s_chain)
                dve.sem_inc(z_first, 2)
                dve.wait_ge(g_loaded, 32)
                for i, slot, t, n in tile_pairs(dve):
                    ch.link(nc.vector.tensor_copy(gnow[:], gate[:, :, bass.ds(t, 1)]))
                    dve.wait_ge(x_loaded[slot], 16 * i + 16)
                    dve.wait_ge(y_loaded[slot], 32 * i + 32)
                    dve.wait_ge(z_stored[slot], 16 * i)
                    o = z[0:n, slot, :]
                    ch.link(nc.vector.tensor_scalar(o, x1[0:n, slot, :], ALPHA, None, ALU.mult))
                    for a in range(2):
                        ch.link(nc.vector.scalar_tensor_tensor(o, ye[0:n, slot, a, :], gnow[0:n, a], o, ALU.mult, ALU.add))
                    dve.sem_inc(z_first, 1)
                    layer_norm(ch, nc, dve, o, n, stats, mv, gain, bias, var_ready, rstd_ready, t + 1)
                    dve.sem_inc(z_ready, 1)
                    ch.restart()


INPUTS = ["x_prompt", "x_sample", "cache_k", "cache_v", "cache_kidx", "state_conv", "page_table", "w_in", "b_in",
          "conv_w", "conv_b", "conv_ln_g", "conv_ln_b", "w_conv_out", "w_attn_out", "w_out", "ln1_g", "ln1_b",
          "router_group_w", "router_group_b", "router_expert_w", "router_expert_b", "w_gate", "w_up", "w_down",
          "ln2_g", "ln2_b"]
OUTPUTS = [("y_prompt", (1, T, D)), ("y_sample", (DB, DS, D)), ("k_prompt", (1, 1, T, NKV, HD)), ("v_prompt", (1, 1, T, NKV, HD)),
           ("ki_prompt", (1, 1, T, HD)), ("conv_prompt", (1, 1, HIST, CC)), ("k_sample", (1, DB, DS, NKV, HD)),
           ("v_sample", (1, DB, DS, NKV, HD)), ("ki_sample", (1, DB, DS, HD)), ("conv_sample", (1, DB, HIST, CC))]


def build(nc, inp, out, upto=99, skip=()):
    c = Ctx()
    c.inp, c.out = inp, out
    c.xp = inp["x_prompt"][0]
    c.xs = inp["x_sample"].rearrange("b s d -> (b s) d")
    c.featT = nc.dram_tensor("featT", (N_IN, TT), F32).ap()
    c.oT = nc.dram_tensor("oT", (CC, TT), F32).ap()
    c.x1 = nc.dram_tensor("x1", (TT + 1, D), F32).ap()
    c.slot_tok = nc.dram_tensor("slot_tok", (NBLK * P, 1), I32).ap()
    c.yb = nc.dram_tensor("yb", (NBLK * P, D), F32).ap()
    c.convT = nc.dram_tensor("convT", (CC, TT), F32).ap()
    with Phase(nc, "g_") as g:
        c.ident = g.sb("ident", [P, P])
        c.cols = g.sb("cols", [P, VEC_N])
        constants(nc, c)
        with Phase(nc, "x_") as ph:
            x_hi, x_lo = (ph.sb(n, [P, KD, HALF], F32R) for n in ("x_hi", "x_lo"))
            taps = ph.sb("taps", [P, CB, TAPS])
            uh = ph.sb("uh", [P, CB, HIST + T])
            for half in range(2):
                turn_input(nc, c, half, x_hi, x_lo, c.cols, taps)
                project(nc, c, half, x_hi, x_lo, c.cols, taps, uh)
        with Phase(nc, "a_") as ph:
            kT = ph.sb("kT", [P, 2, T])
            kiT = ph.sb("kiT", [P, T])
            v_tok = ph.sb("v_tok", [P, NT, 2 * P])
            wi_tok = ph.sb("wi_tok", [P, NT + 1, NIH])
            if upto >= 3:
                keep_keys(nc, c, kT, kiT, v_tok, wi_tok)
            if upto >= 4 and 4 not in skip:
                attend_prompt(nc, c, kT, kiT, v_tok, wi_tok)
        if upto >= 5:
            attend_samples(nc, c)
        with Phase(nc, "b_") as ph:
            logits = ph.sb("logits", [P, NTL, NL])
            gate = ph.sb("gate", [P, 2, NTL])
            place = ph.sb("place", [P, 2, NTL], I32)
            expert_of, weight_slot, is_new = (ph.sb(n, [1, NBLK], I32) for n in ("expert_of", "weight_slot", "is_new"))
            with Phase(nc, "y_") as ph2:
                yT = ph2.sb("yT", [P, CB, TT])
                if upto >= 6:
                    norm_conv(nc, c, yT)
                if upto >= 7:
                    mix(nc, c, yT, logits)
            if upto >= 8:
                route(nc, c, logits, gate, place, expert_of, weight_slot, is_new)
            if upto >= 9:
                experts(nc, c, expert_of, weight_slot, is_new)
            if upto >= 10:
                combine(nc, c, gate, place)


def kernel(**inputs):
    import numpy as _np
    import concourse.bacc as _bacc
    from concourse import mybir as _mybir
    from concourse.bass_utils import run_bass_kernel_spmd as _run

    nc = _bacc.Bacc("TRN2", target_bir_lowering=False, num_devices=1)
    arrays, inp = {}, {}
    for name in INPUTS:
        a = _np.ascontiguousarray(inputs[name])
        arrays[f"in_{name}_dram"] = a
        inp[name] = nc.dram_tensor(f"in_{name}_dram", a.shape, _mybir.dt.from_np(a.dtype), kind="ExternalInput").ap()
    out = {name: nc.dram_tensor(f"out_{name}_dram", shape, _mybir.dt.float32, kind="ExternalOutput").ap() for name, shape in OUTPUTS}
    build(nc, inp, out)
    r = _run(nc, [arrays], core_ids=[0])
    return tuple(r.results[0][f"out_{name}_dram"] for name, _ in OUTPUTS)
```
